# Optimizing a Trainium2 kernel written in Bass

```python
import jax, jax.numpy as jnp
from jax import lax
import numpy as np
import math

D_MODEL = 1024
BATCH = 1
SEQ = 512
DEPTH = 2

N_A_LAYERS = DEPTH // 2
N_B_LAYERS = DEPTH - N_A_LAYERS

D_FF = 2816
RMS_EPS = 1e-6

RWKV_HEAD = 64
RWKV_HEADS = D_MODEL // RWKV_HEAD
DECAY_LORA = 64
AAA_LORA = 64
GATE_LORA = 128
GN_EPS = 64e-5

ATT_HEAD = 64
Q_HEADS = D_MODEL // ATT_HEAD
KV_HEADS = 4
GROUP = Q_HEADS // KV_HEADS
WINDOW = 128
BLOCK = 128
KV_WIDTH = KV_HEADS * ATT_HEAD
MASK_VALUE = -1e30


def rms_norm(x, g):
    xf = x.astype(jnp.float32)
    y = xf * lax.rsqrt(jnp.mean(xf * xf, axis=-1, keepdims=True) + RMS_EPS)
    return (y * g.astype(jnp.float32)).astype(x.dtype)

def swiglu(x, w_in, w_out):
    gate, up = jnp.split(x @ w_in, 2, axis=-1)
    return (jax.nn.silu(gate) * up) @ w_out

def rwkv7_time_mix(x, mu, w_rkv, w_o, w0, w1, w2, a0, a1, a2, g1, g2,
                   k_k, k_a, r_k, gn_g, gn_b):
    B, T, C = x.shape
    H, N = RWKV_HEADS, RWKV_HEAD
    f32 = jnp.float32
    x_prev = jnp.pad(x, ((0, 0), (1, 0), (0, 0)))[:, :-1]
    xx = x_prev - x
    xr, xw, xk, xv, xa, xg = [x + xx * mu[i] for i in range(6)]

    r = xr @ w_rkv[0]
    k = xk @ w_rkv[1]
    v = xv @ w_rkv[2]
    w = -jax.nn.softplus(-(w0 + jnp.tanh(xw @ w1) @ w2)) - 0.5
    decay = jnp.exp(-jnp.exp(w.astype(f32)))
    a = jax.nn.sigmoid(a0 + (xa @ a1) @ a2)
    g = jax.nn.sigmoid(xg @ g1) @ g2

    heads = lambda t: t.reshape(B, T, H, N).astype(f32)
    kk = heads(k * k_k)
    kk = kk / jnp.maximum(jnp.linalg.norm(kk, axis=-1, keepdims=True), 1e-12)
    k = k * (1.0 + (a - 1.0) * k_a)
    r_h, k_h, v_h, a_h, w_h = heads(r), heads(k), heads(v), heads(a), heads(decay)
    b_h = kk * a_h

    def step(S, inp):
        r_t, w_t, k_t, v_t, kk_t, b_t = inp
        sa = jnp.einsum('bhij,bhj->bhi', S, -kk_t)
        S = (S * w_t[:, :, None, :] + sa[..., None] * b_t[:, :, None, :]
             + v_t[..., None] * k_t[:, :, None, :])
        y = jnp.einsum('bhij,bhj->bhi', S, r_t)
        return S, y

    xs = tuple(jnp.moveaxis(t, 1, 0) for t in (r_h, w_h, k_h, v_h, kk, b_h))
    S0 = jnp.zeros((B, H, N, N), f32)
    _, y = lax.scan(step, S0, xs)
    y = jnp.moveaxis(y, 0, 1)

    mean = jnp.mean(y, axis=-1, keepdims=True)
    var = jnp.mean(jnp.square(y - mean), axis=-1, keepdims=True)
    y = ((y - mean) * lax.rsqrt(var + GN_EPS)).reshape(B, T, C)
    y = y * gn_g.astype(f32) + gn_b.astype(f32)
    bonus = jnp.sum(r_h * k_h * r_k.astype(f32), axis=-1, keepdims=True) * v_h
    y = (y + bonus.reshape(B, T, C)).astype(x.dtype)
    return (y * g) @ w_o

def swa_sinks(xq, k_sh, v_sh, w_q, b_q, w_o, b_o, sinks):
    B, T, _ = xq.shape
    NB = T // BLOCK
    q = (xq @ w_q + b_q).reshape(B, NB, BLOCK, KV_HEADS, GROUP, ATT_HEAD)

    def banded(t):
        t = t.reshape(B, NB, BLOCK, KV_HEADS, ATT_HEAD)
        prev = jnp.pad(t, ((0, 0), (1, 0), (0, 0), (0, 0), (0, 0)))[:, :-1]
        return jnp.concatenate([prev, t], axis=2)

    kb, vb = banded(k_sh), banded(v_sh)
    s = jnp.einsum('bnqkgd,bnskd->bnkgqs', q, kb).astype(jnp.float32) * (ATT_HEAD ** -0.5)
    blk = jnp.arange(NB)[:, None, None] * BLOCK
    q_pos = blk + jnp.arange(BLOCK)[None, :, None]
    k_pos = blk - BLOCK + jnp.arange(2 * BLOCK)[None, None, :]
    valid = (k_pos >= 0) & (k_pos <= q_pos) & (q_pos - k_pos < WINDOW)
    s = jnp.where(valid[None, :, None, None], s, MASK_VALUE)
    sink = jnp.broadcast_to(
        sinks.astype(jnp.float32).reshape(1, 1, KV_HEADS, GROUP, 1, 1), s.shape[:-1] + (1,))
    p = jax.nn.softmax(jnp.concatenate([s, sink], axis=-1), axis=-1)[..., :-1]
    o = jnp.einsum('bnkgqs,bnskd->bnqkgd', p.astype(vb.dtype), vb)
    o = o.reshape(B, T, Q_HEADS * ATT_HEAD)
    return o @ w_o + b_o

def first_inputs(seed: int = 0) -> dict:
    key = jax.random.key(seed)
    ks = iter(jax.random.split(key, 32))
    D, NA, NBL = D_MODEL, N_A_LAYERS, N_B_LAYERS
    f32 = jnp.float32

    def nrm(shape, scale):
        return scale * jax.random.normal(next(ks), shape, f32)

    def uni(shape, lo, hi):
        return jax.random.uniform(next(ks), shape, f32, lo, hi)

    return {
        "x": nrm((BATCH, SEQ, D), 1.0),
        "norm_g": 1.0 + nrm((DEPTH, 6, D), 0.05),
        "ffn_w_in": nrm((DEPTH, 2, D, 2 * D_FF), D ** -0.5),
        "ffn_w_out": nrm((DEPTH, 2, D_FF, D), D_FF ** -0.5),
        "rwkv_mu": uni((NA, 6, D), 0.0, 1.0),
        "rwkv_w_rkv": nrm((NA, 3, D, D), D ** -0.5),
        "rwkv_w_o": nrm((NA, D, D), D ** -0.5),
        "rwkv_w0": uni((NA, D), -6.0, -1.0),
        "rwkv_w1": nrm((NA, D, DECAY_LORA), D ** -0.5),
        "rwkv_w2": nrm((NA, DECAY_LORA, D), 0.1 * DECAY_LORA ** -0.5),
        "rwkv_a0": nrm((NA, D), 0.1),
        "rwkv_a1": nrm((NA, D, AAA_LORA), D ** -0.5),
        "rwkv_a2": nrm((NA, AAA_LORA, D), 0.1 * AAA_LORA ** -0.5),
        "rwkv_g1": nrm((NA, D, GATE_LORA), D ** -0.5),
        "rwkv_g2": nrm((NA, GATE_LORA, D), GATE_LORA ** -0.5),
        "rwkv_k_k": 0.85 + nrm((NA, D), 0.05),
        "rwkv_k_a": 1.0 + nrm((NA, D), 0.05),
        "rwkv_r_k": nrm((NA, RWKV_HEADS, RWKV_HEAD), 0.1),
        "rwkv_gn_g": 1.0 + nrm((NA, D), 0.05),
        "rwkv_gn_b": nrm((NA, D), 0.02),
        "kv_norm_g": 1.0 + nrm((D,), 0.05),
        "w_kv": nrm((D, 2 * KV_WIDTH), D ** -0.5),
        "b_kv": nrm((2 * KV_WIDTH,), 0.02),
        "attn_w_q": nrm((NBL, D, Q_HEADS * ATT_HEAD), D ** -0.5),
        "attn_b_q": nrm((NBL, Q_HEADS * ATT_HEAD), 0.02),
        "attn_w_o": nrm((NBL, Q_HEADS * ATT_HEAD, D), (Q_HEADS * ATT_HEAD) ** -0.5),
        "attn_b_o": nrm((NBL, D), 0.02),
        "attn_sinks": nrm((NBL, Q_HEADS), 1.0),
    }

def first_block(x, norm_g, ffn_w_in, ffn_w_out,
              rwkv_mu, rwkv_w_rkv, rwkv_w_o, rwkv_w0, rwkv_w1, rwkv_w2,
              rwkv_a0, rwkv_a1, rwkv_a2, rwkv_g1, rwkv_g2, rwkv_k_k, rwkv_k_a,
              rwkv_r_k, rwkv_gn_g, rwkv_gn_b,
              kv_norm_g, w_kv, b_kv,
              attn_w_q, attn_b_q, attn_w_o, attn_b_o, attn_sinks):
    B, T, _ = x.shape
    h = x
    k_sh = v_sh = None
    for layer in range(DEPTH):
        g = norm_g[layer]
        h = h + 0.5 * rms_norm(swiglu(rms_norm(h, g[0]), ffn_w_in[layer, 0], ffn_w_out[layer, 0]), g[1])
        u = rms_norm(h, g[2])
        if layer < N_A_LAYERS:
            i = layer
            m = rwkv7_time_mix(u, rwkv_mu[i], rwkv_w_rkv[i], rwkv_w_o[i], rwkv_w0[i],
                               rwkv_w1[i], rwkv_w2[i], rwkv_a0[i], rwkv_a1[i], rwkv_a2[i],
                               rwkv_g1[i], rwkv_g2[i], rwkv_k_k[i], rwkv_k_a[i],
                               rwkv_r_k[i], rwkv_gn_g[i], rwkv_gn_b[i])
        else:
            j = layer - N_A_LAYERS
            m = swa_sinks(u, k_sh, v_sh, attn_w_q[j], attn_b_q[j], attn_w_o[j],
                          attn_b_o[j], attn_sinks[j])
        h = h + rms_norm(m, g[3])
        h = h + 0.5 * rms_norm(swiglu(rms_norm(h, g[4]), ffn_w_in[layer, 1], ffn_w_out[layer, 1]), g[5])
        if layer == N_A_LAYERS - 1:
            kv = rms_norm(h, kv_norm_g) @ w_kv + b_kv
            k_sh = kv[..., :KV_WIDTH].reshape(B, T, KV_HEADS, ATT_HEAD)
            v_sh = kv[..., KV_WIDTH:].reshape(B, T, KV_HEADS, ATT_HEAD)
    return h


DEPTH_2 = 1

SB_HEADS = 8
SB_HEAD_DIM = 64
SB_WIDTH = SB_HEADS * SB_HEAD_DIM
MLA_HEADS = 8
MLA_NOPE_DIM = 64
MLA_ROPE_DIM = 32
MLA_V_DIM = 64
MLA_Q_RANK = 384
MLA_KV_RANK = 256
MLA_WIDTH = MLA_HEADS * MLA_V_DIM
MLA_QK_DIM = MLA_NOPE_DIM + MLA_ROPE_DIM

Q_BLOCK = 128
ROPE_BASE = 10000.0
EPS = 1e-6

SPLITS = (SB_WIDTH, SB_WIDTH, SB_WIDTH, SB_WIDTH,
          MLA_Q_RANK, MLA_KV_RANK, MLA_ROPE_DIM, MLA_WIDTH,
          D_MODEL, D_MODEL)
IN_WIDTH = int(sum(SPLITS))
SPLIT_POINTS = tuple(int(v) for v in np.cumsum(SPLITS)[:-1])


def rmsnorm(x, g):
    xf = x.astype(jnp.float32)
    y = xf * lax.rsqrt(jnp.mean(xf * xf, axis=-1, keepdims=True) + EPS)
    return (y * g.astype(jnp.float32)).astype(x.dtype)

def rope(x, positions):
    r = x.shape[-1]
    inv_freq = ROPE_BASE ** (-jnp.arange(0, r, 2, dtype=jnp.float32) / r)
    ang = positions.astype(jnp.float32)[:, :, None, None] * inv_freq
    cos, sin = jnp.cos(ang), jnp.sin(ang)
    xf = x.astype(jnp.float32)
    x1, x2 = xf[..., : r // 2], xf[..., r // 2:]
    return jnp.concatenate([x1 * cos - x2 * sin, x1 * sin + x2 * cos], axis=-1)

def to_blocks(t):
    b, h, s, d = t.shape
    return t.reshape(b, h, s // Q_BLOCK, Q_BLOCK, d).transpose(2, 0, 1, 3, 4)

def from_blocks(t):
    n, b, h, q, d = t.shape
    return t.transpose(1, 2, 0, 3, 4).reshape(b, h, n * q, d)

def stick_breaking_attention(q, k, v):
    s_len = k.shape[2]
    scale = 1.0 / math.sqrt(q.shape[-1])
    key_idx = jnp.arange(s_len)

    def block(args):
        qb, i = args
        z = jnp.einsum('bhqd,bhkd->bhqk', qb, k) * scale
        q_idx = i * Q_BLOCK + jnp.arange(Q_BLOCK)
        strict = key_idx[None, :] < q_idx[:, None]
        log_one_minus = jnp.where(strict, jax.nn.log_sigmoid(-z), 0.0)
        suffix = lax.cumsum(log_one_minus, axis=3, reverse=True) - log_one_minus
        w = jnp.where(strict, jnp.exp(jax.nn.log_sigmoid(z) + suffix), 0.0)
        return jnp.einsum('bhqk,bhkd->bhqd', w, v)

    n_blk = s_len // Q_BLOCK
    out = lax.map(block, (to_blocks(q), jnp.arange(n_blk)))
    return from_blocks(out)

def latent_attention(q_nope, q_pe, k_nope, k_pe, v):
    s_len = k_nope.shape[2]
    scale = 1.0 / math.sqrt(MLA_QK_DIM)
    key_idx = jnp.arange(s_len)

    def block(args):
        qn, qp, i = args
        sc = (jnp.einsum('bhqd,bhkd->bhqk', qn, k_nope)
              + jnp.einsum('bhqr,bkr->bhqk', qp, k_pe)) * scale
        q_idx = i * Q_BLOCK + jnp.arange(Q_BLOCK)
        causal = key_idx[None, :] <= q_idx[:, None]
        p = jax.nn.softmax(jnp.where(causal, sc, -jnp.inf), axis=-1)
        return jnp.einsum('bhqk,bhkd->bhqd', p, v)

    n_blk = s_len // Q_BLOCK
    out = lax.map(block, (to_blocks(q_nope), to_blocks(q_pe), jnp.arange(n_blk)))
    return from_blocks(out)

def split_heads(t, h):
    b, s, w = t.shape
    return t.reshape(b, s, h, w // h).transpose(0, 2, 1, 3)

def merge_heads(t):
    b, h, s, d = t.shape
    return t.transpose(0, 2, 1, 3).reshape(b, s, h * d)

def second_inputs(seed: int = 0) -> dict:
    key = jax.random.key(seed)
    ks = jax.random.split(key, 16)
    f32 = jnp.float32

    def nrm(k, shape, fan_in, mult=1.0):
        return jax.random.normal(k, shape, f32) * (mult * fan_in ** -0.5)

    x = jax.random.normal(ks[0], (BATCH, SEQ, D_MODEL), f32)
    c = jax.random.normal(ks[1], (BATCH, D_MODEL), f32)
    positions = jnp.broadcast_to(jnp.arange(SEQ, dtype=jnp.int32), (BATCH, SEQ))
    w_ada = nrm(ks[2], (DEPTH_2, D_MODEL, 3 * D_MODEL), D_MODEL, 0.2)
    b_ada = jax.random.normal(ks[3], (DEPTH_2, 3 * D_MODEL), f32) * 0.02
    norm_gain = 1.0 + 0.02 * jax.random.normal(ks[4], (DEPTH_2, D_MODEL), f32)
    w_in = nrm(ks[5], (DEPTH_2, D_MODEL, IN_WIDTH), D_MODEL)
    q_norm_gain = 1.0 + 0.02 * jax.random.normal(ks[6], (DEPTH_2, MLA_Q_RANK), f32)
    w_uq = nrm(ks[7], (DEPTH_2, MLA_Q_RANK, MLA_HEADS * MLA_QK_DIM), MLA_Q_RANK)
    kv_norm_gain = 1.0 + 0.02 * jax.random.normal(ks[8], (DEPTH_2, MLA_KV_RANK), f32)
    w_ukv = nrm(ks[9], (DEPTH_2, MLA_KV_RANK, MLA_HEADS * (MLA_NOPE_DIM + MLA_V_DIM)), MLA_KV_RANK)
    w_branch_a = nrm(ks[10], (DEPTH_2, SB_WIDTH, D_MODEL), SB_WIDTH)
    w_branch_b = nrm(ks[11], (DEPTH_2, MLA_WIDTH, D_MODEL), MLA_WIDTH)
    w_out = nrm(ks[12], (DEPTH_2, D_MODEL, D_MODEL), D_MODEL)
    final_norm_gain = 1.0 + 0.02 * jax.random.normal(ks[13], (D_MODEL,), f32)
    return {"x": x, "c": c, "positions": positions, "w_ada": w_ada, "b_ada": b_ada,
            "norm_gain": norm_gain, "w_in": w_in, "q_norm_gain": q_norm_gain, "w_uq": w_uq,
            "kv_norm_gain": kv_norm_gain, "w_ukv": w_ukv, "w_branch_a": w_branch_a,
            "w_branch_b": w_branch_b, "w_out": w_out, "final_norm_gain": final_norm_gain}

def second_block(x, c, positions, w_ada, b_ada, norm_gain, w_in, q_norm_gain, w_uq,
              kv_norm_gain, w_ukv, w_branch_a, w_branch_b, w_out, final_norm_gain):
    b, s, _ = x.shape
    f32 = jnp.float32
    for l in range(DEPTH_2):
        mod = c @ w_ada[l] + b_ada[l]
        shift, scale, gate = jnp.split(mod, 3, axis=-1)
        h = rmsnorm(x, norm_gain[l]) * (1.0 + scale[:, None, :]) + shift[:, None, :]

        proj = h @ w_in[l]
        (sb_q, sb_k, sb_v, sb_z, c_q, c_kv, k_rot, mla_z, g_a, g_b) = jnp.split(proj, SPLIT_POINTS, axis=-1)

        o_a = stick_breaking_attention(split_heads(sb_q, SB_HEADS).astype(f32),
                                       split_heads(sb_k, SB_HEADS).astype(f32),
                                       split_heads(sb_v, SB_HEADS).astype(f32))
        o_a = merge_heads(o_a).astype(x.dtype)
        y_a = (o_a * jax.nn.silu(sb_z)) @ w_branch_a[l]

        q = (rmsnorm(c_q, q_norm_gain[l]) @ w_uq[l]).reshape(b, s, MLA_HEADS, MLA_QK_DIM)
        q_nope = q[..., :MLA_NOPE_DIM].astype(f32)
        q_pe = rope(q[..., MLA_NOPE_DIM:], positions)
        kv = (rmsnorm(c_kv, kv_norm_gain[l]) @ w_ukv[l]).reshape(b, s, MLA_HEADS, MLA_NOPE_DIM + MLA_V_DIM)
        k_nope = kv[..., :MLA_NOPE_DIM].astype(f32)
        v_b = kv[..., MLA_NOPE_DIM:].astype(f32)
        k_pe = rope(k_rot[:, :, None, :], positions)[:, :, 0, :]
        o_b = latent_attention(q_nope.transpose(0, 2, 1, 3), q_pe.transpose(0, 2, 1, 3),
                               k_nope.transpose(0, 2, 1, 3), k_pe, v_b.transpose(0, 2, 1, 3))
        o_b = merge_heads(o_b).astype(x.dtype)
        y_b = (o_b * jax.nn.silu(mla_z)) @ w_branch_b[l]

        merged = jax.nn.sigmoid(g_a) * y_a + jax.nn.sigmoid(g_b) * y_b
        x = x + gate[:, None, :] * (merged @ w_out[l])
    return rmsnorm(x, final_norm_gain)


def setup_inputs(seed=0):
    out = dict(first_inputs(seed))
    for name, value in second_inputs(seed + 1).items():
        if name != "x":
            out[name + "_2"] = value
    return out


def reference(
    x, norm_g, ffn_w_in, ffn_w_out, rwkv_mu, rwkv_w_rkv, rwkv_w_o, rwkv_w0, rwkv_w1, rwkv_w2,
    rwkv_a0, rwkv_a1, rwkv_a2, rwkv_g1, rwkv_g2, rwkv_k_k, rwkv_k_a, rwkv_r_k, rwkv_gn_g,
    rwkv_gn_b, kv_norm_g, w_kv, b_kv, attn_w_q, attn_b_q, attn_w_o, attn_b_o, attn_sinks, c_2,
    positions_2, w_ada_2, b_ada_2, norm_gain_2, w_in_2, q_norm_gain_2, w_uq_2, kv_norm_gain_2,
    w_ukv_2, w_branch_a_2, w_branch_b_2, w_out_2, final_norm_gain_2,
):
    x = first_block(
        x, norm_g, ffn_w_in, ffn_w_out, rwkv_mu, rwkv_w_rkv, rwkv_w_o, rwkv_w0, rwkv_w1,
        rwkv_w2, rwkv_a0, rwkv_a1, rwkv_a2, rwkv_g1, rwkv_g2, rwkv_k_k, rwkv_k_a, rwkv_r_k,
        rwkv_gn_g, rwkv_gn_b, kv_norm_g, w_kv, b_kv, attn_w_q, attn_b_q, attn_w_o, attn_b_o,
        attn_sinks,
    )
    return second_block(
        x, c_2, positions_2, w_ada_2, b_ada_2, norm_gain_2, w_in_2, q_norm_gain_2, w_uq_2,
        kv_norm_gain_2, w_ukv_2, w_branch_a_2, w_branch_b_2, w_out_2, final_norm_gain_2,
    )


_drawn_inputs = setup_inputs


def setup_inputs(seed=0):
    import zlib

    import numpy as np

    out = dict(_drawn_inputs(seed))
    spreads = {}
    factors = {'rwkv_w1': 8.0,
     'rwkv_w2': 8.0,
     'attn_b_q': 5.999,
     'attn_sinks': 3.903,
     'b_ada_2': 8.0,
     'norm_gain_2': 8.0,
     'q_norm_gain_2': 8.0,
     'w_uq_2': 8.0,
     'kv_norm_gain_2': 8.0,
     'w_ukv_2': 4.923,
     'w_branch_b_2': 4.798,
     'final_norm_gain_2': 2.786}
    for name, (base, spread) in spreads.items():
        noise = np.random.default_rng([zlib.crc32(name.encode()), seed]).standard_normal(out[name].shape)
        drawn = base * np.exp(spread * noise) if base else spread * noise
        out[name] = __import__('jax').numpy.asarray(drawn.astype(out[name].dtype))
    for name, factor in factors.items():
        out[name] = (out[name] * factor).astype(out[name].dtype)
    return out
```

```python
from contextlib import ExitStack

import numpy as np
import concourse.bass as bass
from concourse import mybir

ALU = mybir.AluOpType
ACT = mybir.ActivationFunctionType
F32 = mybir.dt.float32
F32R = mybir.dt.float32r

P = 128
T = 512
D = 1024
KT = D // P
FF = 2816
FT = FF // P
UC = 512
RS = 4
RW = 4
TT = T // P
EPS = 1e-6
CH = 64
CHUNKS = T // CH
HEADS = D // 64
KV = 256
MASKED = -1e30
HEADS_B = 8
TRI = P * (1 + 2 + 3 + 4)
ROUND = 1.5 * 2.0 ** 23
TURN = (6.28125, 0.0019350051879882812, 3.019916050955909e-07)
PI = 3.1415925
KAPPA = float(np.exp(-0.5))
FB = FF * 2 // UC
SETB, SETA = 1, 0


def in_units(w):
    k, m = w.shape
    return w.reshape(k // P, P, m // UC, UC).transpose(2, 0, 1, 3).reshape(-1, P, UC)


def ffn_units(w_in, w_out):
    half = UC // 2
    gate, up = w_in[:, :FF].reshape(D, FB, half), w_in[:, FF:].reshape(D, FB, half)
    first = np.concatenate([gate, up], 2).reshape(D, FB * UC)
    return [in_units(first), in_units(w_out)]


FFN_UNITS = FB * KT + FT * (D // UC)


class Columns:

    def __init__(self):
        self.at, self.parts, self.n = {}, [], 0

    def add(self, name, tiles):
        self.at[name] = self.n
        self.n += tiles


def vector_table():
    c = Columns()
    for layer in range(2):
        for i in range(6):
            c.add(f"norm{layer}{i}", KT)
    for i in range(6):
        c.add(f"mu{i}", KT)
    for name in ("w0", "a0", "k_k", "k_a", "r_k", "gn_g", "gn_b"):
        c.add(name, KT)
    c.add("kv_norm", KT)
    c.add("b_k", 2)
    for name in ("b_q", "b_o"):
        c.add(name, KT)
    c.add("gain2", KT)
    c.add("b_ada", 3 * KT)
    c.add("q_norm2", 3)
    c.add("kv_norm2", 2)
    c.add("final", KT)
    c.add("c", KT)
    return c


VEC = vector_table()


def rwkv_units(w1, a1, g1, w_rkv, w2, a2, g2, w_o):
    inner = np.zeros((D, UC), np.float32)
    inner[:, 0:64], inner[:, 192:256], inner[:, 256:384] = w1, a1, g1
    outer = np.zeros((2, P, D), np.float32)
    outer[0, 0:64], outer[1, 64:P] = w2, a2
    return [in_units(inner), in_units(w_rkv[1]), in_units(w_rkv[0]), in_units(outer[0]), in_units(outer[1]),
            in_units(w_rkv[2]), in_units(g2), in_units(w_o)]


def masks_table():
    s, t = np.arange(CH)[:, None], np.arange(CH)[None, :]
    rows = [(t // b % 2 == 1) & (s // b == t // b - 1) for b in (1, 2, 4, 8, 16, 32)]
    rows += [rows[0].T, s < t, s <= t, s == t]
    return np.tile(np.stack(rows, 1).astype(np.float32), (2, 1, 1))


def heads_tables():
    head = np.arange(D) // 64
    spread = (head[None, :] == np.arange(HEADS)[:, None]).astype(np.float32).reshape(HEADS, KT, P)
    return spread.transpose(2, 1, 0), spread


def program(nc, xT, weights, vectors, masks_in, gather_in, spread_in, rows_in, window_in, ada_in, pos_in, rope_in, fold_in,
            tri_in, mask_a_in, mask_b_in, out):
    n_units = weights.shape[0]
    with ExitStack() as ctx:
        place = [-(-nc.sbuf_base // 64) * 64]

        def sb(name, shape, dt=F32, at=None):
            size = int(np.prod(shape[1:])) * 4
            size = -(-size // 64) * 64
            offset = place[0] if at is None else at
            if at is None:
                place[0] += size
            assert offset + size <= nc.sbuf_usable_end, (name, offset + size)
            t = nc.alloc_sbuf_tensor_at(name, shape, dt, offset=offset)
            where[name] = offset
            return t

        where = {}

        def sem(name):
            return ctx.enter_context(nc.semaphore(name))

        bank = [[ctx.enter_context(nc.psum_tensor(f"bank{s}{m}", [P, T], F32)) for m in range(4)] for s in range(2)]
        h = sb("h", [P, KT, T])
        w_raw = sb("w_raw", [P, RS, UC])
        w_hi = sb("w_hi", [P, RW, UC], F32R)
        w_lo = sb("w_lo", [P, RW, UC], F32R)
        vec = sb("vec", [P, VEC.n])
        ident = sb("ident", [P, P])
        ones = sb("ones", [P, P])
        eps = sb("eps", [P, 1])
        sq = sb("sq", [P, 2, T])
        acc = sb("acc", [P, T])
        root = sb("root", [P, TT])
        rinv = sb("rinv", [P, TT])
        diag = sb("diag", [P, TT, P])
        rstd = sb("rstd", [P, T])
        x_hi = sb("x_hi", [P, KT, T], F32R)
        x_lo = sb("x_lo", [P, KT, T], F32R)
        f = sb("f", [P, KT, T])
        mid_hi = sb("mid_hi", [P, FT, T], F32R)
        mid_lo = sb("mid_lo", [P, FT, T], F32R)
        masks = sb("masks", [P, 10, CH])
        rows = sb("rows", [P, KV + 16])
        spread = sb("spread", [HEADS, KT, P])
        gather = sb("gather", [P, KT, HEADS])
        rope_c = sb("rope_c", [P, 4])
        mod = sb("mod", [P, 3 * KT])
        gain_s = sb("gain_s", [P, KT])
        g_buf = f[:, 0:2, :]
        u_buf = f[:, 2:4, :]

        w_loaded = [sem(f"w_loaded{s}") for s in range(RS)]
        w_hi_ready = sem("w_hi_ready")
        w_lo_ready = sem("w_lo_ready")
        w_used = sem("w_used")
        const_ready = sem("const_ready")
        in_loaded = sem("in_loaded")
        stored = sem("stored")

        def count(n, i=None, per=0):
            return n if i is None else i * per + n

        def load_unit(sp, n, i=None):
            slot = n % RS
            sp.dma_start(w_raw[:, slot, :], weights[n] if i is None else
                         weights[bass.ds(i * RS + n, 1)].rearrange("a p c -> (a p) c")).then_inc(w_loaded[slot], 16)

        def split_unit(pool, n, i=None):
            if n < n_units:
                pool.wait_ge(w_loaded[n % RS], count(16 * (n // RS + 1), i, 16 * RW // RS))
                if n >= RW:
                    pool.wait_ge(w_used, count(n - RW + 1, i, RW))
            if n:
                pool.wait_ge(w_hi_ready, count(n, i, RW))
                pool.tensor_tensor(w_lo[:, (n - 1) % RW, :], w_raw[:, (n - 1) % RS, :],
                                   w_hi[:, (n - 1) % RW, :].bitcast(F32), ALU.subtract).then_inc(w_lo_ready, 1)
            if n < n_units:
                pool.tensor_scalar(w_hi[:, n % RW, :], w_raw[:, n % RS, :], 1.0, 0.0, ALU.mult, ALU.add).then_inc(w_hi_ready, 1)

        def unit_products(pe, outs, hi, lo, first, last, n, i=None, per=0):
            pe.wait_ge(w_lo_ready, count(n + 1, i, per))
            s = n % RW
            for m, o in enumerate(outs):
                c = slice(m * P, (m + 1) * P)
                pe.matmul(o, w_hi[:, s, c], hi, start=first, stop=False)
                pe.matmul(o, w_hi[:, s, c], lo, start=False, stop=False)
                done = pe.matmul(o, w_lo[:, s, c], hi, start=False, stop=last)
            done.then_inc(w_used, 1)

        def vcol(name, k):
            return vec[:, VEC.at[name] + k:VEC.at[name] + k + 1]

        class Steps:

            def __init__(self, name, labels):
                self.sem, self.at, self.told = sem(name), {l if isinstance(l, tuple) else (l,): j + 1 for j, l in enumerate(labels)}, 0
                assert len(self.at) == len(labels), name

            def __call__(self, *label, i=None):
                return self.sem, count(self.at[label], i, len(self.at))

            def tell(self, *label):
                self.told += 1
                assert self.at[label] == self.told, (label, self.told)
                return self.sem, 1

        sq_ready = sem("sq_ready")
        sq_used = sem("sq_used")
        sums_ready = sem("sums_ready")
        root_ready = sem("root_ready")
        diag_ready = sem("diag_ready")
        wide_ready = sem("wide_ready")
        norms = []

        class Norm:

            def __init__(self, tiles):
                self.n = len(norms)
                self.sq0 = sum(m.tiles for m in norms)
                self.tiles = tiles
                norms.append(self)

        def square(act, nm, j, src, **bias):
            j += nm.sq0
            if j >= 2:
                act.wait_ge(sq_used, j - 1)
            act.activation(sq[:, j % 2, :], src, ACT.Square, **bias).then_inc(sq_ready, 1)

        def add_square(dve, nm, j):
            first, j = j == 0, j + nm.sq0
            dve.wait_ge(sq_ready, j + 1)
            if first:
                if nm.n:
                    dve.wait_ge(sums_ready, nm.n)
                dve.tensor_copy(acc[:], sq[:, j % 2, :]).then_inc(sq_used, 1)
            else:
                dve.wait_ge(sq_used, j)
                dve.tensor_tensor(acc[:], acc[:], sq[:, j % 2, :], ALU.add).then_inc(sq_used, 1)

        def norm_sums(pe, nm, out):
            pe.wait_ge(sq_used, nm.sq0 + nm.tiles)
            for t in range(TT):
                done = pe.matmul(out[:, t:t + 1], acc[:, t * P:(t + 1) * P], ones[:, 0:1], start=True, stop=True)
            done.then_inc(sums_ready, 1)

        def norm_root(act, nm, sums, width):
            act.wait_ge(sums_ready, nm.n + 1)
            act.activation(root[:], sums[:, 0:TT], ACT.Sqrt, bias=eps[:, 0:1], scale=1.0 / width).then_inc(root_ready, 1)

        def norm_diag(dve, nm):
            d0 = (1 + TT) * nm.n
            dve.wait_ge(root_ready, nm.n + 1)
            dve.reciprocal(rinv[:], root[:]).then_inc(diag_ready, 1)
            dve.wait_ge(diag_ready, d0 + 1)
            for t in range(TT):
                dve.tensor_scalar(diag[:, t, :], ident[:], rinv[:, t:t + 1], None, ALU.mult).then_inc(diag_ready, 1)

        def norm_wide(pe, nm, out):
            pe.wait_ge(diag_ready, (1 + TT) * (nm.n + 1))
            pe.matmul(out[:], ones[:], diag[:].rearrange("p t q -> p (t q)"), start=True, stop=True).then_inc(wide_ready, 1)

        f_ready = sem("f_ready")
        tmp_ready = sem("tmp_ready")
        h_ready = sem("h_ready")

        def output_tensor(pe, s):
            pe.wait_ge(f_ready, s.h0 + 4)
            norm_sums(pe, s.post, bank[SETA][0])
            norm_wide(pe, s.post, bank[SETA][1])

        def output_scalar(act, s):
            for half, set_ in enumerate((SETA, SETB)):
                act.wait_ge(w_used, s.u1 + (half + 1) * s.rows)
                for m in range(4):
                    k = 4 * half + m
                    square(act, s.post, k, bank[set_][m][:], **({} if s.bias is None else {"bias": vcol(s.bias, k)}))
            norm_root(act, s.post, bank[SETA][0], D)

        def output_vector(dve, s):
            for half, set_ in enumerate((SETA, SETB)):
                dve.wait_ge(w_used, s.u1 + (half + 1) * s.rows)
                for m in range(4):
                    k = 4 * half + m
                    dve.wait_ge(sq_ready, s.post.sq0 + k + 1)
                    if s.bias is None:
                        dve.tensor_scalar(f[:, k, :], bank[set_][m][:], vcol(s.gain_out, k), s.half,
                                          ALU.mult, ALU.mult).then_inc(f_ready, 1)
                    else:
                        dve.tensor_scalar(f[:, k, :], bank[set_][m][:], vcol(s.bias, k), vcol(s.gain_out, k),
                                          ALU.add, ALU.mult).then_inc(f_ready, 1)
                    add_square(dve, s.post, k)
            norm_diag(dve, s.post)

        x_hi_ready = sem("x_hi_ready")
        x_lo_ready = sem("x_lo_ready")
        rstd_ready = sem("rstd_ready")
        bank_read = sem("bank_read")
        silu_ready = sem("silu_ready")
        prod_ready = sem("prod_ready")
        mid_hi_ready = sem("mid_hi_ready")
        mid_lo_ready = sem("mid_lo_ready")

        rstds = []

        def new_rstd():
            rstds.append(1)
            return len(rstds) - 1

        class Ffn:
            def __init__(self, number, layer, which, first_unit, x_tiles, updates, kv=None):
                self.kv, self.rs = kv, new_rstd()
                self.u0 = first_unit
                self.u1 = first_unit + FB * KT
                self.end = first_unit + FFN_UNITS
                self.rows = FT
                self.gain_in = f"norm{layer}{[0, 4][which]}"
                self.gain_out, self.bias, self.half = f"norm{layer}{[1, 5][which]}", None, 0.5
                self.n, self.x0 = number, x_tiles
                self.h0 = KT * updates
                self.read0, self.mid0 = 4 * FB * number, FT * number
                self.pre, self.post = Norm(KT), Norm(KT)

        def ffn_tensor(pe, s):
            def block(b, set_, n, i=None):
                for k in range(KT):
                    if b == 0:
                        pe.wait_ge(x_lo_ready, s.x0 + k + 1)
                    unit_products(pe, [o[:] for o in bank[set_]], x_hi[:, k, :], x_lo[:, k, :],
                                  k == 0, k == KT - 1, n + k, i, 2 * KT)

            if s.kv is not None:
                kv_tensor(pe, s)
            block(0, SETB, s.u0)
            if s.kv is None:
                norm_sums(pe, s.pre, bank[SETA][0])
                norm_wide(pe, s.pre, bank[SETA][1])
            pe.wait_ge(rstd_ready, s.rs + 1)
            block(1, SETA, s.u0 + KT)
            with pe.Fori(0, (FB - 3) // 2) as i:
                for j, set_ in enumerate((SETB, SETA)):
                    pe.wait_ge(bank_read, count(s.read0 + 4 * (j + 1), i, 8))
                    block(2 + j, set_, s.u0 + (2 + j) * KT, i)
            pe.wait_ge(bank_read, s.read0 + 4 * (FB - 2))
            block(FB - 1, SETB, s.u0 + (FB - 1) * KT)
            for half, set_ in enumerate((SETA, SETB)):
                pe.wait_ge(bank_read, s.read0 + 4 * (FB - 1 + half))
                for k in range(FT):
                    if half == 0:
                        pe.wait_ge(mid_lo_ready, s.mid0 + k + 1)
                    unit_products(pe, [o[:] for o in bank[set_]], mid_hi[:, k, :], mid_lo[:, k, :],
                                  k == 0, k == FT - 1, s.u1 + half * FT + k)
            output_tensor(pe, s)

        def input_parts_scalar(act, s, updates):
            for k in range(KT):
                if updates:
                    act.wait_ge(h_ready, KT * (updates - 1) + k + 1)
                gain = "kv_norm" if s.kv is not None else s.gain_in
                act.activation(x_hi[:, k, :], h[:, k, :], ACT.Copy, scale=vcol(gain, k)).then_inc(x_hi_ready, 1)
                square(act, s.pre, k, h[:, k, :])
            if s.kv is not None:
                for k in range(KT):
                    act.wait_ge(w_used, s.kv + k + 1)
                    act.activation(x_hi[:, k, :], h[:, k, :], ACT.Copy, scale=vcol(s.gain_in, k)).then_inc(x_hi_ready, 1)

        def input_low(dve, s, k, gain, x0):
            dve.wait_ge(x_hi_ready, x0 + k + 1)
            dve.scalar_tensor_tensor(out=x_lo[:, k, :], in0=h[:, k, :], scalar=vcol(gain, k),
                                     in1=x_hi[:, k, :].bitcast(F32), op0=ALU.mult, op1=ALU.subtract).then_inc(x_lo_ready, 1)

        def input_parts_vector(dve, s, last):
            for k in range(KT):
                if last is not None:
                    update_h(dve, last, k)
                if s.kv is None:
                    input_low(dve, s, k, s.gain_in, s.x0)
                else:
                    input_low(dve, s, k, "kv_norm", s.x0 - KT)
                add_square(dve, s.pre, k)
            if s.kv is not None:
                for k in range(KT):
                    input_low(dve, s, k, s.gain_in, s.x0)

        def ffn_scalar(act, s):
            norm_root(act, s.pre, bank[SETA][0], D)
            act.wait_ge(wide_ready, s.pre.n + 1)
            act.activation(rstd[:], bank[SETA][1][:], ACT.Copy).then_inc(rstd_ready, 1)

            def block(b, i=None):
                for p in range(2):
                    act.wait_ge(bank_read, count(s.read0 + 4 * b + p + 1, i, 8))
                    act.activation(g_buf[:, p, :], g_buf[:, p, :], ACT.Silu).then_inc(silu_ready, 1)
                for p in range(2):
                    act.wait_ge(prod_ready, count(s.mid0 + 2 * b + p + 1, i, 4))
                    o = mid_hi[:, 2 * b + p, :] if i is None else \
                        mid_hi[:, bass.ds(i * 4 + (2 * b + p), 1), :].rearrange("p a t -> p (a t)")
                    act.activation(o, u_buf[:, p, :], ACT.Copy).then_inc(mid_hi_ready, 1)

            block(0)
            with act.Fori(0, (FB - 1) // 2) as i:
                for j in range(2):
                    block(1 + j, i)
            output_scalar(act, s)

        def ffn_vector(dve, s):
            norm_diag(dve, s.pre)
            if s.kv is not None:
                kv_vector(dve, s)

            def block(b, set_, i=None):
                dve.wait_ge(w_used, count(s.u0 + (b + 1) * KT, i, 2 * KT))
                dve.wait_ge(rstd_ready, s.rs + 1)
                for p in range(2):
                    dve.tensor_tensor(g_buf[:, p, :], bank[set_][p][:], rstd[:], ALU.mult).then_inc(bank_read, 1)
                for p in range(2):
                    if b:
                        dve.wait_ge(mid_lo_ready, count(s.mid0 + 2 * b + p - 1, i, 4))
                    dve.tensor_tensor(u_buf[:, p, :], bank[set_][2 + p][:], rstd[:], ALU.mult).then_inc(bank_read, 1)
                for p in range(2):
                    dve.wait_ge(silu_ready, count(s.mid0 + 2 * b + p + 1, i, 4))
                    dve.wait_ge(bank_read, count(s.read0 + 4 * b + p + 3, i, 8))
                    dve.tensor_tensor(u_buf[:, p, :], g_buf[:, p, :], u_buf[:, p, :], ALU.mult).then_inc(prod_ready, 1)
                for p in range(2):
                    dve.wait_ge(mid_hi_ready, count(s.mid0 + 2 * b + p + 1, i, 4))
                    tile = slice(2 * b + p, 2 * b + p + 1) if i is None else bass.ds(i * 4 + (2 * b + p), 1)
                    lo, hi = (x[:, tile, :].rearrange("p a t -> p (a t)") for x in (mid_lo, mid_hi))
                    dve.tensor_tensor(lo, u_buf[:, p, :], hi.bitcast(F32), ALU.subtract).then_inc(mid_lo_ready, 1)

            block(0, SETB)
            with dve.Fori(0, (FB - 1) // 2) as i:
                block(1, SETA, i)
                block(2, SETB, i)
            dve.wait_ge(mid_lo_ready, s.mid0 + FT)
            output_vector(dve, s)

        def update_h(dve, s, k):
            if k == 0:
                dve.wait_ge(wide_ready, s.post.n + 1)
                dve.wait_ge(f_ready, s.h0 + KT)
            dve.tensor_tensor(f[:, k, :], f[:, k, :], bank[SETA][1][:], ALU.mult).then_inc(tmp_ready, 1)
            dve.wait_ge(tmp_ready, s.h0 + k + 1)
            dve.tensor_tensor(h[:, k, :], h[:, k, :], f[:, k, :], ALU.add).then_inc(h_ready, 1)

        r_arr = sb("r_arr", [P, KT, T], at=where["mid_hi"])
        k_arr = sb("k_arr", [P, KT, T], at=where["r_arr"] + 4 * KT * T)
        v_arr = sb("v_arr", [P, TT, D], at=where["k_arr"] + 4 * KT * T)
        s_arr = sb("s_arr", [P, KT, T], at=where["v_arr"] + 4 * KT * T)
        u_arr = sb("u_arr", [P, KT, T + 1], at=where["s_arr"] + 4 * KT * T)
        tg_hi = sb("tg_hi", [P, T], F32R, at=where["u_arr"] + 16448)
        tg_lo = sb("tg_lo", [P, T], F32R, at=where["tg_hi"] + 4 * T)
        assert where["tg_lo"] + 4 * T <= where["mid_hi"] + 2 * 4 * FT * T
        a_arr = sb("a_arr", [P, KT, T], at=where["f"])
        wa_hi = sb("wa_hi", [P, T], F32R)
        wa_lo = sb("wa_lo", [P, T], F32R)
        reset = sb("reset", [P, T])
        omu = sb("omu", [P, 6 * KT])
        head_a = sb("head_a", [HEADS, T])
        head_b = sb("head_b", [HEADS, T], at=where["rstd"])
        head_c = sb("head_c", [HEADS, T], at=where["diag"])
        fac = sb("fac", [P, KT, CHUNKS])
        fac_log = sb("fac_log", [P, KT, CHUNKS])
        gn_eps = sb("gn_eps", [P, 1])
        tmp = [sb(f"tmp{j}", [P, T], at=where["u_arr"] + 4 * T * j) for j in range(8)]
        wa_raw, tg_raw = v_arr[:, 0, 0:T], v_arr[:, 1, 0:T]
        at_ = [where["x_hi"]]

        def pair_buffer(name, shape):
            t = sb(name, shape, at=at_[0])
            at_[0] += 4 * int(np.prod(shape[1:]))
            assert at_[0] <= where["x_hi"] + 2 * 4 * KT * T
            return t

        op_a, op_r, op_b, op_k = (pair_buffer("op_" + n, [P, T]) for n in "arbk")
        op_v, bt_mat, kt_mat = (pair_buffer(n, [P, TT, P]) for n in ("op_v", "bt_mat", "kt_mat"))
        x_mat, xt_mat, e_mat, z_mat, mab_t, mak_t, mrb_t, mrk_t = (pair_buffer(n, [P, 8, CH]) for n in (
            "x_mat", "xt_mat", "e_mat", "z_mat", "mab_t", "mak_t", "mrb_t", "mrk_t"))
        rhs_s = sb("rhs_s", [P, 2, CH], at=where["sq"])
        sa_s = sb("sa_s", [P, 2, CH], at=where["sq"] + 512)
        st_s = sb("st_s", [P, CH], at=where["sq"] + 1024)
        st_f = sb("st_f", [P, CH], at=where["sq"] + 1280)
        fac_b = sb("fac_b", [P, CHUNKS], at=where["sq"] + 1536)

        class Rwkv:
            def __init__(self, first_unit, x_tiles, updates):
                self.x0, self.h0 = x_tiles, KT * updates
                self.n_lora = first_unit
                self.n_k = first_unit + KT
                self.n_r = self.n_k + 2 * KT
                self.n_lora2 = self.n_r + 2 * KT
                self.n_v = self.n_lora2 + 4
                self.n_g = self.n_v + 2 * KT
                self.u1 = self.n_g + 2
                self.rows = KT
                self.end = self.u1 + 2 * KT
                self.pre, self.post = Norm(KT), Norm(KT)
                self.gain_in, self.gain_out, self.bias, self.half = "norm02", "norm03", None, 1.0

        u_ready = sem("u_ready")
        mix_ready = sem("mix_ready")
        mixed = sem("mixed")
        each = range(KT)
        quad = [range(4), range(4, 8)]
        rp = Steps("rwkv_pe", ["sums", ("widen", 0), ("widen", 1)] +
                   [l for k in each for l in [("bonus", k)] + [("widen", k + 2)] * (k + 2 < KT)])
        ra = Steps("rwkv_act", ["w_in", "a_in", "g_in", "wa_hi", "tg_hi"] +
                   [(n, m) for n in ("k", "r", "sg", "a", "sq") for m in each] +
                   [("v", 0, t) for t in range(TT)] + ["norm"] + [("v", 1, t) for t in range(TT)] +
                   [(n, k) for k in each for n in ("Ep", "Em", "Ea", "fac")] + ["bonus"])
        rv = Steps("rwkv_dve", ["omu", "zero", "reset", "reset0", "gn_eps", "wa_lo", "tg_lo", "max", "rec"] +
                   [(n, k) for k in each for n in "cum cm cp fl kk t k2 rk b R K B A".split()])

        X_ORDER = [(i, k) for k in each for i in (1, 4, 5)] + [(i, k) for i in (2, 0, 3) for k in each]

        def x_free(s, q):
            q -= KT
            if q < 3 * KT:
                return s.n_lora + q // 3 + 1
            return (s.n_k, s.n_r, s.n_v)[(q - 3 * KT) // KT] + KT + q % KT + 1

        def rwkv_tensor(pe, s):
            sa, sb_ = bank[SETA], bank[SETB]
            norm_sums(pe, s.pre, sa[0])
            norm_wide(pe, s.pre, sa[1])
            for k in each:
                n = s.n_lora + k
                pe.wait_ge(w_lo_ready, n + 1)
                for j in range(3):
                    q = 3 * k + j
                    pe.wait_ge(x_lo_ready, s.x0 + q + 1)
                    o, c, z = sb_[j // 2], slice(j * P, (j + 1) * P), q % KT
                    first, last = k == 0 and j != 1, k == KT - 1 and j != 0
                    pe.matmul(o[:], w_hi[:, n % RW, c], x_hi[:, z, :], start=first, stop=False)
                    pe.matmul(o[:], w_hi[:, n % RW, c], x_lo[:, z, :], start=False, stop=False)
                    done = pe.matmul(o[:], w_lo[:, n % RW, c], x_hi[:, z, :], start=False, stop=last)
                done.then_inc(w_used, 1)
            pe.wait_ge(u_ready, KT)
            for j, (n0, free_a, free_b) in enumerate(((s.n_k, None, ra("g_in")), (s.n_r, ra("k", 3), ra("k", 7)))):
                for b, (set_, free) in enumerate(((SETA, free_a), (SETB, free_b))):
                    if free:
                        pe.wait_ge(*free)
                    for k in each:
                        if b == 0:
                            pe.wait_ge(x_lo_ready, s.x0 + (3 + j) * KT + k + 1)
                        unit_products(pe, [o[:] for o in bank[set_]], x_hi[:, k, :], x_lo[:, k, :],
                                      k == 0, k == KT - 1, n0 + b * KT + k)
            pe.wait_ge(*rv("wa_lo"))
            for j, free in enumerate((ra("r", 3), ra("r", 7), ra("sg", 3), ra("sg", 7))):
                pe.wait_ge(*free)
                unit_products(pe, [o[:] for o in bank[(SETA, SETB)[j % 2]]], wa_hi[:], wa_lo[:], True, True, s.n_lora2 + j)

            def v_unit(b, k):
                if b == 0:
                    pe.wait_ge(x_lo_ready, s.x0 + 5 * KT + k + 1)
                if k == 0:
                    pe.wait_ge(*(ra("v", 0, TT - 1) if b else ra("a", 3)))
                n = s.n_v + b * KT + k
                pe.wait_ge(w_lo_ready, n + 1)
                for t in range(TT):
                    c = slice(t * P, (t + 1) * P)
                    pe.matmul(sa[t][:], x_hi[:, k, c], w_hi[:, n % RW, :], start=k == 0, stop=False)
                    pe.matmul(sa[t][:], x_lo[:, k, c], w_hi[:, n % RW, :], start=False, stop=False)
                    done = pe.matmul(sa[t][:], x_hi[:, k, c], w_lo[:, n % RW, :], start=False, stop=k == KT - 1)
                done.then_inc(w_used, 1)

            def widen(k):
                if k == 0:
                    pe.wait_ge(*rv("rec"))
                if k >= 2:
                    pe.wait_ge(*rv("kk", k - 2))
                pe.matmul(sb_[1 + k % 2][:], spread[:, k, :], head_b[:], start=True, stop=True).then_inc(*rp.tell("widen", k))

            for k in each:
                v_unit(0, k)
            pe.wait_ge(*ra("a", 7))
            for k in each:
                pe.wait_ge(*ra("sq", k))
                done = pe.matmul(sb_[0][0:HEADS, :], gather[:, k, :], tmp[k][:], start=k == 0, stop=k == KT - 1)
            done.then_inc(*rp.tell("sums"))
            for k in each:
                v_unit(1, k)
                if k == 3:
                    widen(0)
                    widen(1)
            for k in each:
                pe.wait_ge(*rv("rk", k))
                pe.matmul(sb_[3][0:HEADS, :], gather[:, k, :], tmp[1][:], start=k == 0, stop=k == KT - 1).then_inc(*rp.tell("bonus", k))
                if k + 2 < KT:
                    widen(k + 2)

        def rwkv_scalar(act, s):
            for k in each:
                act.wait_ge(h_ready, s.h0 - KT + k + 1)
                square(act, s.pre, k, h[:, k, :])
            norm_root(act, s.pre, bank[SETA][0], D)

            def mix(q):
                i, k = X_ORDER[q]
                act.wait_ge(u_ready, k + 1)
                if q >= 2:
                    act.wait_ge(x_lo_ready, s.x0 + q - 1)
                act.activation(sq[:, q % 2, :], u_arr[:, k, 0:T], ACT.Copy, scale=vcol(f"mu{i}", k)).then_inc(mix_ready, 1)

            def tile(q):
                if q + 1 < len(X_ORDER):
                    mix(q + 1)
                act.wait_ge(mixed, q + 1)
                if q >= KT:
                    act.wait_ge(w_used, x_free(s, q))
                act.activation(x_hi[:, q % KT, :], sq[:, q % 2, :], ACT.Copy).then_inc(x_hi_ready, 1)

            mix(0)
            for q in range(3 * KT):
                tile(q)
            act.wait_ge(w_used, s.n_k)
            act.activation(wa_raw[0:64, :], bank[SETB][0][0:64, :], ACT.Tanh).then_inc(*ra.tell("w_in"))
            act.activation(wa_raw[64:P, :], bank[SETB][0][64:P, :], ACT.Copy).then_inc(*ra.tell("a_in"))
            act.activation(tg_raw, bank[SETB][1][:], ACT.Sigmoid).then_inc(*ra.tell("g_in"))
            act.wait_ge(*ra("g_in"))
            act.activation(wa_hi[:], wa_raw, ACT.Copy).then_inc(*ra.tell("wa_hi"))
            act.activation(tg_hi[:], tg_raw, ACT.Copy).then_inc(*ra.tell("tg_hi"))
            for q in range(3 * KT, 4 * KT):
                tile(q)
            for j, (n0, arr, name) in enumerate(((s.n_k, k_arr, "k"), (s.n_r, r_arr, "r"))):
                for b, set_ in enumerate((SETA, SETB)):
                    act.wait_ge(w_used, n0 + (b + 1) * KT)
                    for m in range(4):
                        act.activation(arr[:, 4 * b + m, :], bank[set_][m][:], ACT.Copy).then_inc(*ra.tell(name, 4 * b + m))
                    if b == 0:
                        for k in each:
                            tile((4 + j) * KT + k)
            for j in range(4):
                act.wait_ge(w_used, s.n_lora2 + j + 1)
                arr, name, bias = ((s_arr, "sg", "w0"), (a_arr, "a", "a0"))[j // 2]
                for m in range(4):
                    k = 4 * (j % 2) + m
                    act.activation(arr[:, k, :], bank[(SETA, SETB)[j % 2]][m][:], ACT.Sigmoid, bias=vcol(bias, k)).then_inc(*ra.tell(name, k))
            act.wait_ge(mixed, len(X_ORDER))
            for k in each:
                act.activation(tmp[k][:], k_arr[:, k, :], ACT.Square, scale=vcol("k_k", k)).then_inc(*ra.tell("sq", k))
            for b in range(2):
                act.wait_ge(w_used, s.n_v + (b + 1) * KT)
                for t in range(TT):
                    act.activation(v_arr[:, t, b * T:(b + 1) * T], bank[SETA][t][:], ACT.Copy).then_inc(*ra.tell("v", b, t))
                if b == 0:
                    act.wait_ge(*rp("sums"))
                    act.activation(head_a[:], bank[SETB][0][0:HEADS, :], ACT.Sqrt).then_inc(*ra.tell("norm"))
            for k in each:
                act.wait_ge(*rv("cp", k))
                if k:
                    act.wait_ge(*rv("A", k - 1))
                act.activation(tmp[5][:], tmp[3][:], ACT.Exp, scale=-KAPPA).then_inc(*ra.tell("Ep", k))
                act.activation(tmp[6][:], tmp[3][:], ACT.Exp, scale=KAPPA).then_inc(*ra.tell("Em", k))
                act.activation(tmp[7][:], tmp[4][:], ACT.Exp, scale=-KAPPA).then_inc(*ra.tell("Ea", k))
                act.wait_ge(*rv("fl", k))
                act.activation(fac[:, k, 0:CHUNKS - 1], fac_log[:, k, 0:CHUNKS - 1], ACT.Exp, scale=-KAPPA).then_inc(*ra.tell("fac", k))
            act.wait_ge(*rp("bonus", KT - 1))
            act.activation(head_a[:], bank[SETB][3][0:HEADS, :], ACT.Copy).then_inc(*ra.tell("bonus"))

        def rwkv_vector(dve, s):
            mu0 = VEC.at["mu0"]
            dve.tensor_scalar(omu[:], vec[:, mu0:mu0 + 6 * KT], -1.0, 1.0, ALU.mult, ALU.add).then_inc(*rv.tell("omu"))
            norm_diag(dve, s.pre)
            dve.memset(u_arr[:, :, 0:1], 0.0).then_inc(*rv.tell("zero"))
            dve.memset(reset[:], 1.0).then_inc(*rv.tell("reset"))
            dve.wait_ge(*rv("reset"))
            dve.memset(reset[:].rearrange("p (c t) -> p c t", t=CH)[:, :, 0:1], 0.0).then_inc(*rv.tell("reset0"))
            dve.memset(gn_eps[:], 64e-5).then_inc(*rv.tell("gn_eps"))
            dve.wait_ge(*rv("zero"))
            dve.wait_ge(wide_ready, s.pre.n + 1)
            for k in each:
                dve.scalar_tensor_tensor(out=u_arr[:, k, 1:T + 1], in0=h[:, k, :], scalar=vcol(s.gain_in, k),
                                         in1=bank[SETA][1][:], op0=ALU.mult, op1=ALU.mult).then_inc(u_ready, 1)

            def mixing(q):
                i, k = X_ORDER[q]
                dve.wait_ge(mix_ready, q + 1)
                dve.wait_ge(u_ready, k + 1)
                dve.scalar_tensor_tensor(out=sq[:, q % 2, :], in0=u_arr[:, k, 1:T + 1], scalar=omu[:, i * KT + k:i * KT + k + 1],
                                         in1=sq[:, q % 2, :], op0=ALU.mult, op1=ALU.add).then_inc(mixed, 1)

            def tile(q):
                if q + 1 < len(X_ORDER):
                    mixing(q + 1)
                dve.wait_ge(x_hi_ready, s.x0 + q + 1)
                dve.tensor_tensor(x_lo[:, q % KT, :], sq[:, q % 2, :], x_hi[:, q % KT, :].bitcast(F32),
                                  ALU.subtract).then_inc(x_lo_ready, 1)

            dve.wait_ge(*rv("omu"))
            mixing(0)
            for q in range(3 * KT):
                tile(q)
            dve.wait_ge(*ra("tg_hi"))
            dve.tensor_tensor(wa_lo[:], wa_raw, wa_hi[:].bitcast(F32), ALU.subtract).then_inc(*rv.tell("wa_lo"))
            dve.tensor_tensor(tg_lo[:], tg_raw, tg_hi[:].bitcast(F32), ALU.subtract).then_inc(*rv.tell("tg_lo"))
            for q in range(3 * KT, len(X_ORDER)):
                tile(q)
            dve.wait_ge(*ra("norm"))
            dve.tensor_scalar(head_a[:], head_a[:], 1e-12, None, ALU.max).then_inc(*rv.tell("max"))
            dve.wait_ge(*rv("max"))
            dve.reciprocal(head_b[:], head_a[:]).then_inc(*rv.tell("rec"))
            for k in each:
                chunks = lambda t: t[:].rearrange("p (c t) -> p c t", t=CH)
                mid = chunks(tmp[2])[:, :, CH // 2 - 1:CH // 2]
                if k == 0:
                    dve.wait_ge(*rp("sums"))
                else:
                    dve.wait_ge(*ra("Ea", k - 1))
                    dve.wait_ge(*rv("fl", k - 1))
                dve.tensor_tensor_scan(tmp[2][:], reset[:], s_arr[:, k, :], 0.0, ALU.mult, ALU.add).then_inc(*rv.tell("cum", k))
                dve.wait_ge(*rv("cum", k))
                dve.tensor_tensor(chunks(tmp[3]), chunks(tmp[2]), mid.to_broadcast([P, CHUNKS, CH]), ALU.subtract).then_inc(*rv.tell("cm", k))
                dve.wait_ge(*rv("cm", k))
                dve.tensor_tensor(tmp[4][:], tmp[3][:], s_arr[:, k, :], ALU.subtract).then_inc(*rv.tell("cp", k))
                dve.tensor_tensor(fac_log[:, k, 0:CHUNKS - 1], chunks(tmp[3])[:, 0:CHUNKS - 1, CH - 1],
                                  chunks(tmp[2])[:, 1:CHUNKS, CH // 2 - 1], ALU.add).then_inc(*rv.tell("fl", k))
                dve.wait_ge(*rp("widen", k))
                dve.scalar_tensor_tensor(out=tmp[0][:], in0=k_arr[:, k, :], scalar=vcol("k_k", k), in1=bank[SETB][1 + k % 2][:],
                                         op0=ALU.mult, op1=ALU.mult).then_inc(*rv.tell("kk", k))
                if k:
                    dve.wait_ge(*rp("bonus", k - 1))
                dve.tensor_scalar(tmp[1][:], a_arr[:, k, :], 1.0, vcol("k_a", k), ALU.subtract, ALU.mult).then_inc(*rv.tell("t", k))
                dve.wait_ge(*rv("t", k))
                dve.scalar_tensor_tensor(out=k_arr[:, k, :], in0=tmp[1][:], scalar=1.0, in1=k_arr[:, k, :],
                                         op0=ALU.add, op1=ALU.mult).then_inc(*rv.tell("k2", k))
                dve.wait_ge(*rv("k2", k))
                dve.scalar_tensor_tensor(out=tmp[1][:], in0=r_arr[:, k, :], scalar=vcol("r_k", k), in1=k_arr[:, k, :],
                                         op0=ALU.mult, op1=ALU.mult).then_inc(*rv.tell("rk", k))
                dve.tensor_tensor(a_arr[:, k, :], tmp[0][:], a_arr[:, k, :], ALU.mult).then_inc(*rv.tell("b", k))
                dve.wait_ge(*ra("Ea", k))
                dve.wait_ge(*rv("b", k))
                dve.tensor_tensor(r_arr[:, k, :], r_arr[:, k, :], tmp[5][:], ALU.mult).then_inc(*rv.tell("R", k))
                dve.tensor_tensor(k_arr[:, k, :], k_arr[:, k, :], tmp[6][:], ALU.mult).then_inc(*rv.tell("K", k))
                dve.tensor_tensor(a_arr[:, k, :], a_arr[:, k, :], tmp[6][:], ALU.mult).then_inc(*rv.tell("B", k))
                dve.scalar_tensor_tensor(out=s_arr[:, k, :], in0=tmp[0][:], scalar=-1.0, in1=tmp[7][:],
                                         op0=ALU.mult, op1=ALU.mult).then_inc(*rv.tell("A", k))

        LEVELS = range(1, 6)
        LAST = CHUNKS - 1
        wp = Steps("pair_pe", ["tr", "ab", "ak", "rk"] + [(n, l) for l in LEVELS for n in ["z"] + ["xz"] * (l < 5) + ["zx"]] +
                   [(n, c) for c in range(CHUNKS) for n in ["s"] * (c > 0) + ["rhs", "sa"] + ["st"] * (c < LAST) + ["y"]])
        wa = Steps("pair_act", ["a", "r", "v", "bt", "mab"] + [("z", l) for l in LEVELS] +
                   [(n, c) for c in range(CHUNKS) for n in ["fade"] * (0 < c < LAST) + ["rhs", "sa"]])
        wv = Steps("pair_dve", ["b", "k", "fac", "kt", "mab", ("x1", 0), ("x1", 1), "xt1", ("x", 0), ("xt", 0), ("e", 1)] +
                   [(n, j) for n in ("mak", "mrb", "mrk") for j in range(2)] +
                   [s_ for l in LEVELS for s_ in [("z", l)] + [("e", l + 1)] * (l < 5) + [("x", l, 0), ("x", l)] * (l < 5) +
                    [("xt", l, 0), ("xt", l)]] +
                   [s_ for c in range(CHUNKS) for s_ in [("rhs", c), ("sa", c)] + [("st", c, 0), ("st", c)] * (c < LAST)] + [("y", 0), "y"])

        def half(j):
            return slice(j * 64, (j + 1) * 64)

        def rows4(j):
            return slice(4 * j, 4 * j + 4)

        def chunk(c):
            return slice(c * CH, (c + 1) * CH)

        def pairs_tensor(pe):
            sa, sb_ = bank[SETA], bank[SETB]
            pe.wait_ge(*rv("A", KT - 1))
            pe.wait_ge(*ra("bonus"))
            with pe.Fori(0, KT) as i:
                def hold(o):
                    pe.matmul(o[:, 0:1], ident[:], ident[:, 0:1], start=True, stop=True)

                def features_product(banks, at, left, right):
                    for c in range(CHUNKS):
                        for j in range(2):
                            done = pe.matmul(banks[j][half(c % 2), at + c // 2 * CH:at + (c // 2 + 1) * CH],
                                             left[half(j), chunk(c)], right[half(j), chunk(c)], start=True, stop=True)
                    return done

                def chunk_product(banks, left, right):
                    for b in range(8):
                        for p in range(2):
                            done = pe.matmul(banks[p][half(p), chunk(b)], left[half(p), b, :], right[half(p), b, :], start=True, stop=True)
                    return done

                pe.wait_ge(*wv("k", i=i))
                for o, op in ((sa[0], op_b), (sa[1], op_k)):
                    for t in range(TT):
                        done = pe.matmul(o[:, t * P:(t + 1) * P], op[:, t * P:(t + 1) * P], ident[:], start=True, stop=True)
                done.then_inc(*wp.tell("tr"))
                pe.wait_ge(*wa("r", i=i))
                hold(sa[2])
                features_product(sa[2:4], 0, op_b, op_a)
                features_product(sa[2:4], 4 * CH, op_a, op_b).then_inc(*wp.tell("ab"))
                features_product(sb_[0:2], 0, op_k, op_a)
                features_product(sb_[0:2], 4 * CH, op_b, op_r).then_inc(*wp.tell("ak"))
                features_product(sb_[2:4], 0, op_k, op_r).then_inc(*wp.tell("rk"))
                pe.wait_ge(*wa("mab", i=i))
                for l in LEVELS:
                    pe.wait_ge(*wv("e", l, i=i))
                    if l > 1:
                        pe.wait_ge(*wv("xt", l - 1, i=i))
                    hold(sa[0])
                    chunk_product(sa[0:2], e_mat, x_mat).then_inc(*wp.tell("z", l))
                    pe.wait_ge(*wa("z", l, i=i))
                    pe.wait_ge(*wv("z", l, i=i))
                    if l == 1:
                        pe.wait_ge(*wv("mrk", 1, i=i))
                    hold(sa[0])
                    if l < 5:
                        chunk_product(sa[2:4], xt_mat, z_mat).then_inc(*wp.tell("xz", l))
                    chunk_product(sb_[0:2], z_mat, xt_mat).then_inc(*wp.tell("zx", l))
                pe.wait_ge(*wv("xt", 5, i=i))
                pe.wait_ge(*wa("v", i=i))
                hold(sa[2])
                for c in range(CHUNKS):
                    p, t = c % 2, c // 2
                    two = range(2)
                    hp, tok = half(p), chunk(c)
                    if c:
                        pe.wait_ge(*wv("st", c - 1, i=i))
                        pe.wait_ge(*wp("y", c - 1, i=i))
                        hold(sa[2])
                        for j in two:
                            pe.matmul(sb_[j][hp, 0:CH], op_a[half(j), tok], st_s[half(j), :], start=True, stop=False)
                        for j in two:
                            done = pe.matmul(sb_[2 + j][half(j), tok], st_s[half(j), :], op_r[half(j), tok], start=True, stop=False)
                        done.then_inc(*wp.tell("s", c))
                        pe.wait_ge(*wp("s", c, i=i))
                        hold(sa[2])
                    for j in two:
                        done = pe.matmul(sb_[j][hp, 0:CH], mak_t[hp, 4 * j + t, :], op_v[hp, t, half(j)], start=c == 0, stop=True)
                    done.then_inc(*wp.tell("rhs", c))
                    for j in two:
                        pe.matmul(sb_[2 + j][half(j), tok], op_v[hp, t, half(j)], mrk_t[hp, 4 * j + t, :], start=c == 0, stop=False)
                    if c < LAST:
                        for j in two:
                            pe.matmul(sa[j][half(j), 0:CH], kt_mat[hp, t, half(j)], op_v[hp, t, half(j)], start=True, stop=False)
                    pe.wait_ge(*wa("rhs", c, i=i))
                    pe.wait_ge(*wv("rhs", c, i=i))
                    hold(sa[2])
                    for j in two:
                        done = pe.matmul(sb_[j][hp, CH:2 * CH], xt_mat[hp, 4 * j + t, :], rhs_s[hp, j, :], start=True, stop=True)
                    done.then_inc(*wp.tell("sa", c))
                    pe.wait_ge(*wa("sa", c, i=i))
                    pe.wait_ge(*wv("sa", c, i=i))
                    hold(sa[2])
                    if c < LAST:
                        for j in two:
                            done = pe.matmul(sa[j][half(j), 0:CH], bt_mat[hp, t, half(j)], sa_s[hp, j, :], start=False, stop=True)
                        done.then_inc(*wp.tell("st", c))
                    for j in two:
                        done = pe.matmul(sb_[2 + j][half(j), tok], sa_s[hp, j, :], mrb_t[hp, 4 * j + t, :], start=False, stop=True)
                    done.then_inc(*wp.tell("y", c))
                pe.wait_ge(*wv("y", i=i))

        def pairs_scalar(act):
            act.wait_ge(*rv("A", KT - 1))
            act.wait_ge(*ra("v", 1, TT - 1))
            with act.Fori(0, KT) as i:
                act.activation(op_a[:], s_arr[:, bass.ds(i, 1), :].rearrange("p a t -> p (a t)"), ACT.Copy).then_inc(*wa.tell("a"))
                act.activation(op_r[:], r_arr[:, bass.ds(i, 1), :].rearrange("p a t -> p (a t)"), ACT.Copy).then_inc(*wa.tell("r"))
                act.activation(op_v[:], v_arr[:, :, bass.ds(i * P, P)], ACT.Copy).then_inc(*wa.tell("v"))
                act.wait_ge(*wp("tr", i=i))
                act.activation(bt_mat[:].rearrange("p a t -> p (a t)"), bank[SETA][0][:], ACT.Copy).then_inc(*wa.tell("bt"))
                act.wait_ge(*wp("ab", i=i))
                act.activation(mab_t[:, rows4(0), :].rearrange("p a t -> p (a t)"), bank[SETA][2][:, 0:4 * CH], ACT.Copy).then_inc(*wa.tell("mab"))
                for l in LEVELS:
                    act.wait_ge(*wp("z", l, i=i))
                    act.activation(z_mat[half(0)].rearrange("p a t -> p (a t)"), bank[SETA][0][half(0), :], ACT.Copy).then_inc(*wa.tell("z", l))
                for c in range(CHUNKS):
                    hp = half(c % 2)
                    if 0 < c < LAST:
                        act.wait_ge(*wv("st", c - 1, i=i))
                        act.activation(st_f[:], st_s[:], ACT.Copy, scale=fac_b[:, c:c + 1]).then_inc(*wa.tell("fade", c))
                    act.wait_ge(*wp("rhs", c, i=i))
                    act.activation(rhs_s[hp, 0, :], bank[SETB][0][hp, 0:CH], ACT.Copy).then_inc(*wa.tell("rhs", c))
                    act.wait_ge(*wp("sa", c, i=i))
                    act.activation(sa_s[hp, 0, :], bank[SETB][0][hp, CH:2 * CH], ACT.Copy).then_inc(*wa.tell("sa", c))

        def pairs_vector(dve):
            sa, sb_ = bank[SETA], bank[SETB]
            dve.wait_ge(*rv("A", KT - 1))
            dve.wait_ge(*ra("fac", KT - 1))

            def mask(j, n):
                return masks[:, j:j + 1, :].to_broadcast([P, n, CH])

            def blocks(t, j=0):
                return t[:, j * 4 * CH:(j + 1) * 4 * CH].rearrange("p (a t) -> p a t", t=CH)

            with dve.Fori(0, KT) as i:
                dve.tensor_copy(op_b[:], a_arr[:, bass.ds(i, 1), :].rearrange("p a t -> p (a t)")).then_inc(*wv.tell("b"))
                dve.tensor_copy(op_k[:], k_arr[:, bass.ds(i, 1), :].rearrange("p a t -> p (a t)")).then_inc(*wv.tell("k"))
                dve.tensor_copy(fac_b[:, 0:LAST], fac[:, bass.ds(i, 1), 0:LAST].rearrange("p a t -> p (a t)")).then_inc(*wv.tell("fac"))
                dve.wait_ge(*wp("tr", i=i))
                dve.tensor_copy(kt_mat[:].rearrange("p a t -> p (a t)"), sa[1][:]).then_inc(*wv.tell("kt"))
                dve.wait_ge(*wp("ab", i=i))
                dve.tensor_copy(mab_t[:, rows4(1), :].rearrange("p a t -> p (a t)"), sa[3][:, 0:4 * CH]).then_inc(*wv.tell("mab"))
                dve.wait_ge(*wa("mab", i=i))
                for j in range(2):
                    dve.tensor_tensor(x_mat[:, rows4(j), :], blocks(sa[2 + j], 1), mask(6, 4), ALU.mult).then_inc(*wv.tell("x1", j))
                dve.wait_ge(*wv("mab", i=i))
                dve.tensor_tensor(xt_mat[:], mab_t[:], mask(0, 8), ALU.mult).then_inc(*wv.tell("xt1"))
                dve.wait_ge(*wv("xt1", i=i))
                dve.tensor_tensor(x_mat[:], x_mat[:], mask(9, 8), ALU.add).then_inc(*wv.tell("x", 0))
                dve.tensor_tensor(xt_mat[:], xt_mat[:], mask(9, 8), ALU.add).then_inc(*wv.tell("xt", 0))
                dve.tensor_tensor(e_mat[:], mab_t[:], mask(1, 8), ALU.mult).then_inc(*wv.tell("e", 1))
                dve.wait_ge(*wp("ak", i=i))
                for name, m, at, w in (("mak", mak_t, 0, 7), ("mrb", mrb_t, 1, 8)):
                    for j in range(2):
                        dve.tensor_tensor(m[:, rows4(j), :], blocks(sb_[j], at), mask(w, 4), ALU.mult).then_inc(*wv.tell(name, j))
                dve.wait_ge(*wp("rk", i=i))
                for j in range(2):
                    dve.tensor_tensor(mrk_t[:, rows4(j), :], blocks(sb_[2 + j]), mask(8, 4), ALU.mult).then_inc(*wv.tell("mrk", j))

                def add_banks(t, banks, name, l):
                    for p in range(2):
                        v = t[half(p)].rearrange("p a t -> p (a t)")
                        dve.tensor_tensor(v, v, banks[p][half(p), :], ALU.add).then_inc(*(wv.tell(name, l, 0) if p == 0 else wv.tell(name, l)))

                for l in LEVELS:
                    dve.wait_ge(*wp("z", l, i=i))
                    dve.tensor_copy(z_mat[half(1)].rearrange("p a t -> p (a t)"), sa[1][half(1), :]).then_inc(*wv.tell("z", l))
                    if l < 5:
                        dve.tensor_tensor(e_mat[:], mab_t[:], mask(l + 1, 8), ALU.mult).then_inc(*wv.tell("e", l + 1))
                        dve.wait_ge(*wp("xz", l, i=i))
                        add_banks(x_mat, sa[2:4], "x", l)
                    dve.wait_ge(*wp("zx", l, i=i))
                    add_banks(xt_mat, sb_[0:2], "xt", l)
                for c in range(CHUNKS):
                    hp = half(c % 2)
                    dve.wait_ge(*wp("rhs", c, i=i))
                    dve.tensor_copy(rhs_s[hp, 1, :], sb_[1][hp, 0:CH]).then_inc(*wv.tell("rhs", c))
                    dve.wait_ge(*wp("sa", c, i=i))
                    dve.tensor_copy(sa_s[hp, 1, :], sb_[1][hp, CH:2 * CH]).then_inc(*wv.tell("sa", c))
                    if c < LAST:
                        if c:
                            dve.wait_ge(*wa("fade", c, i=i))
                        else:
                            dve.wait_ge(*wv("fac", i=i))
                        dve.wait_ge(*wp("st", c, i=i))
                        for j in range(2):
                            signal = wv.tell("st", c, 0) if j == 0 else wv.tell("st", c)
                            o, d, fc = st_s[half(j), :], sa[j][half(j), 0:CH], fac_b[half(j), c:c + 1]
                            if c:
                                dve.scalar_tensor_tensor(out=o, in0=d, scalar=fc, in1=st_f[half(j), :], op0=ALU.mult, op1=ALU.add).then_inc(*signal)
                            else:
                                dve.tensor_scalar(o, d, fc, None, ALU.mult).then_inc(*signal)
                dve.wait_ge(*wp("y", LAST, i=i))
                for j in range(2):
                    dve.tensor_copy(r_arr[half(j), bass.ds(i, 1), :].rearrange("p a t -> p (a t)"),
                                    sb_[2 + j][half(j), :]).then_inc(*(wv.tell("y") if j else wv.tell("y", 0)))

        gp = Steps("group_pe", ["mean"] + [("mean", k) for k in each] + ["var"] + [("rstd", k) for k in each] + [(n, k) for k in each for n in ("bonus", "vt")])
        ga = Steps("group_act", ["mean"] + [("sq", k) for k in each] + ["root"] + [("vt", k) for k in each])
        gv = Steps("group_dve", [("sub", k) for k in each] + ["rec"] + [(n, k) for k in each for n in ("scale", "gain")] +
                   [(n, k) for k in each for n in ("bv", "add")] + [("gate", k) for k in each])

        def group_tensor(pe, s):
            sa, sb_ = bank[SETA], bank[SETB]
            end = KT - 1
            pe.wait_ge(*wv("y", i=end))
            for k in each:
                done = pe.matmul(sa[0][0:HEADS, :], gather[:, k, :], r_arr[:, k, :], start=k == 0, stop=k == end)
            done.then_inc(*gp.tell("mean"))
            pe.wait_ge(*ga("mean"))
            for k in each:
                if k >= 4:
                    pe.wait_ge(*gv("sub", k - 4))
                pe.matmul(sb_[k % 4][:], spread[:, k, :], head_b[:], start=True, stop=True).then_inc(*gp.tell("mean", k))
            for k in each:
                pe.wait_ge(*ga("sq", k))
                done = pe.matmul(sa[1][0:HEADS, :], gather[:, k, :], tmp[k][:], start=k == 0, stop=k == end)
            done.then_inc(*gp.tell("var"))
            pe.wait_ge(*gv("rec"))
            for k in each:
                if k >= 4:
                    pe.wait_ge(*gv("scale", k - 4))
                pe.matmul(sb_[k % 4][:], spread[:, k, :], head_b[:], start=True, stop=True).then_inc(*gp.tell("rstd", k))
            for k in each:
                if k >= 2:
                    pe.wait_ge(*gv("bv", k - 2))
                pe.matmul(sa[2 + k % 2][:], spread[:, k, :], head_a[:], start=True, stop=True).then_inc(*gp.tell("bonus", k))
                if k == 0:
                    pe.wait_ge(*ga("root"))
                if k >= 2:
                    pe.wait_ge(*ga("vt", k - 2))
                for t in range(TT):
                    done = pe.matmul(sa[k % 2][:, t * P:(t + 1) * P], v_arr[:, t, k * P:(k + 1) * P], ident[:], start=True, stop=True)
                done.then_inc(*gp.tell("vt", k))
            pe.wait_ge(*gv("scale", end))
            unit_products(pe, [o[:] for o in sb_], tg_hi[:], tg_lo[:], True, True, s.n_g)
            pe.wait_ge(*gv("bv", end))
            unit_products(pe, [o[:] for o in sa], tg_hi[:], tg_lo[:], True, True, s.n_g + 1)
            pe.wait_ge(*gv("gate", end))
            for b, set_ in enumerate((SETA, SETB)):
                for k in each:
                    if b == 0:
                        pe.wait_ge(x_lo_ready, s.x0 + len(X_ORDER) + k + 1)
                    unit_products(pe, [o[:] for o in bank[set_]], x_hi[:, k, :], x_lo[:, k, :], k == 0, k == end, s.u1 + b * KT + k)
            output_tensor(pe, s)

        def group_scalar(act, s):
            sa = bank[SETA]
            act.wait_ge(*gp("mean"))
            act.activation(head_b[:], sa[0][0:HEADS, :], ACT.Copy, scale=1.0 / 64).then_inc(*ga.tell("mean"))
            for k in each:
                act.wait_ge(*gv("sub", k))
                act.activation(tmp[k][:], r_arr[:, k, :], ACT.Square).then_inc(*ga.tell("sq", k))
            act.wait_ge(*gp("var"))
            act.activation(head_c[:], sa[1][0:HEADS, :], ACT.Sqrt, bias=gn_eps[0:HEADS, :], scale=1.0 / 64).then_inc(*ga.tell("root"))
            for k in each:
                act.wait_ge(*gp("vt", k))
                act.activation(tmp[k][:], sa[k % 2][:], ACT.Copy).then_inc(*ga.tell("vt", k))
            for k in each:
                act.wait_ge(*gv("gate", k))
                act.activation(x_hi[:, k, :], r_arr[:, k, :], ACT.Copy).then_inc(x_hi_ready, 1)
            output_scalar(act, s)

        def group_vector(dve, s):
            sa, sb_ = bank[SETA], bank[SETB]
            y = lambda k: r_arr[:, k, :]
            for k in each:
                dve.wait_ge(*gp("mean", k))
                dve.tensor_tensor(y(k), y(k), sb_[k % 4][:], ALU.subtract).then_inc(*gv.tell("sub", k))
            dve.wait_ge(*ga("root"))
            dve.reciprocal(head_b[:], head_c[:]).then_inc(*gv.tell("rec"))
            for k in each:
                dve.wait_ge(*gp("rstd", k))
                dve.tensor_tensor(y(k), y(k), sb_[k % 4][:], ALU.mult).then_inc(*gv.tell("scale", k))
                dve.wait_ge(*gv("scale", k))
                dve.tensor_scalar(y(k), y(k), vcol("gn_g", k), vcol("gn_b", k), ALU.mult, ALU.add).then_inc(*gv.tell("gain", k))
            for k in each:
                dve.wait_ge(*ga("vt", k))
                dve.tensor_tensor(tmp[k][:], tmp[k][:], sa[2 + k % 2][:], ALU.mult).then_inc(*gv.tell("bv", k))
                dve.wait_ge(*gv("bv", k))
                dve.tensor_tensor(y(k), y(k), tmp[k][:], ALU.add).then_inc(*gv.tell("add", k))
            for k in each:
                dve.wait_ge(w_used, s.n_g + 1 + k // 4)
                dve.wait_ge(*gv("add", KT - 1))
                dve.tensor_tensor(y(k), y(k), bank[(SETB, SETA)[k // 4]][k % 4][:], ALU.mult).then_inc(*gv.tell("gate", k))
            for k in each:
                dve.wait_ge(x_hi_ready, s.x0 + len(X_ORDER) + k + 1)
                dve.tensor_tensor(x_lo[:, k, :], y(k), x_hi[:, k, :].bitcast(F32), ALU.subtract).then_inc(x_lo_ready, 1)
            output_vector(dve, s)

        k_sh = sb("k_sh", [P, 2, T], at=where["wa_hi"])
        v_sh = sb("v_sh", [P, TT, KV], at=where["wa_hi"] + 4 * 2 * T)
        assert where["v_sh"] + 4 * TT * KV <= where["fac"]
        kvv = Steps("kv_dve", [("k", 0), ("k", 1), ("kb", 0), ("kb", 1)] + [("v", t) for t in range(TT)])

        def kv_tensor(pe, s):
            sb_ = bank[SETB]
            for k in each:
                n = s.kv + k
                pe.wait_ge(x_lo_ready, s.x0 - KT + k + 1)
                pe.wait_ge(w_lo_ready, n + 1)
                first, last, hi, lo = k == 0, k == KT - 1, w_hi[:, n % RW, :], w_lo[:, n % RW, :]
                for m in range(2):
                    c = slice(m * P, (m + 1) * P)
                    pe.matmul(sb_[m][:], hi[:, c], x_hi[:, k, :], start=first, stop=False)
                    pe.matmul(sb_[m][:], hi[:, c], x_lo[:, k, :], start=False, stop=False)
                    pe.matmul(sb_[m][:], lo[:, c], x_hi[:, k, :], start=False, stop=last)
                for t in range(TT):
                    o, c = sb_[2 + t // 2][:, t % 2 * KV:(t % 2 + 1) * KV], slice(t * P, (t + 1) * P)
                    pe.matmul(o, x_hi[:, k, c], hi[:, KV:], start=first and t % 2 == 0, stop=False)
                    pe.matmul(o, x_lo[:, k, c], hi[:, KV:], start=False, stop=False)
                    done = pe.matmul(o, x_hi[:, k, c], lo[:, KV:], start=False, stop=last and t % 2 == 1)
                done.then_inc(w_used, 1)
            norm_sums(pe, s.pre, bank[SETA][0])
            norm_wide(pe, s.pre, bank[SETA][1])
            pe.wait_ge(*kvv("v", TT - 1))

        def kv_vector(dve, s):
            sb_ = bank[SETB]
            dve.wait_ge(rstd_ready, s.rs + 1)
            dve.wait_ge(w_used, s.kv + KT)
            dve.wait_ge(diag_ready, (1 + TT) * (s.pre.n + 1))
            for m in range(2):
                dve.tensor_tensor(k_sh[:, m, :], sb_[m][:], rstd[:], ALU.mult).then_inc(*kvv.tell("k", m))
            for m in range(2):
                dve.wait_ge(*kvv("k", m))
                dve.tensor_scalar(k_sh[:, m, :], k_sh[:, m, :], vcol("b_k", m), None, ALU.add).then_inc(*kvv.tell("kb", m))
            for t in range(TT):
                dve.scalar_tensor_tensor(out=v_sh[:, t, :], in0=sb_[2 + t // 2][:, t % 2 * KV:(t % 2 + 1) * KV], scalar=rinv[:, t:t + 1],
                                         in1=rows[:, 0:KV], op0=ALU.mult, op1=ALU.add).then_inc(*kvv.tell("v", t))

        at_[0] = where["mid_hi"]

        def mid_buffer(name, shape, dt=F32):
            t = sb(name, shape, dt, at=at_[0])
            at_[0] += -(-4 * int(np.prod(shape[1:])) // 64) * 64
            assert at_[0] <= where["mid_hi"] + 2 * 4 * FT * T
            return t

        q_t, o_t = (mid_buffer(n, [P, KT, T]) for n in ("q_t", "o_t"))
        q_pair = mid_buffer("q_pair", [P, T])
        window = mid_buffer("window", [P, TT, 2 * P])
        score = mid_buffer("score", [P, 2, TT, 2 * P])
        prob_t = mid_buffer("prob_t", [P, 2, TT, 2, P])
        o_tok = mid_buffer("o_tok", [P, TT, P])
        top, neg, total, sink_e, den, inv = (mid_buffer(n, [P, 2, TT]) for n in ("top", "neg", "total", "sink_e", "den", "inv"))
        sink = mid_buffer("sink", [P, 2])
        ada_w = mid_buffer("ada_w", [P, 3 * D])
        ada_loaded = sem("ada_loaded")

        class Swa:
            def __init__(self, first_unit, x_tiles, updates):
                self.x0, self.h0 = x_tiles, KT * updates
                self.n_q, self.u1, self.rows = first_unit, first_unit + 2 * KT, KT
                self.end = self.u1 + 2 * KT
                self.pre, self.post = Norm(KT), Norm(KT)
                self.rs = new_rstd()
                self.gain_in, self.gain_out, self.bias, self.half, self.kv = "norm12", "norm13", "b_o", 1.0, None

        window_loaded = sem("window_loaded")
        mod_ready = sem("mod_ready")
        qv = Steps("query_dve", [(n, k) for k in each for n in ("q", "bias")])
        two = range(2)
        ap = Steps("swa_pe", [("score", j) for j in two] + [("turn", j) for j in two] + ["value", "turn_o", "ada"])
        aa = Steps("swa_act", [s_ for j in two for s_ in [("exp", j, n) for n in range(TT)] + [("sink", j)]] + [("turn", j) for j in two])
        av = Steps("swa_dve", ["q"] + ["sink"] + [s_ for j in two for s_ in [("mask", j, 0), ("mask", j, 1), ("top", j), ("neg", j)]] +
                   [s_ for j in two for s_ in [("den", j), ("inv", j)]] + [("turn", j) for j in two] + [("o", j) for j in two] + ["turn_o", "ada"])
        SWA_HALF = KT // 2

        def swa_tensor(pe, s):
            sa, sb_ = bank[SETA], bank[SETB]
            for b, set_ in enumerate((SETB, SETA)):
                for k in each:
                    if b == 0:
                        pe.wait_ge(x_lo_ready, s.x0 + k + 1)
                    unit_products(pe, [o[:] for o in bank[set_]], x_hi[:, k, :], x_lo[:, k, :], k == 0, k == KT - 1, s.n_q + b * KT + k)
                if b == 0:
                    norm_sums(pe, s.pre, sa[0])
                    norm_wide(pe, s.pre, sa[1])
                    pe.wait_ge(rstd_ready, s.rs + 1)
            pe.wait_ge(*qv("bias", KT - 1))

            def hold(o):
                pe.matmul(o[:, 0:1], ident[:], ident[:, 0:1], start=True, stop=True)

            for g in range(2):
                with pe.Fori(0, SWA_HALF) as i0:
                    i = i0 + g * SWA_HALF if g else i0
                    pe.wait_ge(*av("q", i=i))
                    hold(sa[0])
                    for j in two:
                        for n in range(TT):
                            k0 = max(n - 1, 0) * P
                            done = pe.matmul(sa[2 * j + n // 2][:, n % 2 * 2 * P:(n % 2 + 1) * 2 * P], q_pair[half(j), n * P:(n + 1) * P],
                                             k_sh[half(j), g, k0:k0 + 2 * P], start=True, stop=True)
                        done.then_inc(*ap.tell("score", j) if not g else (ap.sem, 1))
                    for j in two:
                        pe.wait_ge(*aa("exp", j, TT - 1, i=i))
                        for n in range(TT):
                            for t in range(2):
                                done = pe.matmul(sb_[2 * j + n // 2][:, (n % 2 * 2 + t) * P:(n % 2 * 2 + t + 1) * P],
                                                 score[:, j, n, t * P:(t + 1) * P], ident[:], start=True, stop=True)
                        done.then_inc(*ap.tell("turn", j) if not g else (ap.sem, 1))
                    for j in two:
                        pe.wait_ge(*aa("turn", j, i=i))
                        pe.wait_ge(*av("turn", j, i=i))
                        c = slice((2 * g + j) * 64, (2 * g + j + 1) * 64)
                        for n in range(TT):
                            for t in range(2):
                                done = pe.matmul(sa[0][:, n * P + j * 64:n * P + (j + 1) * 64], prob_t[:, j, n, t, :],
                                                 v_sh[:, max(n - 1, 0) + t, c], start=t == 0, stop=t == 1)
                    done.then_inc(*ap.tell("value") if not g else (ap.sem, 1))
                    pe.wait_ge(*av("o", 1, i=i))
                    for n in range(TT):
                        done = pe.matmul(sb_[0][:, n * P:(n + 1) * P], o_tok[:, n, :], ident[:], start=True, stop=True)
                    done.then_inc(*ap.tell("turn_o") if not g else (ap.sem, 1))
                    pe.wait_ge(ada_loaded, i * 16 + 16)
                    for m in range(3 * KT):
                        done = pe.matmul(sa[3][:, m:m + 1], ada_w[:, m * P:(m + 1) * P], vec[:, bass.ds(i + VEC.at["c"], 1)], start=True, stop=True)
                    done.then_inc(*ap.tell("ada") if not g else (ap.sem, 1))
                    pe.wait_ge(*av("ada", i=i))
            for b, set_ in enumerate((SETA, SETB)):
                for k in each:
                    if b == 0:
                        pe.wait_ge(x_lo_ready, s.x0 + KT + k + 1)
                    unit_products(pe, [o[:] for o in bank[set_]], x_hi[:, k, :], x_lo[:, k, :], k == 0, k == KT - 1, s.u1 + b * KT + k)
            output_tensor(pe, s)

        def swa_scalar(act, s):
            act.wait_ge(w_used, s.n_q)
            act.dma_start(window[:], window_in).then_inc(window_loaded, 16)
            norm_root(act, s.pre, bank[SETA][0], D)
            act.wait_ge(wide_ready, s.pre.n + 1)
            act.activation(rstd[:], bank[SETA][1][:], ACT.Copy).then_inc(rstd_ready, 1)
            with act.Fori(0, KT) as i:
                act.dma_start(ada_w[:], ada_in[bass.ds(i, 1)].rearrange("a p c -> (a p) c")).then_inc(ada_loaded, 16)
                for j in two:
                    act.wait_ge(*av("neg", j, i=i))
                    for n in range(TT):
                        act.activation(score[:, j, n, :], score[:, j, n, :], ACT.Exp, bias=neg[:, j, n:n + 1],
                                       accum_out=total[:, j, n:n + 1]).then_inc(*aa.tell("exp", j, n))
                    act.activation(sink_e[:, j, :], neg[:, j, :], ACT.Exp, bias=sink[:, j:j + 1]).then_inc(*aa.tell("sink", j))
                for j in two:
                    act.wait_ge(*ap("turn", j, i=i))
                    act.activation(prob_t[:, j, 0:2], bank[SETB][2 * j][:].rearrange("p (n t q) -> p n t q", t=2, q=P), ACT.Copy).then_inc(*aa.tell("turn", j))
                act.wait_ge(*ap("ada", i=i))
            output_parts_scalar(act, s.x0 + KT, o_t, lambda k: av("turn_o", i=KT - 1))
            output_scalar(act, s)

        def output_parts_scalar(act, x0, arr, ready):
            for k in each:
                act.wait_ge(*ready(k))
                act.activation(x_hi[:, k, :], arr[:, k, :], ACT.Copy).then_inc(x_hi_ready, 1)

        def output_parts_vector(dve, x0, arr):
            for k in each:
                dve.wait_ge(x_hi_ready, x0 + k + 1)
                dve.tensor_tensor(x_lo[:, k, :], arr[:, k, :], x_hi[:, k, :].bitcast(F32), ALU.subtract).then_inc(x_lo_ready, 1)

        def swa_vector(dve, s):
            sa, sb_ = bank[SETA], bank[SETB]
            norm_diag(dve, s.pre)
            dve.wait_ge(rstd_ready, s.rs + 1)
            for k in each:
                dve.wait_ge(w_used, s.n_q + (k // 4 + 1) * KT)
                dve.tensor_tensor(q_t[:, k, :], bank[(SETB, SETA)[k // 4]][k % 4][:], rstd[:], ALU.mult).then_inc(*qv.tell("q", k))
                dve.wait_ge(*qv("q", k))
                dve.tensor_scalar(q_t[:, k, :], q_t[:, k, :], vcol("b_q", k), None, ALU.add).then_inc(*qv.tell("bias", k))
            dve.wait_ge(*qv("bias", KT - 1))
            dve.wait_ge(window_loaded, 16)
            dve.tensor_copy(mod[:], vec[:, VEC.at["b_ada"]:VEC.at["b_ada"] + 3 * KT]).then_inc(mod_ready, 1)
            dve.wait_ge(mod_ready, 1)
            with dve.Fori(0, KT) as i:
                dve.tensor_copy(q_pair[:], q_t[:, bass.ds(i, 1), :].rearrange("p a t -> p (a t)")).then_inc(*av.tell("q"))
                dve.tensor_copy(sink[:], rows[:, bass.ds(i * 2 + KV, 2)]).then_inc(*av.tell("sink"))
                for j in two:
                    dve.wait_ge(*ap("score", j, i=i))
                    for b in two:
                        dve.scalar_tensor_tensor(out=score[:, j, 2 * b:2 * b + 2, :], in0=sa[2 * j + b][:].rearrange("p (n k) -> p n k", n=2),
                                                 scalar=0.125, in1=window[:, 2 * b:2 * b + 2, :], op0=ALU.mult, op1=ALU.add).then_inc(*av.tell("mask", j, b))
                    dve.wait_ge(*av("mask", j, 1, i=i))
                    dve.tensor_reduce(top[:, j, :], score[:, j], mybir.AxisListType.X, ALU.max).then_inc(*av.tell("top", j))
                    dve.wait_ge(*av("top", j, i=i))
                    dve.tensor_scalar(neg[:, j, :], top[:, j, :], sink[:, j:j + 1], -1.0, ALU.max, ALU.mult).then_inc(*av.tell("neg", j))
                for j in two:
                    dve.wait_ge(*aa("sink", j, i=i))
                    dve.tensor_tensor(den[:, j, :], total[:, j, :], sink_e[:, j, :], ALU.add).then_inc(*av.tell("den", j))
                    dve.wait_ge(*av("den", j, i=i))
                    dve.reciprocal(inv[:, j, :], den[:, j, :]).then_inc(*av.tell("inv", j))
                for j in two:
                    dve.wait_ge(*ap("turn", j, i=i))
                    dve.tensor_copy(prob_t[:, j, 2:4], sb_[2 * j + 1][:].rearrange("p (n t q) -> p n t q", t=2, q=P)).then_inc(*av.tell("turn", j))
                dve.wait_ge(*ap("value", i=i))
                for j in two:
                    dve.tensor_tensor(o_tok[:, :, half(j)], sa[0][:].rearrange("p (n c) -> p n c", n=TT)[:, :, half(j)],
                                      inv[:, j, :].rearrange("p (n o) -> p n o", o=1).to_broadcast([P, TT, 64]), ALU.mult).then_inc(*av.tell("o", j))
                dve.wait_ge(*ap("turn_o", i=i))
                dve.tensor_copy(o_t[:, bass.ds(i, 1), :].rearrange("p a t -> p (a t)"), sb_[0][:]).then_inc(*av.tell("turn_o"))
                dve.wait_ge(*ap("ada", i=i))
                dve.tensor_tensor(mod[:], sa[3][:, 0:3 * KT], mod[:], ALU.add).then_inc(*av.tell("ada"))
            output_parts_vector(dve, s.x0 + KT, o_t)
            output_vector(dve, s)


        at_[0] = where["mid_hi"]
        sb_q, sb_k, sb_v, sb_z = (mid_buffer(n, [P, 4, T]) for n in ("sb_q", "sb_k", "sb_v", "sb_z"))
        c_q, k_rot, c_kv = mid_buffer("c_q", [P, 3, T]), mid_buffer("k_rot", [P, T]), mid_buffer("c_kv", [P, 2, T])
        mla_z, gate_a, gate_b = mid_buffer("mla_z", [P, 4, T]), mid_buffer("gate_a", [P, KT, T]), mid_buffer("gate_b", [P, KT, T])
        x_norm = sb("x_norm", [P, KT, T], at=where["gate_a"])
        at_[0] = where["x_hi"]
        stick_z, stick_l = (pair_buffer(n, [P, 2, TRI]) for n in ("stick_z", "stick_l"))
        qs_pair, ks_pair = (pair_buffer(n, [P, T]) for n in ("qs_pair", "ks_pair"))
        vs_pair = pair_buffer("vs_pair", [P, TT, P])
        mla_q = sb("mla_q", [P, HEADS_B, T], at=where["x_hi"])
        mla_k = sb("mla_k", [P, HEADS_B, T], at=where["x_lo"])
        mla_v = sb("mla_v", [P, TT, T], at=where["sb_k"])
        cq_hi = sb("cq_hi", [P, 3, T], F32R, at=where["f"])
        cq_lo = sb("cq_lo", [P, 3, T], F32R, at=where["sb_v"])
        turns = sb("turns", [P, T], at=where["f"] + 3 * 4 * T)
        turns_q = sb("turns_q", [P, T], at=where["sb_v"] + 3 * 4 * T)
        angle, steps_ = (sb(n, [P, T], at=where["f"] + j * 4 * T) for j, n in enumerate(("angle", "steps")))
        pos = sb("pos", [P, T], mybir.dt.int32, at=where["f"] + 2 * 4 * T)
        fold = sb("fold", [P, P], at=where["f"] + 4 * 4 * T)
        tri = sb("tri", [P, P], at=where["fold"] + 4 * P)
        mask_a = sb("mask_a", [P, TRI], at=where["f"] + 5 * 4 * T)
        mask_b = sb("mask_b", [P, TRI], at=where["f"] + 5 * 4 * T)
        assert where["mask_b"] + 4 * TRI <= where["f"] + 4 * KT * T
        ckv_hi = sb("ckv_hi", [P, 2, T], F32R, at=where["wa_hi"])
        ckv_lo = sb("ckv_lo", [P, 2, T], F32R, at=where["wa_hi"] + 2 * 4 * T)
        score_b = sb("score_b", [P, 2, TRI], at=where["f"])
        prob_b = sb("prob_b", [P, 2, TRI], at=where["c_q"])
        qm_pair = sb("qm_pair", [P, 2, T], at=where["wa_hi"])
        km_pair = sb("km_pair", [P, 2, T], at=where["wa_hi"] + 2 * 4 * T)
        vm_pair = sb("vm_pair", [P, TT, P], at=where["sb_v"])
        ob_tok = sb("ob_tok", [P, TT, P], at=where["sb_v"] + 4 * T)
        at_[0] = where["sb_v"] + 2 * 4 * T
        top_b, neg_b, total_b, inv_b = (mid_buffer(n, [P, 2, TT]) for n in ("top_b", "neg_b", "total_b", "inv_b"))

        STICK_AT = [0, 512, 1024, 896]
        LATENT_AT = [896, 1024, 512, 0]
        BANKS = [(0, 512), (512, 1024), (1024, 1280)]

        class Second:
            def __init__(self, first_unit, x_tiles, updates):
                self.x0, self.h0 = x_tiles, KT * updates
                self.n_in = first_unit
                self.n_uq = first_unit + 11 * KT
                self.n_uk = self.n_uq + 6
                self.n_uv = self.n_uk + 4
                self.n_a = self.n_uv + 2
                self.n_b = self.n_a + 8
                self.n_out = self.n_b + 8
                self.end = self.n_out + 2 * KT
                self.rs = new_rstd()
                self.pre, self.q, self.kv, self.final = Norm(KT), Norm(3), Norm(2), Norm(KT)

        PROJ = [("q", 4), ("k", 4), ("v", 4), ("z", 4), ("cq", 4), ("ckv", 2), ("mz", 4), ("ga0", 4), ("ga1", 4), ("gb0", 4), ("gb1", 4)]
        tables_loaded = sem("tables_loaded")
        mask_loaded = sem("mask_loaded")
        pa = Steps("proj_act", ["sin"] + [(n, m) for n, tiles in PROJ for m in range(tiles)])
        pv = Steps("proj_dve", ["gain"] + [(n, k) for k in each for n in ("norm", "shift")] +
                   ["float", "angle", "near", "steps", "less1", "less2", "less3", "phase", "clip", "one"])
        sp_ = Steps("stick_pe", [("score", j) for j in two] + [("sum", j) for j in two] + [("o", j) for j in two])
        sact = Steps("stick_act", [(n, j) for j in two for n in ("abs", "exp", "ln")] + [("w", j) for j in two])
        sv = Steps("stick_dve", ["q", "k", "v"] + [("z", j, b) for j in two for b in range(3)] + [("soft", j) for j in two] +
                   [("less", j, b) for j in two for b in range(3)] + [("o", j) for j in two])
        lp = Steps("latent_pe", ["fold"])
        la = Steps("latent_act", [("cq_hi", k) for k in range(3)] + [("ckv_hi", k) for k in range(2)] + [("k", k) for k in each])
        lv = Steps("latent_dve", [("cq_lo", k) for k in range(3)] + [("ckv_lo", k) for k in range(2)] + ["turns_q", "rot"] +
                   [(n, k) for n in ("q", "k") for k in each] + [("v", t) for t in range(TT)])
        mp = Steps("mla_pe", [("score", j) for j in two] + [("turn", j) for j in two] + ["value", "turn_o"])
        ma = Steps("mla_act", [("exp", j, n) for j in two for n in range(TT)] + [("turn", j) for j in two])
        mv = Steps("mla_dve", ["q", "k", "v"] + [s_ for j in two for s_ in [("mask", j, b) for b in range(3)] + [("top", j, n) for n in range(TT)] + [("neg", j)]] +
                   [("inv", j) for j in two] + [("turn", j, b) for j in two for b in range(2)] + [("o", j) for j in two] + ["turn_o"])
        bv_ = Steps("branch_dve", [("a", k) for k in each] + [s_ for k in each for s_ in [("b", k), ("sum", k)]] + [("h", k) for k in each] + [("out", k) for k in each])

        def hold(pe, o):
            pe.matmul(o[:, 0:1], ident[:], ident[:, 0:1], start=True, stop=True)

        def second_tensor(pe, s):
            sa, sb_ = bank[SETA], bank[SETB]
            sets = (sb_, sa)
            norm_sums(pe, s.pre, sa[0])
            norm_wide(pe, s.pre, sa[1])
            for b, (name, tiles) in enumerate(PROJ):
                if b >= 2:
                    last, count_ = PROJ[b - 2]
                    pe.wait_ge(*pa(last, count_ - 1))
                for k in each:
                    n = s.n_in + b * KT + k
                    if b == 0:
                        pe.wait_ge(x_lo_ready, s.x0 + k + 1)
                    if name == "v":
                        moving_units(pe, sets[b % 2], x_hi, x_lo, k, KT, n)
                    else:
                        unit_products(pe, [o[:] for o in sets[b % 2][:tiles]], x_hi[:, k, :], x_lo[:, k, :], k == 0, k == KT - 1, n)

        def moving_units(pe, outs, hi, lo, k, tiles, n):
            pe.wait_ge(w_lo_ready, n + 1)
            for t in range(TT):
                c = slice(t * P, (t + 1) * P)
                pe.matmul(outs[t][:], hi[:, k, c], w_hi[:, n % RW, :], start=k == 0, stop=False)
                pe.matmul(outs[t][:], lo[:, k, c], w_hi[:, n % RW, :], start=False, stop=False)
                done = pe.matmul(outs[t][:], hi[:, k, c], w_lo[:, n % RW, :], start=False, stop=k == tiles - 1)
            done.then_inc(w_used, 1)

        def second_scalar(act, s):
            for k in each:
                act.wait_ge(h_ready, s.h0 - KT + k + 1)
                square(act, s.pre, k, h[:, k, :])
            for t, source in ((pos, pos_in), (fold, fold_in), (tri, tri_in), (mask_a, mask_a_in)):
                act.dma_start(t[:], source).then_inc(tables_loaded, 16)
            norm_root(act, s.pre, bank[SETA][0], D)
            for k in each:
                act.wait_ge(*pv("shift", k))
                act.activation(x_hi[:, k, :], x_norm[:, k, :], ACT.Copy).then_inc(x_hi_ready, 1)
            act.wait_ge(*pv("clip"))
            act.activation(turns[:], angle[:], ACT.Sin, scale=rope_c[:, 3:4]).then_inc(*pa.tell("sin"))
            dest = {"q": sb_q, "k": sb_k, "v": sb_v, "z": sb_z, "ckv": c_kv, "mz": mla_z}
            for b, (name, tiles) in enumerate(PROJ):
                act.wait_ge(w_used, s.n_in + (b + 1) * KT)
                func = {"z": ACT.Silu, "m": ACT.Silu, "g": ACT.Sigmoid}.get(name[0], ACT.Copy)
                for m in range(tiles):
                    if name[0] == "g":
                        out_ = (gate_a if name[1] == "a" else gate_b)[:, 4 * int(name[2]) + m, :]
                    elif name == "cq":
                        out_ = c_q[:, m, :] if m < 3 else k_rot[:]
                    else:
                        out_ = dest[name][:, m, :]
                    act.activation(out_, bank[(SETB, SETA)[b % 2]][m][:], func).then_inc(*pa.tell(name, m))

        def second_vector(dve, s):
            dve.scalar_tensor_tensor(out=gain_s[:], in0=mod[:, KT:2 * KT], scalar=1.0, in1=vec[:, VEC.at["gain2"]:VEC.at["gain2"] + KT],
                                     op0=ALU.add, op1=ALU.mult).then_inc(*pv.tell("gain"))
            norm_diag(dve, s.pre)
            dve.wait_ge(wide_ready, s.pre.n + 1)
            dve.wait_ge(*pv("gain"))
            for k in each:
                dve.scalar_tensor_tensor(out=x_norm[:, k, :], in0=h[:, k, :], scalar=gain_s[:, k:k + 1], in1=bank[SETA][1][:],
                                         op0=ALU.mult, op1=ALU.mult).then_inc(*pv.tell("norm", k))
                dve.wait_ge(*pv("norm", k))
                dve.tensor_scalar(x_norm[:, k, :], x_norm[:, k, :], mod[:, k:k + 1], None, ALU.add).then_inc(*pv.tell("shift", k))
                if k:
                    input_rest(dve, s, k - 1)
            input_rest(dve, s, KT - 1)
            dve.wait_ge(tables_loaded, 64)

            def step(name, before, out_, *a):
                if before:
                    dve.wait_ge(*pv(before))
                dve.tensor_scalar(out_[:], *a).then_inc(*pv.tell(name))

            dve.tensor_copy(steps_[:], pos[:]).then_inc(*pv.tell("float"))
            step("angle", "float", angle, steps_[:], rope_c[:, 0:1], None, ALU.mult)
            step("near", "angle", steps_, angle[:], 1.0 / (2 * np.pi), rope_c[:, 1:2], ALU.mult, ALU.add)
            dve.wait_ge(*pv("near"))
            dve.tensor_scalar(steps_[:], steps_[:], ROUND, ROUND, ALU.add, ALU.subtract).then_inc(*pv.tell("steps"))
            before = "steps"
            for j, part in enumerate(TURN):
                dve.wait_ge(*pv(before))
                before = f"less{j + 1}"
                dve.scalar_tensor_tensor(out=angle[:], in0=steps_[:], scalar=-part, in1=angle[:], op0=ALU.mult, op1=ALU.add).then_inc(*pv.tell(before))
            step("phase", before, angle, angle[:], rope_c[:, 2:3], None, ALU.add)
            step("clip", "phase", angle, angle[:], PI, -PI, ALU.min, ALU.max)
            dve.wait_ge(*pa("sin"))
            dve.memset(turns[0:64, :], 1.0).then_inc(*pv.tell("one"))

        def input_rest(dve, s, k):
            dve.wait_ge(x_hi_ready, s.x0 + k + 1)
            dve.tensor_tensor(x_lo[:, k, :], x_norm[:, k, :], x_hi[:, k, :].bitcast(F32), ALU.subtract).then_inc(x_lo_ready, 1)

        def stick_tensor(pe, s):
            sa, sb_ = bank[SETA], bank[SETB]
            banks = (sa, sb_)
            pe.wait_ge(*pa("gb1", 3))
            with pe.Fori(0, 4) as i:
                def at(j, t, first=0, last=None):
                    a = STICK_AT[t]
                    a0, a1 = a + first, a + (TT - t) * P
                    return banks[j][a // T][:, a0 % T:(a1 - 1) % T + 1]

                pe.wait_ge(*sv("k", i=i))
                hold(pe, sa[3])
                for t in range(TT):
                    for j in two:
                        done = pe.matmul(at(j, t), ks_pair[half(j), t * P:(t + 1) * P], qs_pair[half(j), t * P:], start=True, stop=True)
                        if t == TT - 1:
                            done.then_inc(*sp_.tell("score", j))
                for j in two:
                    pe.wait_ge(*sv("soft", j, i=i))
                    for t in range(TT):
                        for u in range(t, TT):
                            a = STICK_AT[u]
                            done = pe.matmul(at(j, t, (u - t) * P), (tri if u == t else ones)[:], stick_l[:, j, a:a + (TT - u) * P],
                                             start=u == t, stop=u == TT - 1)
                    done.then_inc(*sp_.tell("sum", j))
                for j in two:
                    pe.wait_ge(*sact("w", j, i=i))
                    pe.wait_ge(*sv("v", i=i))
                    hold(pe, banks[j][3])
                    for t in range(TT):
                        a = STICK_AT[t]
                        done = pe.matmul(banks[j][3][half(j), t * P:], vs_pair[:, t, half(j)], stick_l[:, j, a:a + (TT - t) * P],
                                         start=t == 0, stop=t == TT - 1)
                    done.then_inc(*sp_.tell("o", j))
                pe.wait_ge(*sv("o", 1, i=i))

        def stick_scalar(act, s):
            with act.Fori(0, 4) as i:
                for j in two:
                    act.wait_ge(*sv("z", j, 2, i=i))
                    act.activation(stick_l[:, j, :], stick_z[:, j, :], ACT.Abs).then_inc(*sact.tell("abs", j))
                    act.wait_ge(*sact("abs", j, i=i))
                    act.activation(stick_l[:, j, :], stick_l[:, j, :], ACT.Exp, scale=-1.0).then_inc(*sact.tell("exp", j))
                    act.wait_ge(*sact("exp", j, i=i))
                    act.activation(stick_l[:, j, :], stick_l[:, j, :], ACT.Ln, bias=1.0).then_inc(*sact.tell("ln", j))
                for j in two:
                    act.wait_ge(*sv("less", j, 2, i=i))
                    act.activation(stick_l[:, j, :], stick_z[:, j, :], ACT.Exp).then_inc(*sact.tell("w", j))

        def stick_vector(dve, s):
            banks = (bank[SETA], bank[SETB])
            dve.wait_ge(*pa("gb1", 3))
            dve.wait_ge(w_used, s.n_uq)
            with dve.Fori(0, 4) as i:
                dve.tensor_copy(qs_pair[:], sb_q[:, bass.ds(i, 1), :].rearrange("p a t -> p (a t)")).then_inc(*sv.tell("q"))
                dve.tensor_copy(ks_pair[:], sb_k[:, bass.ds(i, 1), :].rearrange("p a t -> p (a t)")).then_inc(*sv.tell("k"))
                dve.tensor_copy(vs_pair[:], sb_v[:, :, bass.ds(i * P, P)]).then_inc(*sv.tell("v"))
                for j in two:
                    dve.wait_ge(*sp_("score", j, i=i))
                    for b, (a0, a1) in enumerate(BANKS):
                        dve.scalar_tensor_tensor(out=stick_z[:, j, a0:a1], in0=banks[j][b][:, 0:a1 - a0], scalar=0.125, in1=mask_a[:, a0:a1],
                                                 op0=ALU.mult, op1=ALU.add).then_inc(*sv.tell("z", j, b))
                for j in two:
                    dve.wait_ge(*sact("ln", j, i=i))
                    dve.scalar_tensor_tensor(out=stick_l[:, j, :], in0=stick_z[:, j, :], scalar=0.0, in1=stick_l[:, j, :],
                                             op0=ALU.max, op1=ALU.add).then_inc(*sv.tell("soft", j))
                for j in two:
                    dve.wait_ge(*sp_("sum", j, i=i))
                    for b, (a0, a1) in enumerate(BANKS):
                        dve.tensor_tensor(stick_z[:, j, a0:a1], stick_z[:, j, a0:a1], banks[j][b][:, 0:a1 - a0], ALU.subtract).then_inc(*sv.tell("less", j, b))
                for j in two:
                    dve.wait_ge(*sp_("o", j, i=i))
                    v = sb_z[half(j), bass.ds(i, 1), :].rearrange("p a t -> p (a t)")
                    dve.tensor_tensor(v, banks[j][3][half(j), :], v, ALU.mult).then_inc(*sv.tell("o", j))

        def latent_tensor(pe, s):
            sa, sb_ = bank[SETA], bank[SETB]
            pe.wait_ge(*sv("o", 1, i=3))
            norm_sums(pe, s.q, sa[0])
            norm_wide(pe, s.q, sa[1])
            norm_sums(pe, s.kv, sa[0])
            norm_wide(pe, s.kv, sa[2])
            pe.wait_ge(*lv("rot"))
            pe.matmul(sa[3][:], fold[:], k_rot[:], start=True, stop=True).then_inc(*lp.tell("fold"))
            for b, set_ in enumerate((sb_, sa)):
                if b:
                    pe.wait_ge(rstd_ready, s.rs + 1)
                    pe.wait_ge(*la("k", KT - 1))
                for k in range(3):
                    if b == 0:
                        pe.wait_ge(*lv("cq_lo", k))
                    unit_products(pe, [o[:] for o in set_], cq_hi[:, k, :], cq_lo[:, k, :], k == 0, k == 2, s.n_uq + 3 * b + k)
            for b, set_ in enumerate((sb_, sa)):
                pe.wait_ge(*lv("q", 4 * b + 3))
                for k in range(2):
                    pe.wait_ge(*lv("ckv_lo", k))
                    unit_products(pe, [o[:] for o in set_], ckv_hi[:, k, :], ckv_lo[:, k, :], k == 0, k == 1, s.n_uk + 2 * b + k)
            pe.wait_ge(*lv("k", 3))
            for k in range(2):
                moving_units(pe, sb_, ckv_hi, ckv_lo, k, 2, s.n_uv + k)

        def latent_scalar(act, s):
            act.wait_ge(*sv("o", 1, i=3))
            act.dma_start(mask_b[:], mask_b_in).then_inc(mask_loaded, 16)
            for name, nm, src, hi, tiles in (("q", s.q, c_q, cq_hi, 3), ("kv", s.kv, c_kv, ckv_hi, 2)):
                for k in range(tiles):
                    act.activation(hi[:, k, :], src[:, k, :], ACT.Copy, scale=vcol(f"{name}_norm2", k)).then_inc(*la.tell(f"c{name}_hi", k))
                    square(act, nm, k, src[:, k, :])
                if name == "q":
                    norm_root(act, s.q, bank[SETA][0], 3 * P)
            norm_root(act, s.kv, bank[SETA][0], 2 * P)
            act.wait_ge(wide_ready, s.kv.n + 1)
            act.activation(rstd[:], bank[SETA][2][:], ACT.Copy).then_inc(rstd_ready, 1)
            act.wait_ge(*lp("fold"))
            for k in each:
                act.activation(mla_k[half(1), k, :], bank[SETA][3][half(1), :], ACT.Copy).then_inc(*la.tell("k", k))

        def latent_vector(dve, s):
            sa, sb_ = bank[SETA], bank[SETB]
            sets = (sb_, sa)

            def low(name, nm, src, hi, lo, tiles):
                for k in range(tiles):
                    dve.wait_ge(*la(f"c{name}_hi", k))
                    dve.scalar_tensor_tensor(out=lo[:, k, :], in0=src[:, k, :], scalar=vcol(f"{name}_norm2", k), in1=hi[:, k, :].bitcast(F32),
                                             op0=ALU.mult, op1=ALU.subtract).then_inc(*lv.tell(f"c{name}_lo", k))
                    add_square(dve, nm, k)

            low("q", s.q, c_q, cq_hi, cq_lo, 3)
            norm_diag(dve, s.q)
            low("kv", s.kv, c_kv, ckv_hi, ckv_lo, 2)
            norm_diag(dve, s.kv)
            dve.wait_ge(wide_ready, s.q.n + 1)
            dve.wait_ge(*pv("one"))
            dve.tensor_tensor(turns_q[:], turns[:], sa[1][:], ALU.mult).then_inc(*lv.tell("turns_q"))
            dve.tensor_tensor(k_rot[:], k_rot[:], turns[:], ALU.mult).then_inc(*lv.tell("rot"))
            dve.wait_ge(*lv("turns_q"))
            for k in each:
                dve.wait_ge(w_used, s.n_uq + 3 * (k // 4 + 1))
                dve.tensor_tensor(mla_q[:, k, :], sets[k // 4][k % 4][:], turns_q[:], ALU.mult).then_inc(*lv.tell("q", k))
            dve.wait_ge(rstd_ready, s.rs + 1)
            for k in each:
                dve.wait_ge(w_used, s.n_uk + 2 * (k // 4 + 1))
                dve.tensor_tensor(mla_k[half(0), k, :], sets[k // 4][k % 4][half(0), :], rstd[half(0), :], ALU.mult).then_inc(*lv.tell("k", k))
            dve.wait_ge(w_used, s.n_uv + 2)
            dve.wait_ge(diag_ready, (1 + TT) * (s.kv.n + 1))
            for t in range(TT):
                dve.tensor_scalar(mla_v[:, t, :], sb_[t][:], rinv[:, t:t + 1], None, ALU.mult).then_inc(*lv.tell("v", t))

        LATENT_SCALE = float(1 / np.sqrt(np.float32(96)))

        def mla_tensor(pe, s):
            sa, sb_ = bank[SETA], bank[SETB]
            banks = (sa, sb_)
            pe.wait_ge(*lv("v", TT - 1))
            with pe.Fori(0, 4) as i:
                def at(j, n, t0, t1):
                    a = LATENT_AT[n] + t0 * P
                    return banks[j][a // T][:, a % T:a % T + (t1 - t0) * P]

                pe.wait_ge(*mv("k", i=i))
                for j in two:
                    for n in range(TT):
                        done = pe.matmul(at(j, n, 0, n + 1), qm_pair[:, j, n * P:(n + 1) * P], km_pair[:, j, 0:(n + 1) * P], start=True, stop=True)
                    done.then_inc(*mp.tell("score", j))
                for j in two:
                    pe.wait_ge(*ma("exp", j, TT - 1, i=i))
                    for n in range(TT):
                        for t in range(n + 1):
                            a = LATENT_AT[n] + t * P
                            done = pe.matmul(at(j, n, t, t + 1), score_b[:, j, a:a + P], ident[:], start=True, stop=True)
                    done.then_inc(*mp.tell("turn", j))
                for j in two:
                    pe.wait_ge(*ma("turn", j, i=i))
                    pe.wait_ge(*mv("turn", j, 1, i=i))
                    for n in range(TT):
                        for t in range(n + 1):
                            a = LATENT_AT[n] + t * P
                            done = pe.matmul(sa[3][:, n * P + j * 64:n * P + (j + 1) * 64], prob_b[:, j, a:a + P], vm_pair[:, t, half(j)],
                                             start=t == 0, stop=t == n)
                done.then_inc(*mp.tell("value"))
                pe.wait_ge(*mv("o", 1, i=i))
                for n in range(TT):
                    done = pe.matmul(sb_[3][:, n * P:(n + 1) * P], ob_tok[:, n, :], ident[:], start=True, stop=True)
                done.then_inc(*mp.tell("turn_o"))
                pe.wait_ge(*mv("turn_o", i=i))

        def mla_scalar(act, s):
            banks = (bank[SETA], bank[SETB])
            with act.Fori(0, 4) as i:
                for j in two:
                    act.wait_ge(*mv("neg", j, i=i))
                    for n in range(TT):
                        v = score_b[:, j, LATENT_AT[n]:LATENT_AT[n] + (n + 1) * P]
                        act.activation(v, v, ACT.Exp, bias=neg_b[:, j, n:n + 1], accum_out=total_b[:, j, n:n + 1]).then_inc(*ma.tell("exp", j, n))
                for j in two:
                    act.wait_ge(*mp("turn", j, i=i))
                    act.activation(prob_b[:, j, 0:T], banks[j][0][:], ACT.Copy).then_inc(*ma.tell("turn", j))

        def mla_vector(dve, s):
            banks = (bank[SETA], bank[SETB])
            dve.wait_ge(mask_loaded, 16)
            dve.wait_ge(*lv("v", TT - 1))
            dve.wait_ge(*la("k", KT - 1))
            dve.wait_ge(w_used, s.n_a)
            with dve.Fori(0, 4) as i:
                dve.tensor_copy(qm_pair[:], mla_q[:, bass.ds(i * 2, 2), :]).then_inc(*mv.tell("q"))
                dve.tensor_copy(km_pair[:], mla_k[:, bass.ds(i * 2, 2), :]).then_inc(*mv.tell("k"))
                dve.tensor_copy(vm_pair[:], mla_v[:, :, bass.ds(i * P, P)]).then_inc(*mv.tell("v"))
                for j in two:
                    dve.wait_ge(*mp("score", j, i=i))
                    for b, (a0, a1) in enumerate(BANKS):
                        dve.scalar_tensor_tensor(out=score_b[:, j, a0:a1], in0=banks[j][b][:, 0:a1 - a0], scalar=LATENT_SCALE, in1=mask_b[:, a0:a1],
                                                 op0=ALU.mult, op1=ALU.add).then_inc(*mv.tell("mask", j, b))
                    dve.wait_ge(*mv("mask", j, 2, i=i))
                    for n in range(TT):
                        dve.tensor_reduce(top_b[:, j, n:n + 1], score_b[:, j, LATENT_AT[n]:LATENT_AT[n] + (n + 1) * P],
                                          mybir.AxisListType.X, ALU.max).then_inc(*mv.tell("top", j, n))
                    dve.wait_ge(*mv("top", j, TT - 1, i=i))
                    dve.tensor_scalar(neg_b[:, j, :], top_b[:, j, :], -1.0, None, ALU.mult).then_inc(*mv.tell("neg", j))
                for j in two:
                    dve.wait_ge(*ma("exp", j, TT - 1, i=i))
                    dve.reciprocal(inv_b[:, j, :], total_b[:, j, :]).then_inc(*mv.tell("inv", j))
                for j in two:
                    dve.wait_ge(*mp("turn", j, i=i))
                    for b, (a0, a1) in enumerate(BANKS[1:]):
                        dve.tensor_copy(prob_b[:, j, a0:a1], banks[j][1 + b][:, 0:a1 - a0]).then_inc(*mv.tell("turn", j, b))
                dve.wait_ge(*mp("value", i=i))
                for j in two:
                    dve.tensor_tensor(ob_tok[:, :, half(j)], banks[0][3][:].rearrange("p (n c) -> p n c", n=TT)[:, :, half(j)],
                                      inv_b[:, j, :].rearrange("p (n o) -> p n o", o=1).to_broadcast([P, TT, 64]), ALU.mult).then_inc(*mv.tell("o", j))
                dve.wait_ge(*mp("turn_o", i=i))
                v = mla_z[:, bass.ds(i, 1), :].rearrange("p a t -> p (a t)")
                dve.tensor_tensor(v, banks[1][3][:], v, ALU.mult).then_inc(*mv.tell("turn_o"))

        def branch_tensor(pe, s):
            sa, sb_ = bank[SETA], bank[SETB]
            for branch, n0 in enumerate((s.n_a, s.n_b)):
                for b, set_ in enumerate((sa, sb_)):
                    if branch:
                        pe.wait_ge(*bv_("a", 4 * b + 3))
                    for k in range(4):
                        z = 4 * branch + k
                        pe.wait_ge(x_lo_ready, s.x0 + KT + z + 1)
                        unit_products(pe, [o[:] for o in set_], x_hi[:, z, :], x_lo[:, z, :], k == 0, k == 3, n0 + 4 * b + k)
            for b, set_ in enumerate((sa, sb_)):
                pe.wait_ge(*bv_("sum", 4 * b + 3))
                for k in each:
                    if b == 0:
                        pe.wait_ge(x_lo_ready, s.x0 + 2 * KT + k + 1)
                    unit_products(pe, [o[:] for o in set_], x_hi[:, k, :], x_lo[:, k, :], k == 0, k == KT - 1, s.n_out + b * KT + k)
            pe.wait_ge(*bv_("h", 3))
            norm_sums(pe, s.final, sa[0])
            norm_wide(pe, s.final, sa[1])

        def branch_scalar(act, s):
            act.wait_ge(*mv("turn_o", i=3))
            for k in each:
                act.activation(x_hi[:, k, :], (sb_z, mla_z)[k // 4][:, k % 4, :], ACT.Copy).then_inc(x_hi_ready, 1)
            act.wait_ge(w_used, s.n_out)
            for k in each:
                act.wait_ge(*bv_("sum", k))
                act.activation(x_hi[:, k, :], gate_a[:, k, :], ACT.Copy).then_inc(x_hi_ready, 1)
            for k in each:
                act.wait_ge(*bv_("h", k))
                square(act, s.final, k, h[:, k, :])
            norm_root(act, s.final, bank[SETA][0], D)

        def branch_vector(dve, s):
            sets = (bank[SETA], bank[SETB])
            for k in each:
                dve.wait_ge(x_hi_ready, s.x0 + KT + k + 1)
                dve.tensor_tensor(x_lo[:, k, :], (sb_z, mla_z)[k // 4][:, k % 4, :], x_hi[:, k, :].bitcast(F32), ALU.subtract).then_inc(x_lo_ready, 1)
            for k in each:
                dve.wait_ge(w_used, s.n_a + 4 * (k // 4 + 1))
                dve.tensor_tensor(gate_a[:, k, :], sets[k // 4][k % 4][:], gate_a[:, k, :], ALU.mult).then_inc(*bv_.tell("a", k))
            for k in each:
                dve.wait_ge(w_used, s.n_b + 4 * (k // 4 + 1))
                dve.tensor_tensor(gate_b[:, k, :], sets[k // 4][k % 4][:], gate_b[:, k, :], ALU.mult).then_inc(*bv_.tell("b", k))
                dve.wait_ge(*bv_("b", k))
                dve.tensor_tensor(gate_a[:, k, :], gate_a[:, k, :], gate_b[:, k, :], ALU.add).then_inc(*bv_.tell("sum", k))
            for k in each:
                dve.wait_ge(x_hi_ready, s.x0 + 2 * KT + k + 1)
                dve.tensor_tensor(x_lo[:, k, :], gate_a[:, k, :], x_hi[:, k, :].bitcast(F32), ALU.subtract).then_inc(x_lo_ready, 1)
            for k in each:
                dve.wait_ge(w_used, s.n_out + KT * (k // 4 + 1))
                dve.scalar_tensor_tensor(out=h[:, k, :], in0=sets[k // 4][k % 4][:], scalar=mod[:, 2 * KT + k:2 * KT + k + 1], in1=h[:, k, :],
                                         op0=ALU.mult, op1=ALU.add).then_inc(*bv_.tell("h", k))
            for k in each:
                add_square(dve, s.final, k)
            norm_diag(dve, s.final)
            dve.wait_ge(wide_ready, s.final.n + 1)
            for k in each:
                dve.scalar_tensor_tensor(out=f[:, k, :], in0=h[:, k, :], scalar=vcol("final", k), in1=bank[SETA][1][:],
                                         op0=ALU.mult, op1=ALU.mult).then_inc(*bv_.tell("out", k))

        f0 = Ffn(0, 0, 0, 0, 0, 0)
        mix = Rwkv(f0.end, KT, 1)
        f1 = Ffn(1, 0, 1, mix.end, 8 * KT, 2)
        f2 = Ffn(2, 1, 0, f1.end + KT, 10 * KT, 3, kv=f1.end)
        swa = Swa(f2.end, 11 * KT, 4)
        f3 = Ffn(3, 1, 1, swa.end, 13 * KT, 5)
        second = Second(f3.end, 14 * KT, 6)
        assert second.end == n_units

        block = ctx.enter_context(nc.Block())

        @block.sync
        def _(sp):
            sp.dma_start(vec[:], vectors).then_inc(in_loaded, 16)
            sp.dma_start(h[:], xT).then_inc(in_loaded, 16)
            for t, source in ((masks, masks_in), (gather, gather_in), (spread, spread_in), (rows, rows_in), (rope_c, rope_in)):
                sp.dma_start(t[:], source).then_inc(in_loaded, 16)
            for n in range(RS):
                load_unit(sp, n)
            with sp.Fori(1, n_units // RS) as i:
                for j in range(RS):
                    sp.wait_ge(w_lo_ready, i * RS + (j - RS + 1))
                    load_unit(sp, j, i)
            for n in range(n_units // RS * RS, n_units):
                sp.wait_ge(w_lo_ready, n - RS + 1)
                load_unit(sp, n)
            for k in range(KT):
                sp.wait_ge(*bv_("out", k))
                sp.dma_start(out[:, k, :], f[:, k, :]).then_inc(stored, 16)
            sp.wait_ge(stored, 16 * KT)

        @block.gpsimd
        def _(pool):
            pool.memset(ones[:], 1.0).then_inc(const_ready, 1)
            pool.memset(eps[:], EPS).then_inc(const_ready, 1)
            pool.memset(ident[:], 0.0).then_inc(const_ready, 1)
            pool.wait_ge(const_ready, 3)
            pool.affine_select(out=ident[:], in_=ident[:], compare_op=ALU.not_equal, fill=1.0, base=0,
                               pattern=[[-1, P]], channel_multiplier=1).then_inc(const_ready, 1)

            for n in range(RW):
                split_unit(pool, n)
            with pool.Fori(0, n_units // RW - 1) as i:
                for j in range(RW):
                    split_unit(pool, RW + j, i)
            for n in range(n_units // RW * RW, n_units + 1):
                split_unit(pool, n)

        @block.scalar
        def _(act):
            act.wait_ge(in_loaded, 16 * 7)
            act.wait_ge(const_ready, 4)
            input_parts_scalar(act, f0, 0)
            ffn_scalar(act, f0)
            rwkv_scalar(act, mix)
            pairs_scalar(act)
            group_scalar(act, mix)
            input_parts_scalar(act, f1, 2)
            ffn_scalar(act, f1)
            input_parts_scalar(act, f2, 3)
            ffn_scalar(act, f2)
            input_parts_scalar(act, swa, 4)
            swa_scalar(act, swa)
            input_parts_scalar(act, f3, 5)
            ffn_scalar(act, f3)
            second_scalar(act, second)
            stick_scalar(act, second)
            latent_scalar(act, second)
            mla_scalar(act, second)
            branch_scalar(act, second)

        @block.vector
        def _(dve):
            dve.wait_ge(in_loaded, 16 * 7)
            dve.wait_ge(const_ready, 4)
            input_parts_vector(dve, f0, None)
            ffn_vector(dve, f0)
            for k in range(KT):
                update_h(dve, f0, k)
                add_square(dve, mix.pre, k)
            rwkv_vector(dve, mix)
            pairs_vector(dve)
            group_vector(dve, mix)
            input_parts_vector(dve, f1, mix)
            ffn_vector(dve, f1)
            input_parts_vector(dve, f2, f1)
            ffn_vector(dve, f2)
            input_parts_vector(dve, swa, f2)
            swa_vector(dve, swa)
            input_parts_vector(dve, f3, swa)
            ffn_vector(dve, f3)
            for k in range(KT):
                update_h(dve, f3, k)
                add_square(dve, second.pre, k)
            second_vector(dve, second)
            stick_vector(dve, second)
            latent_vector(dve, second)
            mla_vector(dve, second)
            branch_vector(dve, second)

        @block.tensor
        def _(pe):
            pe.wait_ge(const_ready, 4)
            pe.wait_ge(in_loaded, 16 * 7)
            ffn_tensor(pe, f0)
            rwkv_tensor(pe, mix)
            pairs_tensor(pe)
            group_tensor(pe, mix)
            ffn_tensor(pe, f1)
            ffn_tensor(pe, f2)
            swa_tensor(pe, swa)
            ffn_tensor(pe, f3)
            second_tensor(pe, second)
            stick_tensor(pe, second)
            latent_tensor(pe, second)
            mla_tensor(pe, second)
            branch_tensor(pe, second)


Q_ORDER = [8 * (t // 4) + t % 4 + 4 * j for t in range(KT) for j in range(2)]


def window_table():
    q, k = np.arange(P)[:, None], np.arange(2 * P)[None, :]
    first, other = k <= q, (k > q) & (k <= q + P)
    return np.stack([np.where(m, 0, MASKED) for m in (first, other, other, other)], 1).astype(np.float32)


def second_units(i):
    sizes = (512, 512, 512, 512, 384, 256, 32, 512, D, D)
    q, k, v, z, cq, ckv, rot, mz, ga, gb = np.split(i["w_in_2"][0], np.cumsum(sizes)[:-1], 1)
    none = lambda w, n: np.zeros(w.shape[:-1] + (n,), np.float32)
    swap = lambda w: np.concatenate([w[..., 16:], w[..., :16]], -1)
    w_in = [q, k, v, z, cq, none(cq, 64), rot, swap(rot), ckv, none(ckv, 256), mz, ga, gb]
    uq = i["w_uq_2"][0].reshape(384, HEADS_B, 96)
    uq = np.concatenate([uq, swap(uq[..., 64:])], 2).reshape(384, D)
    ukv = i["w_ukv_2"][0].reshape(256, HEADS_B, 128)
    uk = np.concatenate([ukv[..., :64], none(ukv, 64)], 2).reshape(256, D)
    return [in_units(np.concatenate(w_in, 1)), in_units(uq), in_units(uk), in_units(ukv[..., 64:].reshape(256, 512)),
            in_units(i["w_branch_a_2"][0]), in_units(i["w_branch_b_2"][0]), in_units(i["w_out_2"][0])]


def second_tables():
    p, n = np.arange(P)[:, None], np.arange(P)[None, :]
    rope = np.zeros((P, 4), np.float32)
    rows = np.arange(64, P)
    rope[rows, 0] = np.float32(10000.0) ** (-(rows % 16 * 2).astype(np.float32) / np.float32(32))
    rope[:, 1] = np.where(np.arange(P) < 96, 0.25, 0)
    rope[:, 2] = np.where(np.arange(P) < 96, np.pi / 2, 0)
    rope[:, 3] = np.where((np.arange(P) >= 96) & (np.arange(P) < 112), -1, 1)
    fold = ((p >= 64) & (n >= 64) & (p % 32 == n % 32)).astype(np.float32)
    tri = (p >= n).astype(np.float32)
    stick, latent = np.where(p < n, 0, MASKED), np.where(n <= p, 0, MASKED)
    mask_a, mask_b = np.zeros((2, P, TRI), np.float32)
    for t, a in enumerate((0, 512, 1024, 896)):
        mask_a[:, a:a + P] = stick
    for t, a in enumerate((896, 1024, 512, 0)):
        mask_b[:, a + t * P:a + (t + 1) * P] = latent
    return dict(rope_in=rope, fold_in=fold, tri_in=tri, mask_a_in=mask_a, mask_b_in=mask_b)


def host(i):
    parts = ffn_units(i["ffn_w_in"][0, 0], i["ffn_w_out"][0, 0])
    parts += rwkv_units(*(i["rwkv_" + n][0] for n in "w1 a1 g1 w_rkv w2 a2 g2 w_o".split()))
    parts += ffn_units(i["ffn_w_in"][0, 1], i["ffn_w_out"][0, 1])
    parts += [in_units(i["w_kv"])]
    parts += ffn_units(i["ffn_w_in"][1, 0], i["ffn_w_out"][1, 0])
    parts += [in_units(i["attn_w_q"][0].reshape(D, 16, 64)[:, Q_ORDER].reshape(D, D)),
              in_units(i["attn_w_o"][0].reshape(16, 64, D)[Q_ORDER].reshape(D, D))]
    parts += ffn_units(i["ffn_w_in"][1, 1], i["ffn_w_out"][1, 1])
    parts += second_units(i)
    units = np.concatenate(parts)
    vec = [i["norm_g"], i["rwkv_mu"]] + [i["rwkv_" + n] for n in "w0 a0 k_k k_a r_k gn_g gn_b".split()]
    vec += [i["kv_norm_g"], i["b_kv"][:KV], i["attn_b_q"][0].reshape(16, 64)[Q_ORDER], i["attn_b_o"]]
    vec += [i[n + "_2"] for n in "norm_gain b_ada q_norm_gain kv_norm_gain final_norm_gain c".split()]
    vec = np.concatenate([v.reshape(-1, P) for v in vec]).T
    rows = np.concatenate([i["b_kv"][KV:], i["attn_sinks"][0][Q_ORDER]])
    x = i["x"][0].T.reshape(KT, P, T).transpose(1, 0, 2)
    gather, spread = heads_tables()
    c = np.ascontiguousarray
    return dict(xT=c(x), weights=c(units), vectors=c(vec), masks_in=masks_table(), gather_in=c(gather), spread_in=c(spread),
                rows_in=np.tile(rows, (P, 1)), window_in=window_table(), ada_in=c(i["w_ada_2"][0].reshape(KT, P, 3 * D)),
                pos_in=np.tile(i["positions_2"], (P, 1)), **second_tables())


def kernel(**inputs):
    import concourse.bacc as _bacc
    from concourse.bass_utils import run_bass_kernel_spmd as _run

    arrays = host({name: np.asarray(a) for name, a in inputs.items()})
    nc = _bacc.Bacc("TRN2", target_bir_lowering=False, num_devices=1)
    args = {name: nc.dram_tensor(name, a.shape, mybir.dt.from_np(a.dtype), kind="ExternalInput").ap() for name, a in arrays.items()}
    out = nc.dram_tensor("out", (P, KT, T), F32, kind="ExternalOutput").ap()
    program(nc, out=out, **args)
    r = _run(nc, [arrays], core_ids=[0])
    got = np.asarray(r.results[0]["out"])
    return np.ascontiguousarray(got.transpose(1, 0, 2).reshape(D, T).T)[None]
```

```python
from contextlib import ExitStack

import numpy as np
import concourse.bass as bass
from concourse import mybir

ALU = mybir.AluOpType
ACT = mybir.ActivationFunctionType
F32 = mybir.dt.float32
F32R = mybir.dt.float32r

P = 128
T = 512
D = 1024
KT = D // P
FF = 2816
FT = FF // P
UC = 512
RS = 4
RW = 4
TT = T // P
EPS = 1e-6
CH = 64
CHUNKS = T // CH
HEADS = D // 64
KV = 256
MASKED = -1e30
HEADS_B = 8
TRI = P * (1 + 2 + 3 + 4)
ROUND = 1.5 * 2.0 ** 23
TURN = (6.28125, 0.0019350051879882812, 3.019916050955909e-07)
PI = 3.1415925
KAPPA = float(np.exp(-0.5))
FB = FF * 2 // UC
SETB, SETA = 1, 0


def in_units(w):
    k, m = w.shape
    return w.reshape(k // P, P, m // UC, UC).transpose(2, 0, 1, 3).reshape(-1, P, UC)


def ffn_units(w_in, w_out):
    half = UC // 2
    gate, up = w_in[:, :FF].reshape(D, FB, half), w_in[:, FF:].reshape(D, FB, half)
    first = np.concatenate([gate, up], 2).reshape(D, FB * UC)
    return [in_units(first), in_units(w_out)]


FFN_UNITS = FB * KT + FT * (D // UC)


class Columns:

    def __init__(self):
        self.at, self.parts, self.n = {}, [], 0

    def add(self, name, tiles):
        self.at[name] = self.n
        self.n += tiles


def vector_table():
    c = Columns()
    for layer in range(2):
        for i in range(6):
            c.add(f"norm{layer}{i}", KT)
    for i in range(6):
        c.add(f"mu{i}", KT)
    for name in ("w0", "a0", "k_k", "k_a", "r_k", "gn_g", "gn_b"):
        c.add(name, KT)
    c.add("kv_norm", KT)
    c.add("b_k", 2)
    for name in ("b_q", "b_o"):
        c.add(name, KT)
    c.add("gain2", KT)
    c.add("b_ada", 3 * KT)
    c.add("q_norm2", 3)
    c.add("kv_norm2", 2)
    c.add("final", KT)
    c.add("c", KT)
    return c


VEC = vector_table()


def rwkv_units(w1, a1, g1, w_rkv, w2, a2, g2, w_o):
    inner = np.zeros((D, UC), np.float32)
    inner[:, 0:64], inner[:, 192:256], inner[:, 256:384] = w1, a1, g1
    outer = np.zeros((2, P, D), np.float32)
    outer[0, 0:64], outer[1, 64:P] = w2, a2
    return [in_units(inner), in_units(w_rkv[1]), in_units(w_rkv[0]), in_units(outer[0]), in_units(outer[1]),
            in_units(w_rkv[2]), in_units(g2), in_units(w_o)]


def masks_table():
    s, t = np.arange(CH)[:, None], np.arange(CH)[None, :]
    rows = [(t // b % 2 == 1) & (s // b == t // b - 1) for b in (1, 2, 4, 8, 16, 32)]
    rows += [rows[0].T, s < t, s <= t, s == t]
    return np.tile(np.stack(rows, 1).astype(np.float32), (2, 1, 1))


def heads_tables():
    head = np.arange(D) // 64
    spread = (head[None, :] == np.arange(HEADS)[:, None]).astype(np.float32).reshape(HEADS, KT, P)
    return spread.transpose(2, 1, 0), spread


def program(nc, xT, weights, vectors, masks_in, gather_in, spread_in, rows_in, window_in, ada_in, pos_in, rope_in, fold_in,
            tri_in, mask_a_in, mask_b_in, out):
    n_units = weights.shape[0]
    with ExitStack() as ctx:
        place = [-(-nc.sbuf_base // 64) * 64]

        def sb(name, shape, dt=F32, at=None):
            size = int(np.prod(shape[1:])) * 4
            size = -(-size // 64) * 64
            offset = place[0] if at is None else at
            if at is None:
                place[0] += size
            assert offset + size <= nc.sbuf_usable_end, (name, offset + size)
            t = nc.alloc_sbuf_tensor_at(name, shape, dt, offset=offset)
            where[name] = offset
            return t

        where = {}

        def sem(name):
            return ctx.enter_context(nc.semaphore(name))

        bank = [[ctx.enter_context(nc.psum_tensor(f"bank{s}{m}", [P, T], F32)) for m in range(4)] for s in range(2)]
        h = sb("h", [P, KT, T])
        w_raw = sb("w_raw", [P, RS, UC])
        w_hi = sb("w_hi", [P, RW, UC], F32R)
        w_lo = sb("w_lo", [P, RW, UC], F32R)
        vec = sb("vec", [P, VEC.n])
        ident = sb("ident", [P, P])
        ones = sb("ones", [P, P])
        eps = sb("eps", [P, 1])
        sq = sb("sq", [P, 2, T])
        acc = sb("acc", [P, T])
        root = sb("root", [P, TT])
        rinv = sb("rinv", [P, TT])
        diag = sb("diag", [P, TT, P])
        rstd = sb("rstd", [P, T])
        x_hi = sb("x_hi", [P, KT, T], F32R)
        x_lo = sb("x_lo", [P, KT, T], F32R)
        f = sb("f", [P, KT, T])
        mid_hi = sb("mid_hi", [P, FT, T], F32R)
        mid_lo = sb("mid_lo", [P, FT, T], F32R)
        masks = sb("masks", [P, 10, CH])
        rows = sb("rows", [P, KV + 16])
        spread = sb("spread", [HEADS, KT, P])
        gather = sb("gather", [P, KT, HEADS])
        rope_c = sb("rope_c", [P, 4])
        mod = sb("mod", [P, 3 * KT])
        gain_s = sb("gain_s", [P, KT])
        g_buf = f[:, 0:2, :]
        u_buf = f[:, 2:4, :]

        w_loaded = [sem(f"w_loaded{s}") for s in range(RS)]
        w_hi_ready = sem("w_hi_ready")
        w_lo_ready = sem("w_lo_ready")
        w_used = sem("w_used")
        const_ready = sem("const_ready")
        in_loaded = sem("in_loaded")
        stored = sem("stored")

        def count(n, i=None, per=0):
            return n if i is None else i * per + n

        def load_unit(sp, n, i=None):
            slot = n % RS
            sp.dma_start(w_raw[:, slot, :], weights[n] if i is None else
                         weights[bass.ds(i * RS + n, 1)].rearrange("a p c -> (a p) c")).then_inc(w_loaded[slot], 16)

        def split_unit(pool, n, i=None):
            if n < n_units:
                pool.wait_ge(w_loaded[n % RS], count(16 * (n // RS + 1), i, 16 * RW // RS))
                if n >= RW:
                    pool.wait_ge(w_used, count(n - RW + 1, i, RW))
            if n:
                pool.wait_ge(w_hi_ready, count(n, i, RW))
                pool.tensor_tensor(w_lo[:, (n - 1) % RW, :], w_raw[:, (n - 1) % RS, :],
                                   w_hi[:, (n - 1) % RW, :].bitcast(F32), ALU.subtract).then_inc(w_lo_ready, 1)
            if n < n_units:
                pool.tensor_scalar(w_hi[:, n % RW, :], w_raw[:, n % RS, :], 1.0, 0.0, ALU.mult, ALU.add).then_inc(w_hi_ready, 1)

        def unit_products(pe, outs, hi, lo, first, last, n, i=None, per=0):
            pe.wait_ge(w_lo_ready, count(n + 1, i, per))
            s = n % RW
            for m, o in enumerate(outs):
                c = slice(m * P, (m + 1) * P)
                pe.matmul(o, w_hi[:, s, c], hi, start=first, stop=False)
                pe.matmul(o, w_hi[:, s, c], lo, start=False, stop=False)
                done = pe.matmul(o, w_lo[:, s, c], hi, start=False, stop=last)
            done.then_inc(w_used, 1)

        def vcol(name, k):
            return vec[:, VEC.at[name] + k:VEC.at[name] + k + 1]

        class Steps:

            def __init__(self, name, labels):
                self.sem, self.at, self.told = sem(name), {l if isinstance(l, tuple) else (l,): j + 1 for j, l in enumerate(labels)}, 0
                assert len(self.at) == len(labels), name

            def __call__(self, *label, i=None, k=0, m=1):
                return self.sem, count(self.at[label] + k * len(self.at), i, m * len(self.at))

            def tell(self, *label):
                self.told = self.told % len(self.at) + 1
                assert self.at[label] == self.told, (label, self.told)
                return self.sem, 1

        sq_ready = sem("sq_ready")
        sq_used = sem("sq_used")
        sums_ready = sem("sums_ready")
        root_ready = sem("root_ready")
        diag_ready = sem("diag_ready")
        wide_ready = sem("wide_ready")
        norms = []

        class Norm:

            def __init__(self, tiles):
                self.n = len(norms)
                self.sq0 = sum(m.tiles for m in norms)
                self.tiles = tiles
                norms.append(self)

        def square(act, nm, j, src, **bias):
            j += nm.sq0
            if j >= 2:
                act.wait_ge(sq_used, j - 1)
            act.activation(sq[:, j % 2, :], src, ACT.Square, **bias).then_inc(sq_ready, 1)

        def add_square(dve, nm, j):
            first, j = j == 0, j + nm.sq0
            dve.wait_ge(sq_ready, j + 1)
            if first:
                if nm.n:
                    dve.wait_ge(sums_ready, nm.n)
                dve.tensor_copy(acc[:], sq[:, j % 2, :]).then_inc(sq_used, 1)
            else:
                dve.wait_ge(sq_used, j)
                dve.tensor_tensor(acc[:], acc[:], sq[:, j % 2, :], ALU.add).then_inc(sq_used, 1)

        def norm_sums(pe, nm, out):
            pe.wait_ge(sq_used, nm.sq0 + nm.tiles)
            for t in range(TT):
                done = pe.matmul(out[:, t:t + 1], acc[:, t * P:(t + 1) * P], ones[:, 0:1], start=True, stop=True)
            done.then_inc(sums_ready, 1)

        def norm_root(act, nm, sums, width):
            act.wait_ge(sums_ready, nm.n + 1)
            act.activation(root[:], sums[:, 0:TT], ACT.Sqrt, bias=eps[:, 0:1], scale=1.0 / width).then_inc(root_ready, 1)

        def norm_diag(dve, nm):
            d0 = (1 + TT) * nm.n
            dve.wait_ge(root_ready, nm.n + 1)
            dve.reciprocal(rinv[:], root[:]).then_inc(diag_ready, 1)
            dve.wait_ge(diag_ready, d0 + 1)
            for t in range(TT):
                dve.tensor_scalar(diag[:, t, :], ident[:], rinv[:, t:t + 1], None, ALU.mult).then_inc(diag_ready, 1)

        def norm_wide(pe, nm, out):
            pe.wait_ge(diag_ready, (1 + TT) * (nm.n + 1))
            pe.matmul(out[:], ones[:], diag[:].rearrange("p t q -> p (t q)"), start=True, stop=True).then_inc(wide_ready, 1)

        f_ready = sem("f_ready")
        tmp_ready = sem("tmp_ready")
        h_ready = sem("h_ready")

        def output_tensor(pe, s):
            pe.wait_ge(f_ready, s.h0 + 4)
            norm_sums(pe, s.post, bank[SETA][0])
            norm_wide(pe, s.post, bank[SETA][1])

        def output_scalar(act, s):
            for half, set_ in enumerate((SETA, SETB)):
                act.wait_ge(w_used, s.u1 + (half + 1) * s.rows)
                for m in range(4):
                    k = 4 * half + m
                    square(act, s.post, k, bank[set_][m][:], **({} if s.bias is None else {"bias": vcol(s.bias, k)}))
            norm_root(act, s.post, bank[SETA][0], D)

        def output_vector(dve, s):
            for half, set_ in enumerate((SETA, SETB)):
                dve.wait_ge(w_used, s.u1 + (half + 1) * s.rows)
                for m in range(4):
                    k = 4 * half + m
                    dve.wait_ge(sq_ready, s.post.sq0 + k + 1)
                    if s.bias is None:
                        dve.tensor_scalar(f[:, k, :], bank[set_][m][:], vcol(s.gain_out, k), s.half,
                                          ALU.mult, ALU.mult).then_inc(f_ready, 1)
                    else:
                        dve.tensor_scalar(f[:, k, :], bank[set_][m][:], vcol(s.bias, k), vcol(s.gain_out, k),
                                          ALU.add, ALU.mult).then_inc(f_ready, 1)
                    add_square(dve, s.post, k)
            norm_diag(dve, s.post)

        x_hi_ready = sem("x_hi_ready")
        x_lo_ready = sem("x_lo_ready")
        rstd_ready = sem("rstd_ready")
        bank_read = sem("bank_read")
        silu_ready = sem("silu_ready")
        prod_ready = sem("prod_ready")
        mid_hi_ready = sem("mid_hi_ready")
        mid_lo_ready = sem("mid_lo_ready")

        rstds = []

        def new_rstd():
            rstds.append(1)
            return len(rstds) - 1

        class Ffn:
            def __init__(self, number, layer, which, first_unit, x_tiles, updates, kv=None):
                self.kv, self.rs = kv, new_rstd()
                self.u0 = first_unit
                self.u1 = first_unit + FB * KT
                self.end = first_unit + FFN_UNITS
                self.rows = FT
                self.gain_in = f"norm{layer}{[0, 4][which]}"
                self.gain_out, self.bias, self.half = f"norm{layer}{[1, 5][which]}", None, 0.5
                self.n, self.x0 = number, x_tiles
                self.h0 = KT * updates
                self.read0, self.mid0 = 4 * FB * number, FT * number
                self.pre, self.post = Norm(KT), Norm(KT)

        def ffn_tensor(pe, s):
            def block(b, set_, n, i=None):
                for k in range(KT):
                    if b == 0:
                        pe.wait_ge(x_lo_ready, s.x0 + k + 1)
                    unit_products(pe, [o[:] for o in bank[set_]], x_hi[:, k, :], x_lo[:, k, :],
                                  k == 0, k == KT - 1, n + k, i, 2 * KT)

            if s.kv is not None:
                kv_tensor(pe, s)
            block(0, SETB, s.u0)
            if s.kv is None:
                norm_sums(pe, s.pre, bank[SETA][0])
                norm_wide(pe, s.pre, bank[SETA][1])
            pe.wait_ge(rstd_ready, s.rs + 1)
            block(1, SETA, s.u0 + KT)
            with pe.Fori(0, (FB - 3) // 2) as i:
                for j, set_ in enumerate((SETB, SETA)):
                    pe.wait_ge(bank_read, count(s.read0 + 4 * (j + 1), i, 8))
                    block(2 + j, set_, s.u0 + (2 + j) * KT, i)
            pe.wait_ge(bank_read, s.read0 + 4 * (FB - 2))
            block(FB - 1, SETB, s.u0 + (FB - 1) * KT)
            for half, set_ in enumerate((SETA, SETB)):
                pe.wait_ge(bank_read, s.read0 + 4 * (FB - 1 + half))
                for k in range(FT):
                    if half == 0:
                        pe.wait_ge(mid_lo_ready, s.mid0 + k + 1)
                    unit_products(pe, [o[:] for o in bank[set_]], mid_hi[:, k, :], mid_lo[:, k, :],
                                  k == 0, k == FT - 1, s.u1 + half * FT + k)
            output_tensor(pe, s)

        def input_parts_scalar(act, s, updates):
            for k in range(KT):
                if updates:
                    act.wait_ge(h_ready, KT * (updates - 1) + k + 1)
                gain = "kv_norm" if s.kv is not None else s.gain_in
                act.activation(x_hi[:, k, :], h[:, k, :], ACT.Copy, scale=vcol(gain, k)).then_inc(x_hi_ready, 1)
                square(act, s.pre, k, h[:, k, :])
            if s.kv is not None:
                for k in range(KT):
                    act.wait_ge(w_used, s.kv + k + 1)
                    act.activation(x_hi[:, k, :], h[:, k, :], ACT.Copy, scale=vcol(s.gain_in, k)).then_inc(x_hi_ready, 1)

        def input_low(dve, s, k, gain, x0):
            dve.wait_ge(x_hi_ready, x0 + k + 1)
            dve.scalar_tensor_tensor(out=x_lo[:, k, :], in0=h[:, k, :], scalar=vcol(gain, k),
                                     in1=x_hi[:, k, :].bitcast(F32), op0=ALU.mult, op1=ALU.subtract).then_inc(x_lo_ready, 1)

        def input_parts_vector(dve, s, last):
            for k in range(KT):
                if last is not None:
                    update_h(dve, last, k)
                if s.kv is None:
                    input_low(dve, s, k, s.gain_in, s.x0)
                else:
                    input_low(dve, s, k, "kv_norm", s.x0 - KT)
                add_square(dve, s.pre, k)
            if s.kv is not None:
                for k in range(KT):
                    input_low(dve, s, k, s.gain_in, s.x0)

        def ffn_scalar(act, s):
            norm_root(act, s.pre, bank[SETA][0], D)
            act.wait_ge(wide_ready, s.pre.n + 1)
            act.activation(rstd[:], bank[SETA][1][:], ACT.Copy).then_inc(rstd_ready, 1)

            def block(b, i=None):
                for p in range(2):
                    act.wait_ge(bank_read, count(s.read0 + 4 * b + p + 1, i, 8))
                    act.activation(g_buf[:, p, :], g_buf[:, p, :], ACT.Silu).then_inc(silu_ready, 1)
                for p in range(2):
                    act.wait_ge(prod_ready, count(s.mid0 + 2 * b + p + 1, i, 4))
                    o = mid_hi[:, 2 * b + p, :] if i is None else \
                        mid_hi[:, bass.ds(i * 4 + (2 * b + p), 1), :].rearrange("p a t -> p (a t)")
                    act.activation(o, u_buf[:, p, :], ACT.Copy).then_inc(mid_hi_ready, 1)

            block(0)
            with act.Fori(0, (FB - 1) // 2) as i:
                for j in range(2):
                    block(1 + j, i)
            output_scalar(act, s)

        def ffn_vector(dve, s):
            norm_diag(dve, s.pre)
            if s.kv is not None:
                kv_vector(dve, s)

            def block(b, set_, i=None):
                dve.wait_ge(w_used, count(s.u0 + (b + 1) * KT, i, 2 * KT))
                dve.wait_ge(rstd_ready, s.rs + 1)
                for p in range(2):
                    dve.tensor_tensor(g_buf[:, p, :], bank[set_][p][:], rstd[:], ALU.mult).then_inc(bank_read, 1)
                for p in range(2):
                    if b:
                        dve.wait_ge(mid_lo_ready, count(s.mid0 + 2 * b + p - 1, i, 4))
                    dve.tensor_tensor(u_buf[:, p, :], bank[set_][2 + p][:], rstd[:], ALU.mult).then_inc(bank_read, 1)
                for p in range(2):
                    dve.wait_ge(silu_ready, count(s.mid0 + 2 * b + p + 1, i, 4))
                    dve.wait_ge(bank_read, count(s.read0 + 4 * b + p + 3, i, 8))
                    dve.tensor_tensor(u_buf[:, p, :], g_buf[:, p, :], u_buf[:, p, :], ALU.mult).then_inc(prod_ready, 1)
                for p in range(2):
                    dve.wait_ge(mid_hi_ready, count(s.mid0 + 2 * b + p + 1, i, 4))
                    tile = slice(2 * b + p, 2 * b + p + 1) if i is None else bass.ds(i * 4 + (2 * b + p), 1)
                    lo, hi = (x[:, tile, :].rearrange("p a t -> p (a t)") for x in (mid_lo, mid_hi))
                    dve.tensor_tensor(lo, u_buf[:, p, :], hi.bitcast(F32), ALU.subtract).then_inc(mid_lo_ready, 1)

            block(0, SETB)
            with dve.Fori(0, (FB - 1) // 2) as i:
                block(1, SETA, i)
                block(2, SETB, i)
            dve.wait_ge(mid_lo_ready, s.mid0 + FT)
            output_vector(dve, s)

        def update_h(dve, s, k):
            if k == 0:
                dve.wait_ge(wide_ready, s.post.n + 1)
                dve.wait_ge(f_ready, s.h0 + KT)
            dve.tensor_tensor(f[:, k, :], f[:, k, :], bank[SETA][1][:], ALU.mult).then_inc(tmp_ready, 1)
            dve.wait_ge(tmp_ready, s.h0 + k + 1)
            dve.tensor_tensor(h[:, k, :], h[:, k, :], f[:, k, :], ALU.add).then_inc(h_ready, 1)

        r_arr = sb("r_arr", [P, KT, T], at=where["mid_hi"])
        k_arr = sb("k_arr", [P, KT, T], at=where["r_arr"] + 4 * KT * T)
        v_arr = sb("v_arr", [P, TT, D], at=where["k_arr"] + 4 * KT * T)
        s_arr = sb("s_arr", [P, KT, T], at=where["v_arr"] + 4 * KT * T)
        u_arr = sb("u_arr", [P, KT, T + 1], at=where["s_arr"] + 4 * KT * T)
        tg_hi = sb("tg_hi", [P, T], F32R, at=where["u_arr"] + 16448)
        tg_lo = sb("tg_lo", [P, T], F32R, at=where["tg_hi"] + 4 * T)
        assert where["tg_lo"] + 4 * T <= where["mid_hi"] + 2 * 4 * FT * T
        a_arr = sb("a_arr", [P, KT, T], at=where["f"])
        wa_hi = sb("wa_hi", [P, T], F32R)
        wa_lo = sb("wa_lo", [P, T], F32R)
        reset = sb("reset", [P, T])
        omu = sb("omu", [P, 6 * KT])
        head_a = sb("head_a", [HEADS, T])
        head_b = sb("head_b", [HEADS, T], at=where["rstd"])
        head_c = sb("head_c", [HEADS, T], at=where["diag"])
        fac = sb("fac", [P, KT, CHUNKS])
        fac_log = sb("fac_log", [P, KT, CHUNKS])
        gn_eps = sb("gn_eps", [P, 1])
        tmp = [sb(f"tmp{j}", [P, T], at=where["u_arr"] + 4 * T * j) for j in range(8)]
        wa_raw, tg_raw = v_arr[:, 0, 0:T], v_arr[:, 1, 0:T]
        at_ = [where["x_hi"]]

        def pair_buffer(name, shape):
            t = sb(name, shape, at=at_[0])
            at_[0] += 4 * int(np.prod(shape[1:]))
            assert at_[0] <= where["x_hi"] + 2 * 4 * KT * T
            return t

        op_a, op_r, a_next, r_next, op_b, op_k = (pair_buffer(n, [P, T]) for n in ("op_a", "op_r", "a_next", "r_next", "op_b", "op_k"))
        op_v, bt_mat, kt_mat = (pair_buffer(n, [P, TT, P]) for n in ("op_v", "bt_mat", "kt_mat"))
        x_mat, xt_mat, xt_c, mak_t, mrb_t, mrk_t = (pair_buffer(n, [P, 8, CH]) for n in ("x_mat", "xt_mat", "xt_c", "mak_t", "mrb_t", "mrk_t"))
        e_mat, mab_t, *z_mat = (sb(n, [P, 8, CH], at=where["u_arr"] + 4 * T * j)
                                for j, n in enumerate(["e_mat", "mab_t"] + [f"z_mat{l}" for l in range(1, 6)]))
        rhs_s = sb("rhs_s", [P, 2, CH], at=where["sq"])
        sa_s = sb("sa_s", [P, 2, CH], at=where["sq"] + 512)
        st_s = sb("st_s", [P, CH], at=where["sq"] + 1024)
        st_f = sb("st_f", [P, CH], at=where["sq"] + 1280)
        fac_b = sb("fac_b", [P, CHUNKS], at=where["sq"] + 1536)

        class Rwkv:
            def __init__(self, first_unit, x_tiles, updates):
                self.x0, self.h0 = x_tiles, KT * updates
                self.n_lora = first_unit
                self.n_k = first_unit + KT
                self.n_r = self.n_k + 2 * KT
                self.n_lora2 = self.n_r + 2 * KT
                self.n_v = self.n_lora2 + 4
                self.n_g = self.n_v + 2 * KT
                self.u1 = self.n_g + 2
                self.rows = KT
                self.end = self.u1 + 2 * KT
                self.pre, self.post = Norm(KT), Norm(KT)
                self.gain_in, self.gain_out, self.bias, self.half = "norm02", "norm03", None, 1.0

        u_ready = sem("u_ready")
        mix_ready = sem("mix_ready")
        mixed = sem("mixed")
        each = range(KT)
        quad = [range(4), range(4, 8)]
        EARLY = 2
        rp = Steps("rwkv_pe", ["sums", ("widen", 0), ("widen", 1)] +
                   [l for k in each for l in [("bonus", k)] + [("widen", k + 2)] * (k + 2 < KT)])
        ra = Steps("rwkv_act", ["w_in", "a_in", "g_in", "wa_hi", "tg_hi"] +
                   [(n, m) for n in ("k", "r", "sg", "a", "sq") for m in each] +
                   ["norm"] + [("v", 0, t) for t in range(TT)] + [(n, k) for k in range(EARLY) for n in ("Ep", "Em", "Ea", "fac")] +
                   [("v", 1, t) for t in range(TT)] + [(n, k) for k in range(EARLY, KT) for n in ("Ep", "Em", "Ea", "fac")] + ["bonus"])
        rv = Steps("rwkv_dve", ["omu", "zero", "reset", "reset0", "gn_eps", "wa_lo", "tg_lo", "max", "rec"] +
                   [(n, k) for k in each for n in "cum cm cp fl kk t k2 rk b R K B A".split()])

        X_ORDER = [(i, k) for k in each for i in (1, 4, 5)] + [(i, k) for i in (2, 0, 3) for k in each]

        def x_free(s, q):
            q -= KT
            if q < 3 * KT:
                return s.n_lora + q // 3 + 1
            return (s.n_k, s.n_r, s.n_v)[(q - 3 * KT) // KT] + KT + q % KT + 1

        def rwkv_tensor(pe, s):
            sa, sb_ = bank[SETA], bank[SETB]
            norm_sums(pe, s.pre, sa[0])
            norm_wide(pe, s.pre, sa[1])
            for k in each:
                n = s.n_lora + k
                pe.wait_ge(w_lo_ready, n + 1)
                for j in range(3):
                    q = 3 * k + j
                    pe.wait_ge(x_lo_ready, s.x0 + q + 1)
                    o, c, z = sb_[j // 2], slice(j * P, (j + 1) * P), q % KT
                    first, last = k == 0 and j != 1, k == KT - 1 and j != 0
                    pe.matmul(o[:], w_hi[:, n % RW, c], x_hi[:, z, :], start=first, stop=False)
                    pe.matmul(o[:], w_hi[:, n % RW, c], x_lo[:, z, :], start=False, stop=False)
                    done = pe.matmul(o[:], w_lo[:, n % RW, c], x_hi[:, z, :], start=False, stop=last)
                done.then_inc(w_used, 1)
            pe.wait_ge(u_ready, KT)
            for j, (n0, free_a, free_b) in enumerate(((s.n_k, None, ra("g_in")), (s.n_r, ra("k", 3), ra("k", 7)))):
                for b, (set_, free) in enumerate(((SETA, free_a), (SETB, free_b))):
                    if free:
                        pe.wait_ge(*free)
                    for k in each:
                        if b == 0:
                            pe.wait_ge(x_lo_ready, s.x0 + (3 + j) * KT + k + 1)
                        unit_products(pe, [o[:] for o in bank[set_]], x_hi[:, k, :], x_lo[:, k, :],
                                      k == 0, k == KT - 1, n0 + b * KT + k)
            pe.wait_ge(*rv("wa_lo"))
            for j, free in enumerate((ra("r", 3), ra("r", 7), ra("sg", 3), ra("sg", 7))):
                pe.wait_ge(*free)
                unit_products(pe, [o[:] for o in bank[(SETA, SETB)[j % 2]]], wa_hi[:], wa_lo[:], True, True, s.n_lora2 + j)

            def v_unit(b, k):
                if b == 0:
                    pe.wait_ge(x_lo_ready, s.x0 + 5 * KT + k + 1)
                if k == 0:
                    pe.wait_ge(*(ra("v", 0, TT - 1) if b else ra("a", 3)))
                n = s.n_v + b * KT + k
                pe.wait_ge(w_lo_ready, n + 1)
                for t in range(TT):
                    c = slice(t * P, (t + 1) * P)
                    pe.matmul(sa[t][:], x_hi[:, k, c], w_hi[:, n % RW, :], start=k == 0, stop=False)
                    pe.matmul(sa[t][:], x_lo[:, k, c], w_hi[:, n % RW, :], start=False, stop=False)
                    done = pe.matmul(sa[t][:], x_hi[:, k, c], w_lo[:, n % RW, :], start=False, stop=k == KT - 1)
                done.then_inc(w_used, 1)

            def widen(k):
                if k == 0:
                    pe.wait_ge(*rv("rec"))
                if k >= 2:
                    pe.wait_ge(*rv("kk", k - 2))
                pe.matmul(sb_[1 + k % 2][:], spread[:, k, :], head_b[:], start=True, stop=True).then_inc(*rp.tell("widen", k))

            for k in range(4):
                v_unit(0, k)
            pe.wait_ge(*ra("a", 7))
            for k in each:
                pe.wait_ge(*ra("sq", k))
                done = pe.matmul(sb_[0][0:HEADS, :], gather[:, k, :], tmp[k][:], start=k == 0, stop=k == KT - 1)
            done.then_inc(*rp.tell("sums"))
            for k in range(4, KT):
                v_unit(0, k)
            widen(0)
            widen(1)
            def bonus(k):
                pe.wait_ge(*rv("rk", k))
                pe.matmul(sb_[3][0:HEADS, :], gather[:, k, :], tmp[1][:], start=k == 0, stop=k == KT - 1).then_inc(*rp.tell("bonus", k))
                if k + 2 < KT:
                    widen(k + 2)

            for k in each:
                v_unit(1, k)
                if k in (4, 6):
                    bonus(k // 2 - 2)
            for k in range(EARLY, KT):
                bonus(k)

        def rwkv_scalar(act, s):
            for k in each:
                act.wait_ge(h_ready, s.h0 - KT + k + 1)
                square(act, s.pre, k, h[:, k, :])
            norm_root(act, s.pre, bank[SETA][0], D)

            def mix(q):
                i, k = X_ORDER[q]
                act.wait_ge(u_ready, k + 1)
                if q >= 2:
                    act.wait_ge(x_lo_ready, s.x0 + q - 1)
                act.activation(sq[:, q % 2, :], u_arr[:, k, 0:T], ACT.Copy, scale=vcol(f"mu{i}", k)).then_inc(mix_ready, 1)

            def tile(q):
                if q + 1 < len(X_ORDER):
                    mix(q + 1)
                act.wait_ge(mixed, q + 1)
                if q >= KT:
                    act.wait_ge(w_used, x_free(s, q))
                act.activation(x_hi[:, q % KT, :], sq[:, q % 2, :], ACT.Copy).then_inc(x_hi_ready, 1)

            mix(0)
            for q in range(3 * KT):
                tile(q)
            act.wait_ge(w_used, s.n_k)
            act.activation(wa_raw[0:64, :], bank[SETB][0][0:64, :], ACT.Tanh).then_inc(*ra.tell("w_in"))
            act.activation(wa_raw[64:P, :], bank[SETB][0][64:P, :], ACT.Copy).then_inc(*ra.tell("a_in"))
            act.activation(tg_raw, bank[SETB][1][:], ACT.Sigmoid).then_inc(*ra.tell("g_in"))
            act.wait_ge(*ra("g_in"))
            act.activation(wa_hi[:], wa_raw, ACT.Copy).then_inc(*ra.tell("wa_hi"))
            act.activation(tg_hi[:], tg_raw, ACT.Copy).then_inc(*ra.tell("tg_hi"))
            for q in range(3 * KT, 4 * KT):
                tile(q)
            for j, (n0, arr, name) in enumerate(((s.n_k, k_arr, "k"), (s.n_r, r_arr, "r"))):
                for b, set_ in enumerate((SETA, SETB)):
                    act.wait_ge(w_used, n0 + (b + 1) * KT)
                    for m in range(4):
                        act.activation(arr[:, 4 * b + m, :], bank[set_][m][:], ACT.Copy).then_inc(*ra.tell(name, 4 * b + m))
                    if b == 0:
                        for k in each:
                            tile((4 + j) * KT + k)
            for j in range(4):
                act.wait_ge(w_used, s.n_lora2 + j + 1)
                arr, name, bias = ((s_arr, "sg", "w0"), (a_arr, "a", "a0"))[j // 2]
                for m in range(4):
                    k = 4 * (j % 2) + m
                    act.activation(arr[:, k, :], bank[(SETA, SETB)[j % 2]][m][:], ACT.Sigmoid, bias=vcol(bias, k)).then_inc(*ra.tell(name, k))
            act.wait_ge(mixed, len(X_ORDER))
            for k in each:
                act.activation(tmp[k][:], k_arr[:, k, :], ACT.Square, scale=vcol("k_k", k)).then_inc(*ra.tell("sq", k))
            def factors(k):
                act.wait_ge(*rv("cp", k))
                if k:
                    act.wait_ge(*rv("A", k - 1))
                act.activation(tmp[5][:], tmp[3][:], ACT.Exp, scale=-KAPPA).then_inc(*ra.tell("Ep", k))
                act.activation(tmp[6][:], tmp[3][:], ACT.Exp, scale=KAPPA).then_inc(*ra.tell("Em", k))
                act.activation(tmp[7][:], tmp[4][:], ACT.Exp, scale=-KAPPA).then_inc(*ra.tell("Ea", k))
                act.wait_ge(*rv("fl", k))
                act.activation(fac[:, k, 0:CHUNKS - 1], fac_log[:, k, 0:CHUNKS - 1], ACT.Exp, scale=-KAPPA).then_inc(*ra.tell("fac", k))

            act.wait_ge(*rp("sums"))
            act.activation(head_a[:], bank[SETB][0][0:HEADS, :], ACT.Sqrt).then_inc(*ra.tell("norm"))
            for b in range(2):
                act.wait_ge(w_used, s.n_v + (b + 1) * KT)
                for t in range(TT):
                    act.activation(v_arr[:, t, b * T:(b + 1) * T], bank[SETA][t][:], ACT.Copy).then_inc(*ra.tell("v", b, t))
                if b == 0:
                    for k in range(EARLY):
                        factors(k)
            for k in range(EARLY, KT):
                factors(k)
            act.wait_ge(*rp("bonus", KT - 1))
            act.activation(head_a[:], bank[SETB][3][0:HEADS, :], ACT.Copy).then_inc(*ra.tell("bonus"))

        def rwkv_vector(dve, s):
            mu0 = VEC.at["mu0"]
            dve.tensor_scalar(omu[:], vec[:, mu0:mu0 + 6 * KT], -1.0, 1.0, ALU.mult, ALU.add).then_inc(*rv.tell("omu"))
            norm_diag(dve, s.pre)
            dve.memset(u_arr[:, :, 0:1], 0.0).then_inc(*rv.tell("zero"))
            dve.memset(reset[:], 1.0).then_inc(*rv.tell("reset"))
            dve.wait_ge(*rv("reset"))
            dve.memset(reset[:].rearrange("p (c t) -> p c t", t=CH)[:, :, 0:1], 0.0).then_inc(*rv.tell("reset0"))
            dve.memset(gn_eps[:], 64e-5).then_inc(*rv.tell("gn_eps"))
            dve.wait_ge(*rv("zero"))
            dve.wait_ge(wide_ready, s.pre.n + 1)
            for k in each:
                dve.scalar_tensor_tensor(out=u_arr[:, k, 1:T + 1], in0=h[:, k, :], scalar=vcol(s.gain_in, k),
                                         in1=bank[SETA][1][:], op0=ALU.mult, op1=ALU.mult).then_inc(u_ready, 1)

            def mixing(q):
                i, k = X_ORDER[q]
                dve.wait_ge(mix_ready, q + 1)
                dve.wait_ge(u_ready, k + 1)
                dve.scalar_tensor_tensor(out=sq[:, q % 2, :], in0=u_arr[:, k, 1:T + 1], scalar=omu[:, i * KT + k:i * KT + k + 1],
                                         in1=sq[:, q % 2, :], op0=ALU.mult, op1=ALU.add).then_inc(mixed, 1)

            def tile(q):
                if q + 1 < len(X_ORDER):
                    mixing(q + 1)
                dve.wait_ge(x_hi_ready, s.x0 + q + 1)
                dve.tensor_tensor(x_lo[:, q % KT, :], sq[:, q % 2, :], x_hi[:, q % KT, :].bitcast(F32),
                                  ALU.subtract).then_inc(x_lo_ready, 1)

            dve.wait_ge(*rv("omu"))
            mixing(0)
            for q in range(3 * KT):
                tile(q)
            dve.wait_ge(*ra("tg_hi"))
            dve.tensor_tensor(wa_lo[:], wa_raw, wa_hi[:].bitcast(F32), ALU.subtract).then_inc(*rv.tell("wa_lo"))
            dve.tensor_tensor(tg_lo[:], tg_raw, tg_hi[:].bitcast(F32), ALU.subtract).then_inc(*rv.tell("tg_lo"))
            for q in range(3 * KT, len(X_ORDER)):
                tile(q)
            dve.wait_ge(*ra("norm"))
            dve.tensor_scalar(head_a[:], head_a[:], 1e-12, None, ALU.max).then_inc(*rv.tell("max"))
            dve.wait_ge(*rv("max"))
            dve.reciprocal(head_b[:], head_a[:]).then_inc(*rv.tell("rec"))
            for k in each:
                chunks = lambda t: t[:].rearrange("p (c t) -> p c t", t=CH)
                mid = chunks(tmp[2])[:, :, CH // 2 - 1:CH // 2]
                if k == 0:
                    dve.wait_ge(*rp("sums"))
                else:
                    dve.wait_ge(*ra("Ea", k - 1))
                    dve.wait_ge(*rv("fl", k - 1))
                dve.tensor_tensor_scan(tmp[2][:], reset[:], s_arr[:, k, :], 0.0, ALU.mult, ALU.add).then_inc(*rv.tell("cum", k))
                dve.wait_ge(*rv("cum", k))
                dve.tensor_tensor(chunks(tmp[3]), chunks(tmp[2]), mid.to_broadcast([P, CHUNKS, CH]), ALU.subtract).then_inc(*rv.tell("cm", k))
                dve.wait_ge(*rv("cm", k))
                dve.tensor_tensor(tmp[4][:], tmp[3][:], s_arr[:, k, :], ALU.subtract).then_inc(*rv.tell("cp", k))
                dve.tensor_tensor(fac_log[:, k, 0:CHUNKS - 1], chunks(tmp[3])[:, 0:CHUNKS - 1, CH - 1],
                                  chunks(tmp[2])[:, 1:CHUNKS, CH // 2 - 1], ALU.add).then_inc(*rv.tell("fl", k))
                dve.wait_ge(*rp("widen", k))
                dve.scalar_tensor_tensor(out=tmp[0][:], in0=k_arr[:, k, :], scalar=vcol("k_k", k), in1=bank[SETB][1 + k % 2][:],
                                         op0=ALU.mult, op1=ALU.mult).then_inc(*rv.tell("kk", k))
                if k:
                    dve.wait_ge(*rp("bonus", k - 1))
                dve.tensor_scalar(tmp[1][:], a_arr[:, k, :], 1.0, vcol("k_a", k), ALU.subtract, ALU.mult).then_inc(*rv.tell("t", k))
                dve.wait_ge(*rv("t", k))
                dve.scalar_tensor_tensor(out=k_arr[:, k, :], in0=tmp[1][:], scalar=1.0, in1=k_arr[:, k, :],
                                         op0=ALU.add, op1=ALU.mult).then_inc(*rv.tell("k2", k))
                dve.wait_ge(*rv("k2", k))
                dve.scalar_tensor_tensor(out=tmp[1][:], in0=r_arr[:, k, :], scalar=vcol("r_k", k), in1=k_arr[:, k, :],
                                         op0=ALU.mult, op1=ALU.mult).then_inc(*rv.tell("rk", k))
                dve.tensor_tensor(a_arr[:, k, :], tmp[0][:], a_arr[:, k, :], ALU.mult).then_inc(*rv.tell("b", k))
                dve.wait_ge(*ra("Ea", k))
                dve.wait_ge(*rv("b", k))
                dve.tensor_tensor(r_arr[:, k, :], r_arr[:, k, :], tmp[5][:], ALU.mult).then_inc(*rv.tell("R", k))
                dve.tensor_tensor(k_arr[:, k, :], k_arr[:, k, :], tmp[6][:], ALU.mult).then_inc(*rv.tell("K", k))
                dve.tensor_tensor(a_arr[:, k, :], a_arr[:, k, :], tmp[6][:], ALU.mult).then_inc(*rv.tell("B", k))
                dve.scalar_tensor_tensor(out=s_arr[:, k, :], in0=tmp[0][:], scalar=-1.0, in1=tmp[7][:],
                                         op0=ALU.mult, op1=ALU.mult).then_inc(*rv.tell("A", k))

        LEVELS = range(1, 6)
        LAST = CHUNKS - 1
        two = range(2)
        ip = Steps("inverse_pe", ["ab"] + [(n, l) for l in LEVELS for n in ("z", "zx")] + ["ak", "rk", "tr"])
        ia = Steps("inverse_act", ["a_next", "r_next", "mab"] + [("z", l) for l in LEVELS] + ["a", "r", "v", "bt"])
        iv = Steps("inverse_dve", ["b", "k", "mab", ("x1", 0), ("x1", 1), "xt1", ("x", 0), ("xt", 0), ("e", 1)] +
                   [s_ for l in LEVELS[:-1] for s_ in [("z", l), ("e", l + 1), ("x", l, 0), ("x", l), ("xt", l, 0), ("xt", l)]] +
                   [("z", 5), "xt_copy", ("xt", 5, 0), ("xt", 5), "fac"] + [(n, j) for n in ("mak", "mrb", "mrk") for j in two] + ["kt"])
        cp = Steps("chain_pe", [(n, c) for c in range(CHUNKS) for n in ["s"] * (c > 0) + ["rhs", "sa"] + ["st"] * (c < LAST) + ["y"]])
        ca = Steps("chain_act", [(n, c) for c in range(CHUNKS) for n in ["fade"] * (0 < c < LAST) + ["rhs", "sa"]])
        cv = Steps("chain_dve", [s_ for c in range(CHUNKS) for s_ in [("rhs", c), ("sa", c)] + [("st", c, 0), ("st", c)] * (c < LAST)] + [("y", 0), "y"])
        cv0 = sem("z_zero")
        POINTS = dict(zip([0] + list(range(4, 24, 2)), range(11)))

        def half(j):
            return slice(j * 64, (j + 1) * 64)

        def rows4(j):
            return slice(4 * j, 4 * j + 4)

        def chunk(c):
            return slice(c * CH, (c + 1) * CH)

        def halves(t, l, h_):
            if len(t.shape) == 3:
                return t.rearrange("p n (g h w) -> p (n g) h w", h=2, w=2 ** l)[:, :, h_, :]
            return t.rearrange("p (g h w) -> p g h w", h=2, w=2 ** l)[:, :, h_, :]

        def packed(t, l):
            return t.rearrange("p (g w) -> p g w", w=2 ** l)

        def pairs_tensor(pe):
            sa, sb_ = bank[SETA], bank[SETB]

            def hold(o):
                pe.matmul(o[0:1, 0:1], ident[:, 0:1], ident[:, 0:1], start=True, stop=True)

            def hold_open(o):
                pe.matmul(o[0:1, T - 1:T], ident[:, 0:1], ident[:, 0:1], start=False, stop=True, skip_group_check=True)

            def features_product(banks, at, left, right):
                for c in range(CHUNKS):
                    for j in two:
                        done = pe.matmul(banks[j][half(c % 2), at + c // 2 * CH:at + (c // 2 + 1) * CH],
                                         left[half(j), chunk(c)], right[half(j), chunk(c)], start=True, stop=True)
                return done

            def chunk_product(banks, at, left, right, l, h_):
                for b in range(8):
                    for p in two:
                        done = pe.matmul(banks[p][half(p), at + b * 32:at + (b + 1) * 32], left[half(p), b, :],
                                         halves(right[half(p), b, :], l, h_), start=True, stop=True)
                return done

            def inverse(step, **n):
                if step == 0:
                    pe.wait_ge(*iv("b", **n))
                    pe.wait_ge(*ia("a_next", **n))
                    hold(sa[2])
                    features_product(sa[2:4], 0, op_b, a_next)
                    features_product(sa[2:4], 4 * CH, a_next, op_b).then_inc(*ip.tell("ab"))
                    return
                l = (step + 1) // 2
                if step % 2:
                    pe.wait_ge(*iv("e", l, **n))
                    pe.wait_ge(*ia("mab", **n))
                    if l > 1:
                        pe.wait_ge(*iv("xt", l - 1, **n))
                    hold(sa[2])
                    chunk_product(sa[2:4], 0, e_mat, x_mat, l, 0).then_inc(*ip.tell("z", l))
                else:
                    pe.wait_ge(*ia("z", l, **n))
                    pe.wait_ge(*iv("z", l, **n))
                    hold(sa[0])
                    if l < 5:
                        chunk_product(sa[0:2], 0, xt_mat, z_mat[l - 1], l, 0)
                    chunk_product(sa[0:2], 256, z_mat[l - 1], xt_mat, l, 1).then_inc(*ip.tell("zx", l))

            def prepare(**n):
                pe.wait_ge(*ia("r_next", **n))
                pe.wait_ge(*iv("k", **n))
                hold(sa[2])
                features_product(sa[2:4], 0, op_k, a_next)
                features_product(sa[2:4], 4 * CH, op_b, r_next).then_inc(*ip.tell("ak"))
                features_product(sb_[0:2], 0, op_k, r_next).then_inc(*ip.tell("rk"))
                pe.wait_ge(*iv("xt", 5, **n))
                for o, op in ((sa[0], op_b), (sa[1], op_k)):
                    for t in range(TT):
                        done = pe.transpose(o[:, t * P:(t + 1) * P], op[:, t * P:(t + 1) * P], ident[:])
                done.then_inc(*ip.tell("tr"))

            def chain(point, **n):
                for c in range(CHUNKS):
                    p, t = c % 2, c // 2
                    hp, tok = half(p), chunk(c)
                    if c:
                        pe.wait_ge(*cv("st", c - 1, **n))
                        pe.wait_ge(*cp("y", c - 1, **n))
                        hold_open(sb_[0])
                        for j in two:
                            pe.matmul(sb_[j][hp, 0:CH], op_a[half(j), tok], st_s[half(j), :], start=True, stop=False)
                        for j in two:
                            done = pe.matmul(sb_[2 + j][half(j), tok], st_s[half(j), :], op_r[half(j), tok], start=True, stop=False)
                        done.then_inc(*cp.tell("s", c))
                        pe.wait_ge(*cp("s", c, **n))
                        hold_open(sb_[0])
                    for j in two:
                        done = pe.matmul(sb_[j][hp, 0:CH], mak_t[hp, 4 * j + t, :], op_v[hp, t, half(j)], start=c == 0, stop=True)
                    done.then_inc(*cp.tell("rhs", c))
                    for j in two:
                        pe.matmul(sb_[2 + j][half(j), tok], op_v[hp, t, half(j)], mrk_t[hp, 4 * j + t, :], start=c == 0, stop=False)
                    point(3 * c)
                    pe.wait_ge(*ca("rhs", c, **n))
                    pe.wait_ge(*cv("rhs", c, **n))
                    hold_open(sb_[0])
                    for j in two:
                        done = pe.matmul(sb_[j][hp, CH:2 * CH], xt_c[hp, 4 * j + t, :], rhs_s[hp, j, :], start=True, stop=True)
                    done.then_inc(*cp.tell("sa", c))
                    point(3 * c + 1)
                    pe.wait_ge(*ca("sa", c, **n))
                    pe.wait_ge(*cv("sa", c, **n))
                    hold_open(sb_[0])
                    if c < LAST:
                        for j in two:
                            pe.matmul(sb_[j][half(j), 2 * CH:3 * CH], kt_mat[hp, t, half(j)], op_v[hp, t, half(j)], start=True, stop=False)
                        for j in two:
                            done = pe.matmul(sb_[j][half(j), 2 * CH:3 * CH], bt_mat[hp, t, half(j)], sa_s[hp, j, :], start=False, stop=True)
                        done.then_inc(*cp.tell("st", c))
                    for j in two:
                        done = pe.matmul(sb_[2 + j][half(j), tok], sa_s[hp, j, :], mrb_t[hp, 4 * j + t, :], start=False, stop=True)
                    done.then_inc(*cp.tell("y", c))
                    point(3 * c + 2)

            pe.wait_ge(*rv("A", KT - 1))
            pe.wait_ge(*ra("bonus"))
            for step in range(11):
                inverse(step)
            prepare()
            with pe.Fori(0, KT - 1) as i:
                pe.wait_ge(*iv("kt", i=i))
                pe.wait_ge(*ia("bt", i=i))
                hold(sa[0])
                chain(lambda q: inverse(POINTS[q], i=i, k=1) if q in POINTS else None, i=i)
                pe.wait_ge(*cv("y", i=i))
                prepare(i=i, k=1)
            pe.wait_ge(*iv("kt", k=KT - 1))
            pe.wait_ge(*ia("bt", k=KT - 1))
            chain(lambda q: None, k=KT - 1)

        def tile_of(t, i, k):
            return t[:, k:k + 1, :] if i is None else t[:, bass.ds(i + k if k else i, 1), :]

        def flat(t):
            return t.rearrange("p a t -> p (a t)")

        def pairs_scalar(act):
            def inverse(step, i=None, k=0):
                n = dict(i=i, k=k)
                if step == 0:
                    act.wait_ge(*ip("ab", **n))
                    act.activation(flat(mab_t[:, rows4(0), :]), bank[SETA][2][:, 0:4 * CH], ACT.Copy).then_inc(*ia.tell("mab"))
                elif step % 2:
                    l = (step + 1) // 2
                    act.wait_ge(*ip("z", l, **n))
                    act.activation(halves(z_mat[l - 1][half(0)], l, 0), packed(bank[SETA][2][half(0), 0:256], l), ACT.Copy).then_inc(*ia.tell("z", l))

            def begin(i=None, k=0):
                act.activation(a_next[:], flat(tile_of(s_arr, i, k)), ACT.Copy).then_inc(*ia.tell("a_next"))
                act.activation(r_next[:], flat(tile_of(r_arr, i, k)), ACT.Copy).then_inc(*ia.tell("r_next"))

            def prepare(i=None, k=0):
                n = dict(i=i, k=k)
                act.activation(op_a[:], a_next[:], ACT.Copy).then_inc(*ia.tell("a"))
                act.activation(op_r[:], r_next[:], ACT.Copy).then_inc(*ia.tell("r"))
                act.activation(op_v[:], v_arr[:, :, 0:P] if i is None else v_arr[:, :, bass.ds(i * P + P, P)], ACT.Copy).then_inc(*ia.tell("v"))
                act.wait_ge(*ip("tr", **n))
                act.wait_ge(*ia("r", **n))
                act.activation(flat(bt_mat[:]), bank[SETA][0][:], ACT.Copy).then_inc(*ia.tell("bt"))

            def chain(point, **n):
                for c in range(CHUNKS):
                    hp = half(c % 2)
                    if 0 < c < LAST:
                        act.wait_ge(*cv("st", c - 1, **n))
                        act.activation(st_f[:], st_s[:], ACT.Copy, scale=fac_b[:, c:c + 1]).then_inc(*ca.tell("fade", c))
                    act.wait_ge(*cp("rhs", c, **n))
                    act.activation(rhs_s[hp, 0, :], bank[SETB][0][hp, 0:CH], ACT.Copy).then_inc(*ca.tell("rhs", c))
                    point(3 * c)
                    act.wait_ge(*cp("sa", c, **n))
                    act.activation(sa_s[hp, 0, :], bank[SETB][0][hp, CH:2 * CH], ACT.Copy).then_inc(*ca.tell("sa", c))
                    point(3 * c + 1)
                    point(3 * c + 2)

            act.wait_ge(*rv("A", KT - 1))
            act.wait_ge(*ra("v", 1, TT - 1))
            act.wait_ge(cv0, len(LEVELS))
            begin()
            for step in range(11):
                inverse(step)
            act.wait_ge(*ia("r_next"))
            prepare()
            with act.Fori(0, KT - 1) as i:
                begin(i, 1)
                chain(lambda q: inverse(POINTS[q], i, 1) if q in POINTS else None, i=i)
                act.wait_ge(*cp("y", LAST, i=i))
                prepare(i, 1)
            chain(lambda q: None, k=KT - 1)

        def pairs_vector(dve):
            sa, sb_ = bank[SETA], bank[SETB]

            def mask(j, n):
                return masks[:, j:j + 1, :].to_broadcast([P, n, CH])

            def blocks(t, j=0):
                return t[:, j * 4 * CH:(j + 1) * 4 * CH].rearrange("p (a t) -> p a t", t=CH)

            def begin(i=None, k=0):
                dve.tensor_copy(op_b[:], flat(tile_of(a_arr, i, k))).then_inc(*iv.tell("b"))
                dve.tensor_copy(op_k[:], flat(tile_of(k_arr, i, k))).then_inc(*iv.tell("k"))

            def add_halves(name, l, h_, at, t, out_, **n):
                for p in two:
                    dve.tensor_tensor(halves(out_[half(p)], l, h_), halves(t[half(p)], l, h_), packed(sa[p][half(p), at:at + 256], l),
                                      ALU.add).then_inc(*(iv.tell(name, l) if p else iv.tell(name, l, 0)))

            def inverse(step, i=None, k=0):
                n = dict(i=i, k=k)
                if step == 0:
                    dve.wait_ge(*ip("ab", **n))
                    dve.tensor_copy(flat(mab_t[:, rows4(1), :]), sa[3][:, 0:4 * CH]).then_inc(*iv.tell("mab"))
                    dve.wait_ge(*ia("mab", **n))
                    for j in two:
                        dve.tensor_tensor(x_mat[:, rows4(j), :], blocks(sa[2 + j], 1), mask(6, 4), ALU.mult).then_inc(*iv.tell("x1", j))
                    dve.wait_ge(*iv("mab", **n))
                    dve.tensor_tensor(xt_mat[:], mab_t[:], mask(0, 8), ALU.mult).then_inc(*iv.tell("xt1"))
                    dve.wait_ge(*iv("xt1", **n))
                    dve.tensor_tensor(x_mat[:], x_mat[:], mask(9, 8), ALU.add).then_inc(*iv.tell("x", 0))
                    dve.tensor_tensor(xt_mat[:], xt_mat[:], mask(9, 8), ALU.add).then_inc(*iv.tell("xt", 0))
                    dve.tensor_tensor(e_mat[:], mab_t[:], mask(1, 8), ALU.mult).then_inc(*iv.tell("e", 1))
                    return
                l = (step + 1) // 2
                if step % 2:
                    dve.wait_ge(*ip("z", l, **n))
                    dve.tensor_copy(halves(z_mat[l - 1][half(1)], l, 0), packed(sa[3][half(1), 0:256], l)).then_inc(*iv.tell("z", l))
                    if l < 5:
                        dve.tensor_tensor(e_mat[:], mab_t[:], mask(l + 1, 8), ALU.mult).then_inc(*iv.tell("e", l + 1))
                elif l < 5:
                    dve.wait_ge(*ip("zx", l, **n))
                    add_halves("x", l, 0, 0, x_mat, x_mat, **n)
                    add_halves("xt", l, 1, 256, xt_mat, xt_mat, **n)

            def prepare(i=None, k=0):
                n = dict(i=i, k=k)
                dve.wait_ge(*iv("xt", 4, **n))
                dve.tensor_copy(halves(xt_c[:], 5, 0), halves(xt_mat[:], 5, 0)).then_inc(*iv.tell("xt_copy"))
                dve.wait_ge(*ip("zx", 5, **n))
                add_halves("xt", 5, 1, 256, xt_mat, xt_c, **n)
                dve.tensor_copy(fac_b[:, 0:LAST], flat(tile_of(fac, i, k)[:, :, 0:LAST])).then_inc(*iv.tell("fac"))
                dve.wait_ge(*ip("rk", **n))
                for name, m, banks, at, w in (("mak", mak_t, sa[2:4], 0, 7), ("mrb", mrb_t, sa[2:4], 1, 8), ("mrk", mrk_t, sb_[0:2], 0, 8)):
                    for j in two:
                        dve.tensor_tensor(m[:, rows4(j), :], blocks(banks[j], at), mask(w, 4), ALU.mult).then_inc(*iv.tell(name, j))
                dve.wait_ge(*ip("tr", **n))
                dve.tensor_copy(flat(kt_mat[:]), sa[1][:]).then_inc(*iv.tell("kt"))

            def chain(point, **n):
                dve.wait_ge(*iv("fac", **n))
                for c in range(CHUNKS):
                    hp = half(c % 2)
                    dve.wait_ge(*cp("rhs", c, **n))
                    dve.tensor_copy(rhs_s[hp, 1, :], sb_[1][hp, 0:CH]).then_inc(*cv.tell("rhs", c))
                    point(3 * c)
                    dve.wait_ge(*cp("sa", c, **n))
                    dve.tensor_copy(sa_s[hp, 1, :], sb_[1][hp, CH:2 * CH]).then_inc(*cv.tell("sa", c))
                    point(3 * c + 1)
                    if c < LAST:
                        if c:
                            dve.wait_ge(*ca("fade", c, **n))
                        dve.wait_ge(*cp("st", c, **n))
                        for j in two:
                            signal = cv.tell("st", c) if j else cv.tell("st", c, 0)
                            o, d, fc = st_s[half(j), :], sb_[j][half(j), 2 * CH:3 * CH], fac_b[half(j), c:c + 1]
                            if c:
                                dve.scalar_tensor_tensor(out=o, in0=d, scalar=fc, in1=st_f[half(j), :], op0=ALU.mult, op1=ALU.add).then_inc(*signal)
                            else:
                                dve.tensor_scalar(o, d, fc, None, ALU.mult).then_inc(*signal)
                    point(3 * c + 2)
                dve.wait_ge(*cp("y", LAST, **n))
                for j in two:
                    dve.tensor_copy(flat(tile_of(r_arr, n.get("i"), n.get("k", 0))[half(j)]), sb_[2 + j][half(j), :]).then_inc(
                        *(cv.tell("y") if j else cv.tell("y", 0)))

            dve.wait_ge(*rv("A", KT - 1))
            dve.wait_ge(*ra("fac", KT - 1))
            dve.wait_ge(*rp("bonus", KT - 1))
            for z in z_mat:
                dve.memset(z[:], 0.0).then_inc(cv0, 1)
            dve.wait_ge(cv0, len(LEVELS))
            begin()
            for step in range(11):
                inverse(step)
            prepare()
            with dve.Fori(0, KT - 1) as i:
                begin(i, 1)
                chain(lambda q: inverse(POINTS[q], i, 1) if q in POINTS else None, i=i)
                prepare(i, 1)
            chain(lambda q: None, k=KT - 1)

        gp = Steps("group_pe", ["mean"] + [("mean", k) for k in each] + ["var"] + [("rstd", k) for k in each] + [(n, k) for k in each for n in ("bonus", "vt")])
        ga = Steps("group_act", ["mean"] + [("sq", k) for k in each] + ["root"] + [("vt", k) for k in each])
        gv = Steps("group_dve", [("sub", k) for k in each] + ["rec"] + [(n, k) for k in each for n in ("scale", "gain")] +
                   [(n, k) for k in each for n in ("bv", "add")] + [("gate", k) for k in each])

        def group_tensor(pe, s):
            sa, sb_ = bank[SETA], bank[SETB]
            end = KT - 1
            pe.wait_ge(*cv("y", k=end))
            for k in each:
                done = pe.matmul(sa[0][0:HEADS, :], gather[:, k, :], r_arr[:, k, :], start=k == 0, stop=k == end)
            done.then_inc(*gp.tell("mean"))
            pe.wait_ge(*ga("mean"))
            for k in each:
                if k >= 4:
                    pe.wait_ge(*gv("sub", k - 4))
                pe.matmul(sb_[k % 4][:], spread[:, k, :], head_b[:], start=True, stop=True).then_inc(*gp.tell("mean", k))
            for k in each:
                pe.wait_ge(*ga("sq", k))
                done = pe.matmul(sa[1][0:HEADS, :], gather[:, k, :], tmp[k][:], start=k == 0, stop=k == end)
            done.then_inc(*gp.tell("var"))
            pe.wait_ge(*gv("rec"))
            for k in each:
                if k >= 4:
                    pe.wait_ge(*gv("scale", k - 4))
                pe.matmul(sb_[k % 4][:], spread[:, k, :], head_b[:], start=True, stop=True).then_inc(*gp.tell("rstd", k))
            for k in each:
                if k >= 2:
                    pe.wait_ge(*gv("bv", k - 2))
                pe.matmul(sa[2 + k % 2][:], spread[:, k, :], head_a[:], start=True, stop=True).then_inc(*gp.tell("bonus", k))
                if k == 0:
                    pe.wait_ge(*ga("root"))
                if k >= 2:
                    pe.wait_ge(*ga("vt", k - 2))
                for t in range(TT):
                    done = pe.transpose(sa[k % 2][:, t * P:(t + 1) * P], v_arr[:, t, k * P:(k + 1) * P], ident[:])
                done.then_inc(*gp.tell("vt", k))
            pe.wait_ge(*gv("scale", end))
            unit_products(pe, [o[:] for o in sb_], tg_hi[:], tg_lo[:], True, True, s.n_g)
            pe.wait_ge(*gv("bv", end))
            unit_products(pe, [o[:] for o in sa], tg_hi[:], tg_lo[:], True, True, s.n_g + 1)
            pe.wait_ge(*gv("gate", end))
            for b, set_ in enumerate((SETA, SETB)):
                for k in each:
                    if b == 0:
                        pe.wait_ge(x_lo_ready, s.x0 + len(X_ORDER) + k + 1)
                    unit_products(pe, [o[:] for o in bank[set_]], x_hi[:, k, :], x_lo[:, k, :], k == 0, k == end, s.u1 + b * KT + k)
            output_tensor(pe, s)

        def group_scalar(act, s):
            sa = bank[SETA]
            act.wait_ge(*gp("mean"))
            act.activation(head_b[:], sa[0][0:HEADS, :], ACT.Copy, scale=1.0 / 64).then_inc(*ga.tell("mean"))
            for k in each:
                act.wait_ge(*gv("sub", k))
                act.activation(tmp[k][:], r_arr[:, k, :], ACT.Square).then_inc(*ga.tell("sq", k))
            act.wait_ge(*gp("var"))
            act.activation(head_c[:], sa[1][0:HEADS, :], ACT.Sqrt, bias=gn_eps[0:HEADS, :], scale=1.0 / 64).then_inc(*ga.tell("root"))
            for k in each:
                act.wait_ge(*gp("vt", k))
                act.activation(tmp[k][:], sa[k % 2][:], ACT.Copy).then_inc(*ga.tell("vt", k))
            for k in each:
                act.wait_ge(*gv("gate", k))
                act.activation(x_hi[:, k, :], r_arr[:, k, :], ACT.Copy).then_inc(x_hi_ready, 1)
            output_scalar(act, s)

        def group_vector(dve, s):
            sa, sb_ = bank[SETA], bank[SETB]
            y = lambda k: r_arr[:, k, :]
            for k in each:
                dve.wait_ge(*gp("mean", k))
                dve.tensor_tensor(y(k), y(k), sb_[k % 4][:], ALU.subtract).then_inc(*gv.tell("sub", k))
            dve.wait_ge(*ga("root"))
            dve.reciprocal(head_b[:], head_c[:]).then_inc(*gv.tell("rec"))
            for k in each:
                dve.wait_ge(*gp("rstd", k))
                dve.tensor_tensor(y(k), y(k), sb_[k % 4][:], ALU.mult).then_inc(*gv.tell("scale", k))
                dve.wait_ge(*gv("scale", k))
                dve.tensor_scalar(y(k), y(k), vcol("gn_g", k), vcol("gn_b", k), ALU.mult, ALU.add).then_inc(*gv.tell("gain", k))
            for k in each:
                dve.wait_ge(*ga("vt", k))
                dve.tensor_tensor(tmp[k][:], tmp[k][:], sa[2 + k % 2][:], ALU.mult).then_inc(*gv.tell("bv", k))
                dve.wait_ge(*gv("bv", k))
                dve.tensor_tensor(y(k), y(k), tmp[k][:], ALU.add).then_inc(*gv.tell("add", k))
            for k in each:
                dve.wait_ge(w_used, s.n_g + 1 + k // 4)
                dve.wait_ge(*gv("add", KT - 1))
                dve.tensor_tensor(y(k), y(k), bank[(SETB, SETA)[k // 4]][k % 4][:], ALU.mult).then_inc(*gv.tell("gate", k))
            for k in each:
                dve.wait_ge(x_hi_ready, s.x0 + len(X_ORDER) + k + 1)
                dve.tensor_tensor(x_lo[:, k, :], y(k), x_hi[:, k, :].bitcast(F32), ALU.subtract).then_inc(x_lo_ready, 1)
            output_vector(dve, s)

        k_sh = sb("k_sh", [P, 2, T], at=where["wa_hi"])
        v_sh = sb("v_sh", [P, TT, KV], at=where["wa_hi"] + 4 * 2 * T)
        assert where["v_sh"] + 4 * TT * KV <= where["fac"]
        kvv = Steps("kv_dve", [("k", 0), ("k", 1), ("kb", 0), ("kb", 1)] + [("v", t) for t in range(TT)])

        def kv_tensor(pe, s):
            sb_ = bank[SETB]
            for k in each:
                n = s.kv + k
                pe.wait_ge(x_lo_ready, s.x0 - KT + k + 1)
                pe.wait_ge(w_lo_ready, n + 1)
                first, last, hi, lo = k == 0, k == KT - 1, w_hi[:, n % RW, :], w_lo[:, n % RW, :]
                for m in range(2):
                    c = slice(m * P, (m + 1) * P)
                    pe.matmul(sb_[m][:], hi[:, c], x_hi[:, k, :], start=first, stop=False)
                    pe.matmul(sb_[m][:], hi[:, c], x_lo[:, k, :], start=False, stop=False)
                    pe.matmul(sb_[m][:], lo[:, c], x_hi[:, k, :], start=False, stop=last)
                for t in range(TT):
                    o, c = sb_[2 + t // 2][:, t % 2 * KV:(t % 2 + 1) * KV], slice(t * P, (t + 1) * P)
                    pe.matmul(o, x_hi[:, k, c], hi[:, KV:], start=first and t % 2 == 0, stop=False)
                    pe.matmul(o, x_lo[:, k, c], hi[:, KV:], start=False, stop=False)
                    done = pe.matmul(o, x_hi[:, k, c], lo[:, KV:], start=False, stop=last and t % 2 == 1)
                done.then_inc(w_used, 1)
            norm_sums(pe, s.pre, bank[SETA][0])
            norm_wide(pe, s.pre, bank[SETA][1])
            pe.wait_ge(*kvv("v", TT - 1))

        def kv_vector(dve, s):
            sb_ = bank[SETB]
            dve.wait_ge(rstd_ready, s.rs + 1)
            dve.wait_ge(w_used, s.kv + KT)
            dve.wait_ge(diag_ready, (1 + TT) * (s.pre.n + 1))
            for m in range(2):
                dve.tensor_tensor(k_sh[:, m, :], sb_[m][:], rstd[:], ALU.mult).then_inc(*kvv.tell("k", m))
            for m in range(2):
                dve.wait_ge(*kvv("k", m))
                dve.tensor_scalar(k_sh[:, m, :], k_sh[:, m, :], vcol("b_k", m), None, ALU.add).then_inc(*kvv.tell("kb", m))
            for t in range(TT):
                dve.scalar_tensor_tensor(out=v_sh[:, t, :], in0=sb_[2 + t // 2][:, t % 2 * KV:(t % 2 + 1) * KV], scalar=rinv[:, t:t + 1],
                                         in1=rows[:, 0:KV], op0=ALU.mult, op1=ALU.add).then_inc(*kvv.tell("v", t))

        at_[0] = where["mid_hi"]

        def mid_buffer(name, shape, dt=F32):
            t = sb(name, shape, dt, at=at_[0])
            at_[0] += -(-4 * int(np.prod(shape[1:])) // 64) * 64
            assert at_[0] <= where["mid_hi"] + 2 * 4 * FT * T
            return t

        q_t, o_t = (mid_buffer(n, [P, KT, T]) for n in ("q_t", "o_t"))
        q_one = mid_buffer("q_one", [P, 2, T])
        window = mid_buffer("window", [P, TT, 2 * P])
        score = mid_buffer("score", [P, 2, TT, 2 * P])
        prob_t = mid_buffer("prob_t", [P, 2, TT, 2, P])
        o_tok = mid_buffer("o_tok", [P, TT, P])
        top, neg, total, sink_e, den, inv = (mid_buffer(n, [P, 2, TT]) for n in ("top", "neg", "total", "sink_e", "den", "inv"))
        sink = mid_buffer("sink", [P, 2])
        ada_c = mid_buffer("ada_c", [P, 1])
        ada_sum = mid_buffer("ada_sum", [P, 3 * D])
        ada_w = mid_buffer("ada_w", [P, 3 * D])

        class Swa:
            def __init__(self, first_unit, x_tiles, updates):
                self.x0, self.h0 = x_tiles, KT * updates
                self.n_q, self.u1, self.rows = first_unit, first_unit + 2 * KT, KT
                self.end = self.u1 + 2 * KT
                self.pre, self.post = Norm(KT), Norm(KT)
                self.rs = new_rstd()
                self.gain_in, self.gain_out, self.bias, self.half, self.kv = "norm12", "norm13", "b_o", 1.0, None

        window_loaded = sem("window_loaded")
        ada_loaded = sem("ada_loaded")
        ada_ready = sem("ada_ready")
        mod_ready = sem("mod_ready")
        q_zero = sem("q_zero")
        qv = Steps("query_dve", [(n, k) for k in each for n in ("q", "bias")])
        gp_ = Steps("score_pe", [("score", j) for j in two])
        ga_ = Steps("score_act", [s_ for j in two for s_ in [("exp", j, n) for n in range(TT)] + [("sink", j)]])
        gv_ = Steps("score_dve", [("q", 0), "q", "sink"] + [s_ for j in two for s_ in [("mask", j, 0), ("mask", j, 1), ("top", j), ("neg", j)]])
        ap = Steps("value_pe", [("turn", j) for j in two] + ["value", "turn_o"])
        aa = Steps("value_act", [("turn", j) for j in two])
        av = Steps("value_dve", [s_ for j in two for s_ in [("den", j), ("inv", j)]] + [("turn", j) for j in two] + [("o", j) for j in two] + ["turn_o", "ada_c", "ada"])

        def swa_rounds(eng, values, scores):
            scores(0, i=None, k=0)
            with eng.Fori(0, 3) as i:
                values(0, lambda: scores(1, i=i, k=1, m=2), i=i, k=0, m=2)
                values(1, lambda: scores(0, i=i, k=2, m=2), i=i, k=1, m=2)
            values(0, lambda: scores(1, i=None, k=7), i=None, k=6)
            values(1, lambda: None, i=None, k=7)

        def round_of(i, k, m=1):
            return k if i is None else i * m + k if k else i * m

        def tile_at(t, i, k, m=1):
            return flat(t[:, k:k + 1, :] if i is None else t[:, bass.ds(round_of(i, k, m), 1), :])

        def swa_tensor(pe, s):
            sa, sb_ = bank[SETA], bank[SETB]
            for b, set_ in enumerate((SETB, SETA)):
                for k in each:
                    if b == 0:
                        pe.wait_ge(x_lo_ready, s.x0 + k + 1)
                    unit_products(pe, [o[:] for o in bank[set_]], x_hi[:, k, :], x_lo[:, k, :], k == 0, k == KT - 1, s.n_q + b * KT + k)
                if b == 0:
                    norm_sums(pe, s.pre, sa[0])
                    norm_wide(pe, s.pre, sa[1])
                    pe.wait_ge(rstd_ready, s.rs + 1)
            pe.wait_ge(*qv("bias", KT - 1))

            def scores(g, **n):
                pe.wait_ge(*gv_("q", **n))
                for t in range(TT):
                    k0 = max(t - 1, 0) * P
                    for j in two:
                        done = pe.matmul(sa[2 * j + t // 2][:, t % 2 * 2 * P:(t % 2 + 1) * 2 * P], q_one[:, j, t * P:(t + 1) * P],
                                         k_sh[:, g, k0:k0 + 2 * P], start=True, stop=True)
                        if t == TT - 1:
                            done.then_inc(*gp_.tell("score", j))

            def values(g, between, **n):
                for j in two:
                    pe.wait_ge(*ga_("exp", j, TT - 1, **n))
                    for q in range(TT):
                        for t in range(2):
                            done = pe.transpose(sb_[2 * j + q // 2][:, (q % 2 * 2 + t) * P:(q % 2 * 2 + t + 1) * P],
                                                score[:, j, q, t * P:(t + 1) * P], ident[:])
                    done.then_inc(*ap.tell("turn", j))
                between()
                for j in two:
                    pe.wait_ge(*aa("turn", j, **n))
                    pe.wait_ge(*av("turn", j, **n))
                    c = slice((2 * g + j) * 64, (2 * g + j + 1) * 64)
                    for q in range(TT):
                        for t in range(2):
                            done = pe.matmul(sb_[0][:, q * P + j * 64:q * P + (j + 1) * 64], prob_t[:, j, q, t, :],
                                             v_sh[:, max(q - 1, 0) + t, c], start=t == 0, stop=t == 1)
                done.then_inc(*ap.tell("value"))
                pe.wait_ge(*av("o", 1, **n))
                for t in range(TT):
                    done = pe.transpose(sb_[1][:, t * P:(t + 1) * P], o_tok[:, t, :], ident[:])
                done.then_inc(*ap.tell("turn_o"))
                pe.wait_ge(*av("turn_o", **n))

            swa_rounds(pe, values, scores)
            pe.wait_ge(*av("ada", k=KT - 1))
            for m in range(3 * KT):
                done = pe.matmul(sb_[3][:, m:m + 1], ada_sum[:, m * P:(m + 1) * P], ones[:, 0:1], start=True, stop=True)
            done.then_inc(ada_ready, 1)
            for b, set_ in enumerate((SETA, SETB)):
                for k in each:
                    if b == 0:
                        pe.wait_ge(x_lo_ready, s.x0 + KT + k + 1)
                    elif k == 0:
                        pe.wait_ge(mod_ready, 2)
                    unit_products(pe, [o[:] for o in bank[set_]], x_hi[:, k, :], x_lo[:, k, :], k == 0, k == KT - 1, s.u1 + b * KT + k)
            output_tensor(pe, s)

        def swa_scalar(act, s):
            act.wait_ge(w_used, s.n_q)
            act.dma_start(window[:], window_in).then_inc(window_loaded, 16)
            norm_root(act, s.pre, bank[SETA][0], D)
            act.wait_ge(wide_ready, s.pre.n + 1)
            act.activation(rstd[:], bank[SETA][1][:], ACT.Copy).then_inc(rstd_ready, 1)

            def scores(g, **n):
                for j in two:
                    act.wait_ge(*gv_("neg", j, **n))
                    for t in range(TT):
                        act.activation(score[:, j, t, :], score[:, j, t, :], ACT.Exp, bias=neg[:, j, t:t + 1],
                                       accum_out=total[:, j, t:t + 1]).then_inc(*ga_.tell("exp", j, t))
                    act.activation(sink_e[:, j, :], neg[:, j, :], ACT.Exp, bias=sink[:, j:j + 1]).then_inc(*ga_.tell("sink", j))

            def values(g, between, **n):
                source = ada_in[n["k"]] if n["i"] is None else ada_in[bass.ds(round_of(**n), 1)].rearrange("a p c -> (a p) c")
                act.dma_start(ada_w[:], source).then_inc(ada_loaded, 16)
                for j in two:
                    act.wait_ge(*ap("turn", j, **n))
                    act.activation(prob_t[:, j, 0:2], bank[SETB][2 * j][:].rearrange("p (n t q) -> p n t q", t=2, q=P), ACT.Copy).then_inc(*aa.tell("turn", j))
                between()
                act.wait_ge(*av("ada", **n))

            swa_rounds(act, values, scores)
            output_parts_scalar(act, s.x0 + KT, o_t, lambda k: av("turn_o", k=KT - 1))
            output_scalar(act, s)

        def output_parts_scalar(act, x0, arr, ready):
            for k in each:
                act.wait_ge(*ready(k))
                act.activation(x_hi[:, k, :], arr[:, k, :], ACT.Copy).then_inc(x_hi_ready, 1)

        def output_parts_vector(dve, x0, arr):
            for k in each:
                dve.wait_ge(x_hi_ready, x0 + k + 1)
                dve.tensor_tensor(x_lo[:, k, :], arr[:, k, :], x_hi[:, k, :].bitcast(F32), ALU.subtract).then_inc(x_lo_ready, 1)

        def swa_vector(dve, s):
            sa, sb_ = bank[SETA], bank[SETB]
            norm_diag(dve, s.pre)
            dve.memset(ada_sum[:], 0.0).then_inc(mod_ready, 1)
            dve.memset(q_one[:], 0.0).then_inc(q_zero, 1)
            dve.wait_ge(rstd_ready, s.rs + 1)
            for k in each:
                dve.wait_ge(w_used, s.n_q + (k // 4 + 1) * KT)
                dve.tensor_tensor(q_t[:, k, :], bank[(SETB, SETA)[k // 4]][k % 4][:], rstd[:], ALU.mult).then_inc(*qv.tell("q", k))
                dve.wait_ge(*qv("q", k))
                dve.tensor_scalar(q_t[:, k, :], q_t[:, k, :], vcol("b_q", k), None, ALU.add).then_inc(*qv.tell("bias", k))
            dve.wait_ge(*qv("bias", KT - 1))
            dve.wait_ge(window_loaded, 16)
            dve.wait_ge(mod_ready, 1)
            dve.wait_ge(q_zero, 1)

            def load(**n):
                for j in two:
                    dve.tensor_copy(q_one[half(j), j, :], tile_at(q_t, **n)[half(j)]).then_inc(*(gv_.tell("q") if j else gv_.tell("q", 0)))

            def scores(g, i, k, m=1):
                n = dict(i=i, k=k, m=m)
                if i is None and k == 0:
                    load(**n)
                c = KV + 2 * k
                dve.tensor_copy(sink[:], rows[:, c:c + 2] if i is None else rows[:, bass.ds(i * (2 * m) + c, 2)]).then_inc(*gv_.tell("sink"))
                for j in two:
                    dve.wait_ge(*gp_("score", j, **n))
                    for b in two:
                        dve.scalar_tensor_tensor(out=score[:, j, 2 * b:2 * b + 2, :], in0=sa[2 * j + b][:].rearrange("p (n k) -> p n k", n=2),
                                                 scalar=0.125, in1=window[:, 2 * b:2 * b + 2, :], op0=ALU.mult, op1=ALU.add).then_inc(*gv_.tell("mask", j, b))
                    dve.wait_ge(*gv_("mask", j, 1, **n))
                    dve.tensor_reduce(top[:, j, :], score[:, j], mybir.AxisListType.X, ALU.max).then_inc(*gv_.tell("top", j))
                    dve.wait_ge(*gv_("top", j, **n))
                    dve.tensor_scalar(neg[:, j, :], top[:, j, :], sink[:, j:j + 1], -1.0, ALU.max, ALU.mult).then_inc(*gv_.tell("neg", j))

            def values(g, between, i, k, m=1):
                n = dict(i=i, k=k, m=m)
                if i is not None or k < KT - 1:
                    load(i=i, k=k + 1, m=m)
                for j in two:
                    dve.wait_ge(*ga_("sink", j, **n))
                    dve.tensor_tensor(den[:, j, :], total[:, j, :], sink_e[:, j, :], ALU.add).then_inc(*av.tell("den", j))
                    dve.wait_ge(*av("den", j, **n))
                    dve.reciprocal(inv[:, j, :], den[:, j, :]).then_inc(*av.tell("inv", j))
                for j in two:
                    dve.wait_ge(*ap("turn", j, **n))
                    dve.tensor_copy(prob_t[:, j, 2:4], sb_[2 * j + 1][:].rearrange("p (n t q) -> p n t q", t=2, q=P)).then_inc(*av.tell("turn", j))
                between()
                dve.wait_ge(*ap("value", **n))
                for j in two:
                    dve.tensor_tensor(o_tok[:, :, half(j)], sb_[0][:].rearrange("p (n c) -> p n c", n=TT)[:, :, half(j)],
                                      inv[:, j, :].rearrange("p (n o) -> p n o", o=1).to_broadcast([P, TT, 64]), ALU.mult).then_inc(*av.tell("o", j))
                dve.wait_ge(*ap("turn_o", **n))
                dve.tensor_copy(tile_at(o_t, **n), sb_[1][:]).then_inc(*av.tell("turn_o"))
                c = VEC.at["c"] + k
                dve.tensor_copy(ada_c[:], vec[:, c:c + 1] if i is None else vec[:, bass.ds(i * m + c, 1)]).then_inc(*av.tell("ada_c"))
                dve.wait_ge(*av("ada_c", **n))
                dve.wait_ge(ada_loaded, 16 * k + 16 if i is None else i * (16 * m) + (16 * k + 16))
                dve.scalar_tensor_tensor(out=ada_sum[:], in0=ada_w[:], scalar=ada_c[:, 0:1], in1=ada_sum[:], op0=ALU.mult, op1=ALU.add).then_inc(*av.tell("ada"))

            swa_rounds(dve, values, scores)
            output_parts_vector(dve, s.x0 + KT, o_t)
            dve.wait_ge(ada_ready, 1)
            dve.tensor_tensor(mod[:], bank[SETB][3][:, 0:3 * KT], vec[:, VEC.at["b_ada"]:VEC.at["b_ada"] + 3 * KT], ALU.add).then_inc(mod_ready, 1)
            output_vector(dve, s)

        at_[0] = where["mid_hi"]
        sb_q, sb_k, sb_v, sb_z = (mid_buffer(n, [P, 4, T]) for n in ("sb_q", "sb_k", "sb_v", "sb_z"))
        c_q, k_rot, c_kv = mid_buffer("c_q", [P, 3, T]), mid_buffer("k_rot", [P, T]), mid_buffer("c_kv", [P, 2, T])
        mla_z, gate_a, gate_b = mid_buffer("mla_z", [P, 4, T]), mid_buffer("gate_a", [P, KT, T]), mid_buffer("gate_b", [P, KT, T])
        x_norm = sb("x_norm", [P, KT, T], at=where["gate_a"])
        at_[0] = where["x_hi"]
        stick_z, stick_l = (pair_buffer(n, [P, 2, TRI]) for n in ("stick_z", "stick_l"))
        ks_pair = pair_buffer("ks_pair", [P, T])
        qs_one = sb("qs_one", [P, 2, T], at=where["wa_hi"])
        vs_pair = pair_buffer("vs_pair", [P, TT, P])
        mla_q = sb("mla_q", [P, HEADS_B, T], at=where["x_hi"])
        mla_k = sb("mla_k", [P, HEADS_B, T], at=where["x_lo"])
        mla_v = sb("mla_v", [P, TT, T], at=where["sb_k"])
        cq_hi = sb("cq_hi", [P, 3, T], F32R, at=where["f"])
        cq_lo = sb("cq_lo", [P, 3, T], F32R, at=where["sb_v"])
        turns = sb("turns", [P, T], at=where["f"] + 3 * 4 * T)
        turns_q = sb("turns_q", [P, T], at=where["sb_v"] + 3 * 4 * T)
        angle, steps_ = (sb(n, [P, T], at=where["f"] + j * 4 * T) for j, n in enumerate(("angle", "steps")))
        pos = sb("pos", [P, T], mybir.dt.int32, at=where["f"] + 2 * 4 * T)
        fold = sb("fold", [P, P], at=where["f"] + 4 * 4 * T)
        tri = sb("tri", [P, P], at=where["fold"] + 4 * P)
        mask_a = sb("mask_a", [P, TRI], at=where["f"] + 5 * 4 * T)
        mask_b = sb("mask_b", [P, TRI], at=where["f"] + 5 * 4 * T)
        assert where["mask_b"] + 4 * TRI <= where["f"] + 4 * KT * T
        ckv_hi = sb("ckv_hi", [P, 2, T], F32R, at=where["wa_hi"])
        ckv_lo = sb("ckv_lo", [P, 2, T], F32R, at=where["wa_hi"] + 2 * 4 * T)
        score_b = sb("score_b", [P, 2, TRI], at=where["f"])
        prob_b = sb("prob_b", [P, 2, TRI], at=where["c_q"])
        qm_pair = sb("qm_pair", [P, 2, T], at=where["wa_hi"])
        km_pair = sb("km_pair", [P, 2, T], at=where["wa_hi"] + 2 * 4 * T)
        vm_pair = sb("vm_pair", [P, TT, P], at=where["sb_v"])
        ob_tok = sb("ob_tok", [P, TT, P], at=where["sb_v"] + 4 * T)
        at_[0] = where["sb_v"] + 2 * 4 * T
        top_b, neg_b, total_b, inv_b = (mid_buffer(n, [P, 2, TT]) for n in ("top_b", "neg_b", "total_b", "inv_b"))

        STICK_AT = [0, 512, 1024, 896]
        LATENT_AT = [896, 1024, 512, 0]
        BANKS = [(0, 512), (512, 1024), (1024, 1280)]

        class Second:
            def __init__(self, first_unit, x_tiles, updates):
                self.x0, self.h0 = x_tiles, KT * updates
                self.n_in = first_unit
                self.n_uq = first_unit + 11 * KT
                self.n_uk = self.n_uq + 6
                self.n_uv = self.n_uk + 4
                self.n_a = self.n_uv + 2
                self.n_b = self.n_a + 8
                self.n_out = self.n_b + 8
                self.end = self.n_out + 2 * KT
                self.rs = new_rstd()
                self.pre, self.q, self.kv, self.final = Norm(KT), Norm(3), Norm(2), Norm(KT)

        PROJ = [("q", 4), ("k", 4), ("v", 4), ("z", 4), ("cq", 4), ("ckv", 2), ("mz", 4), ("ga0", 4), ("ga1", 4), ("gb0", 4), ("gb1", 4)]
        tables_loaded = sem("tables_loaded")
        mask_loaded = sem("mask_loaded")
        pa = Steps("proj_act", ["sin"] + [(n, m) for n, tiles in PROJ for m in range(tiles)])
        pv = Steps("proj_dve", ["gain"] + [(n, k) for k in each for n in ("norm", "shift")] +
                   ["float", "angle", "near", "steps", "less1", "less2", "less3", "phase", "clip", "one"])
        sp_ = Steps("stick_score_pe", [("score", j) for j in two])
        sact = Steps("stick_score_act", [(n, j) for j in two for n in ("abs", "exp", "ln")])
        sv = Steps("stick_score_dve", [("q", 0), ("q", 1), "k"] + [("z", j, b) for j in two for b in range(3)])
        wp_ = Steps("stick_value_pe", [(n, j) for n in ("sum", "o") for j in two])
        wa_ = Steps("stick_value_act", [("w", j) for j in two])
        wv_ = Steps("stick_value_dve", ["v"] + [("soft", j) for j in two] + [("less", j, b) for j in two for b in range(3)] + [("o", j) for j in two])
        lp = Steps("latent_pe", ["fold"])
        la = Steps("latent_act", [("cq_hi", k) for k in range(3)] + [("ckv_hi", k) for k in range(2)] + [("k", k) for k in each])
        lv = Steps("latent_dve", [("cq_lo", k) for k in range(3)] + [("ckv_lo", k) for k in range(2)] + ["turns_q", "rot"] +
                   [(n, k) for n in ("q", "k") for k in each] + [("v", t) for t in range(TT)])
        ms_p = Steps("mla_score_pe", [("score", j) for j in two])
        ms_a = Steps("mla_score_act", [("exp", j, n) for j in two for n in range(TT)])
        ms_v = Steps("mla_score_dve", ["q", "k"] + [s_ for j in two for s_ in [("mask", j, b) for b in range(3)] + [("top", j, n) for n in range(TT)] + [("neg", j)]])
        mp = Steps("mla_value_pe", [("turn", j) for j in two] + ["value", "turn_o"])
        ma = Steps("mla_value_act", [("turn", j) for j in two])
        mv = Steps("mla_value_dve", ["v"] + [("inv", j) for j in two] + [("turn", j, b) for j in two for b in range(2)] + [("o", j) for j in two] + ["turn_o"])
        bv_ = Steps("branch_dve", [("a", k) for k in each] + [s_ for k in each for s_ in [("b", k), ("sum", k)]] + [("h", k) for k in each] + [("out", k) for k in each])

        def hold(pe, o):
            pe.matmul(o[0:1, 0:1], ident[:, 0:1], ident[:, 0:1], start=True, stop=True)

        def second_tensor(pe, s):
            sa, sb_ = bank[SETA], bank[SETB]
            sets = (sb_, sa)
            norm_sums(pe, s.pre, sa[0])
            norm_wide(pe, s.pre, sa[1])
            for b, (name, tiles) in enumerate(PROJ):
                if b >= 2:
                    last, count_ = PROJ[b - 2]
                    pe.wait_ge(*pa(last, count_ - 1))
                for k in each:
                    n = s.n_in + b * KT + k
                    if b == 0:
                        pe.wait_ge(x_lo_ready, s.x0 + k + 1)
                    if name == "v":
                        moving_units(pe, sets[b % 2], x_hi, x_lo, k, KT, n)
                    else:
                        unit_products(pe, [o[:] for o in sets[b % 2][:tiles]], x_hi[:, k, :], x_lo[:, k, :], k == 0, k == KT - 1, n)

        def moving_units(pe, outs, hi, lo, k, tiles, n):
            pe.wait_ge(w_lo_ready, n + 1)
            for t in range(TT):
                c = slice(t * P, (t + 1) * P)
                pe.matmul(outs[t][:], hi[:, k, c], w_hi[:, n % RW, :], start=k == 0, stop=False)
                pe.matmul(outs[t][:], lo[:, k, c], w_hi[:, n % RW, :], start=False, stop=False)
                done = pe.matmul(outs[t][:], hi[:, k, c], w_lo[:, n % RW, :], start=False, stop=k == tiles - 1)
            done.then_inc(w_used, 1)

        def second_scalar(act, s):
            for k in each:
                act.wait_ge(h_ready, s.h0 - KT + k + 1)
                square(act, s.pre, k, h[:, k, :])
            for t, source in ((pos, pos_in), (fold, fold_in), (tri, tri_in), (mask_a, mask_a_in)):
                act.dma_start(t[:], source).then_inc(tables_loaded, 16)
            norm_root(act, s.pre, bank[SETA][0], D)
            for k in each:
                act.wait_ge(*pv("shift", k))
                act.activation(x_hi[:, k, :], x_norm[:, k, :], ACT.Copy).then_inc(x_hi_ready, 1)
            act.wait_ge(*pv("clip"))
            act.activation(turns[:], angle[:], ACT.Sin, scale=rope_c[:, 3:4]).then_inc(*pa.tell("sin"))
            dest = {"q": sb_q, "k": sb_k, "v": sb_v, "z": sb_z, "ckv": c_kv, "mz": mla_z}
            for b, (name, tiles) in enumerate(PROJ):
                act.wait_ge(w_used, s.n_in + (b + 1) * KT)
                func = {"z": ACT.Silu, "m": ACT.Silu, "g": ACT.Sigmoid}.get(name[0], ACT.Copy)
                for m in range(tiles):
                    if name[0] == "g":
                        out_ = (gate_a if name[1] == "a" else gate_b)[:, 4 * int(name[2]) + m, :]
                    elif name == "cq":
                        out_ = c_q[:, m, :] if m < 3 else k_rot[:]
                    else:
                        out_ = dest[name][:, m, :]
                    act.activation(out_, bank[(SETB, SETA)[b % 2]][m][:], func).then_inc(*pa.tell(name, m))

        def second_vector(dve, s):
            dve.scalar_tensor_tensor(out=gain_s[:], in0=mod[:, KT:2 * KT], scalar=1.0, in1=vec[:, VEC.at["gain2"]:VEC.at["gain2"] + KT],
                                     op0=ALU.add, op1=ALU.mult).then_inc(*pv.tell("gain"))
            norm_diag(dve, s.pre)
            dve.wait_ge(wide_ready, s.pre.n + 1)
            dve.wait_ge(*pv("gain"))
            for k in each:
                dve.scalar_tensor_tensor(out=x_norm[:, k, :], in0=h[:, k, :], scalar=gain_s[:, k:k + 1], in1=bank[SETA][1][:],
                                         op0=ALU.mult, op1=ALU.mult).then_inc(*pv.tell("norm", k))
                dve.wait_ge(*pv("norm", k))
                dve.tensor_scalar(x_norm[:, k, :], x_norm[:, k, :], mod[:, k:k + 1], None, ALU.add).then_inc(*pv.tell("shift", k))
                if k:
                    input_rest(dve, s, k - 1)
            input_rest(dve, s, KT - 1)
            dve.wait_ge(tables_loaded, 64)

            def step(name, before, out_, *a):
                if before:
                    dve.wait_ge(*pv(before))
                dve.tensor_scalar(out_[:], *a).then_inc(*pv.tell(name))

            dve.tensor_copy(steps_[:], pos[:]).then_inc(*pv.tell("float"))
            step("angle", "float", angle, steps_[:], rope_c[:, 0:1], None, ALU.mult)
            step("near", "angle", steps_, angle[:], 1.0 / (2 * np.pi), rope_c[:, 1:2], ALU.mult, ALU.add)
            dve.wait_ge(*pv("near"))
            dve.tensor_scalar(steps_[:], steps_[:], ROUND, ROUND, ALU.add, ALU.subtract).then_inc(*pv.tell("steps"))
            before = "steps"
            for j, part in enumerate(TURN):
                dve.wait_ge(*pv(before))
                before = f"less{j + 1}"
                dve.scalar_tensor_tensor(out=angle[:], in0=steps_[:], scalar=-part, in1=angle[:], op0=ALU.mult, op1=ALU.add).then_inc(*pv.tell(before))
            step("phase", before, angle, angle[:], rope_c[:, 2:3], None, ALU.add)
            step("clip", "phase", angle, angle[:], PI, -PI, ALU.min, ALU.max)
            dve.wait_ge(*pa("sin"))
            dve.memset(turns[0:64, :], 1.0).then_inc(*pv.tell("one"))

        def input_rest(dve, s, k):
            dve.wait_ge(x_hi_ready, s.x0 + k + 1)
            dve.tensor_tensor(x_lo[:, k, :], x_norm[:, k, :], x_hi[:, k, :].bitcast(F32), ALU.subtract).then_inc(x_lo_ready, 1)

        def pair_rounds(eng, values, scores):
            scores(None, i=None, k=0)
            with eng.Fori(0, 3) as i:
                values(lambda: scores(dict(i=i, k=0), i=i, k=1), i=i, k=0)
            values(lambda: None, i=None, k=3)

        def stick_tensor(pe, s):
            sa, sb_ = bank[SETA], bank[SETB]
            banks = (sa, sb_)
            pe.wait_ge(*pa("gb1", 3))

            def at(j, t, first=0):
                a0, a1 = STICK_AT[t] + first, STICK_AT[t] + (TT - t) * P
                return banks[j][a0 // T][:, a0 % T:(a1 - 1) % T + 1]

            def scores(before, **r):
                pe.wait_ge(*sv("k", **r))
                for t in range(TT):
                    for j in two:
                        done = pe.matmul(at(j, t), ks_pair[:, t * P:(t + 1) * P], qs_one[:, j, t * P:], start=True, stop=True)
                        if t == TT - 1:
                            done.then_inc(*sp_.tell("score", j))

            def values(between, **r):
                for j in two:
                    pe.wait_ge(*wv_("soft", j, **r))
                    for t in range(TT):
                        for u in range(t, TT):
                            a = STICK_AT[u]
                            done = pe.matmul(at(j, t, (u - t) * P), (tri if u == t else ones)[:], stick_l[:, j, a:a + (TT - u) * P],
                                             start=u == t, stop=u == TT - 1)
                    done.then_inc(*wp_.tell("sum", j))
                for j in two:
                    pe.wait_ge(*wv_("less", j, 2, **r))
                between()
                for j in two:
                    pe.wait_ge(*wa_("w", j, **r))
                    hold(pe, banks[j][3])
                    for t in range(TT):
                        a = STICK_AT[t]
                        done = pe.matmul(banks[j][3][half(j), t * P:], vs_pair[:, t, half(j)], stick_l[:, j, a:a + (TT - t) * P],
                                         start=t == 0, stop=t == TT - 1)
                    done.then_inc(*wp_.tell("o", j))

            pair_rounds(pe, values, scores)
            pe.wait_ge(*wv_("o", 1, k=3))

        def stick_scalar(act, s):
            def scores(before, **r):
                for j in two:
                    if before:
                        act.wait_ge(*wp_("o", j, **before))
                    act.wait_ge(*sv("z", j, 2, **r))
                    act.activation(stick_l[:, j, :], stick_z[:, j, :], ACT.Abs).then_inc(*sact.tell("abs", j))
                    act.wait_ge(*sact("abs", j, **r))
                    act.activation(stick_l[:, j, :], stick_l[:, j, :], ACT.Exp, scale=-1.0).then_inc(*sact.tell("exp", j))
                    act.wait_ge(*sact("exp", j, **r))
                    act.activation(stick_l[:, j, :], stick_l[:, j, :], ACT.Ln, bias=1.0).then_inc(*sact.tell("ln", j))

            def values(between, **r):
                for j in two:
                    act.wait_ge(*wv_("less", j, 2, **r))
                    act.activation(stick_l[:, j, :], stick_z[:, j, :], ACT.Exp).then_inc(*wa_.tell("w", j))
                between()

            pair_rounds(act, values, scores)

        def stick_vector(dve, s):
            banks = (bank[SETA], bank[SETB])
            dve.wait_ge(*pa("gb1", 3))
            dve.wait_ge(w_used, s.n_uq)
            dve.memset(qs_one[:], 0.0).then_inc(q_zero, 1)
            dve.wait_ge(q_zero, 2)

            def load(**r):
                for j in two:
                    dve.tensor_copy(qs_one[half(j), j, :], tile_at(sb_q, **r)[half(j)]).then_inc(*sv.tell("q", j))
                dve.tensor_copy(ks_pair[:], tile_at(sb_k, **r)).then_inc(*sv.tell("k"))

            def scores(before, **r):
                if not before:
                    load(**r)
                for j in two:
                    if before:
                        dve.wait_ge(*wa_("w", j, **before))
                    dve.wait_ge(*sp_("score", j, **r))
                    for b, (a0, a1) in enumerate(BANKS):
                        dve.scalar_tensor_tensor(out=stick_z[:, j, a0:a1], in0=banks[j][b][:, 0:a1 - a0], scalar=0.125, in1=mask_a[:, a0:a1],
                                                 op0=ALU.mult, op1=ALU.add).then_inc(*sv.tell("z", j, b))

            def values(between, i, k):
                r = dict(i=i, k=k)
                if i is not None:
                    load(i=i, k=k + 1)
                dve.tensor_copy(vs_pair[:], sb_v[:, :, k * P:(k + 1) * P] if i is None else sb_v[:, :, bass.ds(i * P, P)]).then_inc(*wv_.tell("v"))
                for j in two:
                    dve.wait_ge(*sact("ln", j, **r))
                    dve.scalar_tensor_tensor(out=stick_l[:, j, :], in0=stick_z[:, j, :], scalar=0.0, in1=stick_l[:, j, :],
                                             op0=ALU.max, op1=ALU.add).then_inc(*wv_.tell("soft", j))
                for j in two:
                    dve.wait_ge(*wp_("sum", j, **r))
                    for b, (a0, a1) in enumerate(BANKS):
                        dve.tensor_tensor(stick_z[:, j, a0:a1], stick_z[:, j, a0:a1], banks[j][b][:, 0:a1 - a0], ALU.subtract).then_inc(*wv_.tell("less", j, b))
                between()
                for j in two:
                    dve.wait_ge(*wp_("o", j, **r))
                    v = tile_at(sb_z, **r)[half(j)]
                    dve.tensor_tensor(v, banks[j][3][half(j), :], v, ALU.mult).then_inc(*wv_.tell("o", j))

            pair_rounds(dve, values, scores)

        def latent_tensor(pe, s):
            sa, sb_ = bank[SETA], bank[SETB]
            pe.wait_ge(*wv_("o", 1, k=3))
            norm_sums(pe, s.q, sa[0])
            norm_wide(pe, s.q, sa[1])
            norm_sums(pe, s.kv, sa[0])
            norm_wide(pe, s.kv, sa[2])
            pe.wait_ge(*lv("rot"))
            pe.matmul(sa[3][:], fold[:], k_rot[:], start=True, stop=True).then_inc(*lp.tell("fold"))
            for b, set_ in enumerate((sb_, sa)):
                if b:
                    pe.wait_ge(rstd_ready, s.rs + 1)
                    pe.wait_ge(*la("k", KT - 1))
                for k in range(3):
                    if b == 0:
                        pe.wait_ge(*lv("cq_lo", k))
                    unit_products(pe, [o[:] for o in set_], cq_hi[:, k, :], cq_lo[:, k, :], k == 0, k == 2, s.n_uq + 3 * b + k)
            for b, set_ in enumerate((sb_, sa)):
                pe.wait_ge(*lv("q", 4 * b + 3))
                for k in range(2):
                    pe.wait_ge(*lv("ckv_lo", k))
                    unit_products(pe, [o[:] for o in set_], ckv_hi[:, k, :], ckv_lo[:, k, :], k == 0, k == 1, s.n_uk + 2 * b + k)
            pe.wait_ge(*lv("k", 3))
            for k in range(2):
                moving_units(pe, sb_, ckv_hi, ckv_lo, k, 2, s.n_uv + k)

        def latent_scalar(act, s):
            act.wait_ge(*wv_("o", 1, k=3))
            act.dma_start(mask_b[:], mask_b_in).then_inc(mask_loaded, 16)
            for name, nm, src, hi, tiles in (("q", s.q, c_q, cq_hi, 3), ("kv", s.kv, c_kv, ckv_hi, 2)):
                for k in range(tiles):
                    act.activation(hi[:, k, :], src[:, k, :], ACT.Copy, scale=vcol(f"{name}_norm2", k)).then_inc(*la.tell(f"c{name}_hi", k))
                    square(act, nm, k, src[:, k, :])
                if name == "q":
                    norm_root(act, s.q, bank[SETA][0], 3 * P)
            norm_root(act, s.kv, bank[SETA][0], 2 * P)
            act.wait_ge(wide_ready, s.kv.n + 1)
            act.activation(rstd[:], bank[SETA][2][:], ACT.Copy).then_inc(rstd_ready, 1)
            act.wait_ge(*lp("fold"))
            for k in each:
                act.activation(mla_k[half(1), k, :], bank[SETA][3][half(1), :], ACT.Copy).then_inc(*la.tell("k", k))

        def latent_vector(dve, s):
            sa, sb_ = bank[SETA], bank[SETB]
            sets = (sb_, sa)

            def low(name, nm, src, hi, lo, tiles):
                for k in range(tiles):
                    dve.wait_ge(*la(f"c{name}_hi", k))
                    dve.scalar_tensor_tensor(out=lo[:, k, :], in0=src[:, k, :], scalar=vcol(f"{name}_norm2", k), in1=hi[:, k, :].bitcast(F32),
                                             op0=ALU.mult, op1=ALU.subtract).then_inc(*lv.tell(f"c{name}_lo", k))
                    add_square(dve, nm, k)

            low("q", s.q, c_q, cq_hi, cq_lo, 3)
            norm_diag(dve, s.q)
            low("kv", s.kv, c_kv, ckv_hi, ckv_lo, 2)
            norm_diag(dve, s.kv)
            dve.wait_ge(wide_ready, s.q.n + 1)
            dve.wait_ge(*pv("one"))
            dve.tensor_tensor(turns_q[:], turns[:], sa[1][:], ALU.mult).then_inc(*lv.tell("turns_q"))
            dve.tensor_tensor(k_rot[:], k_rot[:], turns[:], ALU.mult).then_inc(*lv.tell("rot"))
            dve.wait_ge(*lv("turns_q"))
            for k in each:
                dve.wait_ge(w_used, s.n_uq + 3 * (k // 4 + 1))
                dve.tensor_tensor(mla_q[:, k, :], sets[k // 4][k % 4][:], turns_q[:], ALU.mult).then_inc(*lv.tell("q", k))
            dve.wait_ge(rstd_ready, s.rs + 1)
            for k in each:
                dve.wait_ge(w_used, s.n_uk + 2 * (k // 4 + 1))
                dve.tensor_tensor(mla_k[half(0), k, :], sets[k // 4][k % 4][half(0), :], rstd[half(0), :], ALU.mult).then_inc(*lv.tell("k", k))
            dve.wait_ge(w_used, s.n_uv + 2)
            dve.wait_ge(diag_ready, (1 + TT) * (s.kv.n + 1))
            for t in range(TT):
                dve.tensor_scalar(mla_v[:, t, :], sb_[t][:], rinv[:, t:t + 1], None, ALU.mult).then_inc(*lv.tell("v", t))

        LATENT_SCALE = float(1 / np.sqrt(np.float32(96)))

        def mla_rounds(eng, values, scores):
            scores(i=None, k=0)
            with eng.Fori(0, 3) as i:
                values(lambda: scores(i=i, k=1), i=i, k=0)
            values(lambda: None, i=None, k=3)

        def mla_tensor(pe, s):
            sa, sb_ = bank[SETA], bank[SETB]
            banks = (sa, sb_)
            pe.wait_ge(*lv("v", TT - 1))

            def at(j, n, t0, t1):
                a = LATENT_AT[n] + t0 * P
                return banks[j][a // T][:, a % T:a % T + (t1 - t0) * P]

            def scores(**r):
                pe.wait_ge(*ms_v("k", **r))
                for j in two:
                    for n in range(TT):
                        done = pe.matmul(at(j, n, 0, n + 1), qm_pair[:, j, n * P:(n + 1) * P], km_pair[:, j, 0:(n + 1) * P], start=True, stop=True)
                    done.then_inc(*ms_p.tell("score", j))

            def values(between, **r):
                for j in two:
                    pe.wait_ge(*ms_a("exp", j, TT - 1, **r))
                    for n in range(TT):
                        for t in range(n + 1):
                            a = LATENT_AT[n] + t * P
                            done = pe.transpose(at(j, n, t, t + 1), score_b[:, j, a:a + P], ident[:])
                    done.then_inc(*mp.tell("turn", j))
                for j in two:
                    pe.wait_ge(*ma("turn", j, **r))
                    pe.wait_ge(*mv("turn", j, 1, **r))
                between()
                for j in two:
                    for n in range(TT):
                        for t in range(n + 1):
                            a = LATENT_AT[n] + t * P
                            done = pe.matmul(sa[3][:, n * P + j * 64:n * P + (j + 1) * 64], prob_b[:, j, a:a + P], vm_pair[:, t, half(j)],
                                             start=t == 0, stop=t == n)
                done.then_inc(*mp.tell("value"))
                pe.wait_ge(*mv("o", 1, **r))
                for n in range(TT):
                    done = pe.transpose(sb_[3][:, n * P:(n + 1) * P], ob_tok[:, n, :], ident[:])
                done.then_inc(*mp.tell("turn_o"))

            mla_rounds(pe, values, scores)
            pe.wait_ge(*mv("turn_o", k=3))

        def mla_scalar(act, s):
            banks = (bank[SETA], bank[SETB])

            def scores(**r):
                for j in two:
                    act.wait_ge(*ms_v("neg", j, **r))
                    for n in range(TT):
                        v = score_b[:, j, LATENT_AT[n]:LATENT_AT[n] + (n + 1) * P]
                        act.activation(v, v, ACT.Exp, bias=neg_b[:, j, n:n + 1], accum_out=total_b[:, j, n:n + 1]).then_inc(*ms_a.tell("exp", j, n))

            def values(between, **r):
                for j in two:
                    act.wait_ge(*mp("turn", j, **r))
                    act.activation(prob_b[:, j, 0:T], banks[j][0][:], ACT.Copy).then_inc(*ma.tell("turn", j))
                between()

            mla_rounds(act, values, scores)

        def mla_vector(dve, s):
            banks = (bank[SETA], bank[SETB])
            dve.wait_ge(mask_loaded, 16)
            dve.wait_ge(*lv("v", TT - 1))
            dve.wait_ge(*la("k", KT - 1))
            dve.wait_ge(w_used, s.n_a)

            def load(i, k):
                for name, pair, source in (("q", qm_pair, mla_q), ("k", km_pair, mla_k)):
                    dve.tensor_copy(pair[:], source[:, 2 * k:2 * k + 2, :] if i is None else source[:, bass.ds(i * 2 + 2 * k, 2), :]).then_inc(*ms_v.tell(name))

            def scores(**r):
                if r["i"] is None:
                    load(**r)
                for j in two:
                    dve.wait_ge(*ms_p("score", j, **r))
                    for b, (a0, a1) in enumerate(BANKS):
                        dve.scalar_tensor_tensor(out=score_b[:, j, a0:a1], in0=banks[j][b][:, 0:a1 - a0], scalar=LATENT_SCALE, in1=mask_b[:, a0:a1],
                                                 op0=ALU.mult, op1=ALU.add).then_inc(*ms_v.tell("mask", j, b))
                    dve.wait_ge(*ms_v("mask", j, 2, **r))
                    for n in range(TT):
                        dve.tensor_reduce(top_b[:, j, n:n + 1], score_b[:, j, LATENT_AT[n]:LATENT_AT[n] + (n + 1) * P],
                                          mybir.AxisListType.X, ALU.max).then_inc(*ms_v.tell("top", j, n))
                    dve.wait_ge(*ms_v("top", j, TT - 1, **r))
                    dve.tensor_scalar(neg_b[:, j, :], top_b[:, j, :], -1.0, None, ALU.mult).then_inc(*ms_v.tell("neg", j))

            def values(between, i, k):
                r = dict(i=i, k=k)
                if i is not None:
                    load(i, 1)
                dve.tensor_copy(vm_pair[:], mla_v[:, :, k * P:(k + 1) * P] if i is None else mla_v[:, :, bass.ds(i * P, P)]).then_inc(*mv.tell("v"))
                for j in two:
                    dve.wait_ge(*ms_a("exp", j, TT - 1, **r))
                    dve.reciprocal(inv_b[:, j, :], total_b[:, j, :]).then_inc(*mv.tell("inv", j))
                for j in two:
                    dve.wait_ge(*mp("turn", j, **r))
                    for b, (a0, a1) in enumerate(BANKS[1:]):
                        dve.tensor_copy(prob_b[:, j, a0:a1], banks[j][1 + b][:, 0:a1 - a0]).then_inc(*mv.tell("turn", j, b))
                between()
                dve.wait_ge(*mp("value", **r))
                for j in two:
                    dve.tensor_tensor(ob_tok[:, :, half(j)], banks[0][3][:].rearrange("p (n c) -> p n c", n=TT)[:, :, half(j)],
                                      inv_b[:, j, :].rearrange("p (n o) -> p n o", o=1).to_broadcast([P, TT, 64]), ALU.mult).then_inc(*mv.tell("o", j))
                dve.wait_ge(*mp("turn_o", **r))
                v = flat(mla_z[:, k:k + 1, :] if i is None else mla_z[:, bass.ds(i, 1), :])
                dve.tensor_tensor(v, banks[1][3][:], v, ALU.mult).then_inc(*mv.tell("turn_o"))

            mla_rounds(dve, values, scores)

        def branch_tensor(pe, s):
            sa, sb_ = bank[SETA], bank[SETB]
            for branch, n0 in enumerate((s.n_a, s.n_b)):
                for b, set_ in enumerate((sa, sb_)):
                    if branch:
                        pe.wait_ge(*bv_("a", 4 * b + 3))
                    for k in range(4):
                        z = 4 * branch + k
                        pe.wait_ge(x_lo_ready, s.x0 + KT + z + 1)
                        unit_products(pe, [o[:] for o in set_], x_hi[:, z, :], x_lo[:, z, :], k == 0, k == 3, n0 + 4 * b + k)
            for b, set_ in enumerate((sa, sb_)):
                pe.wait_ge(*bv_("sum", 4 * b + 3))
                for k in each:
                    if b == 0:
                        pe.wait_ge(x_lo_ready, s.x0 + 2 * KT + k + 1)
                    unit_products(pe, [o[:] for o in set_], x_hi[:, k, :], x_lo[:, k, :], k == 0, k == KT - 1, s.n_out + b * KT + k)
            pe.wait_ge(*bv_("h", 3))
            norm_sums(pe, s.final, sa[0])
            norm_wide(pe, s.final, sa[1])

        def branch_scalar(act, s):
            act.wait_ge(*mv("turn_o", k=3))
            for k in each:
                act.activation(x_hi[:, k, :], (sb_z, mla_z)[k // 4][:, k % 4, :], ACT.Copy).then_inc(x_hi_ready, 1)
            act.wait_ge(w_used, s.n_out)
            for k in each:
                act.wait_ge(*bv_("sum", k))
                act.activation(x_hi[:, k, :], gate_a[:, k, :], ACT.Copy).then_inc(x_hi_ready, 1)
            for k in each:
                act.wait_ge(*bv_("h", k))
                square(act, s.final, k, h[:, k, :])
            norm_root(act, s.final, bank[SETA][0], D)

        def branch_vector(dve, s):
            sets = (bank[SETA], bank[SETB])
            for k in each:
                dve.wait_ge(x_hi_ready, s.x0 + KT + k + 1)
                dve.tensor_tensor(x_lo[:, k, :], (sb_z, mla_z)[k // 4][:, k % 4, :], x_hi[:, k, :].bitcast(F32), ALU.subtract).then_inc(x_lo_ready, 1)
            for k in each:
                dve.wait_ge(w_used, s.n_a + 4 * (k // 4 + 1))
                dve.tensor_tensor(gate_a[:, k, :], sets[k // 4][k % 4][:], gate_a[:, k, :], ALU.mult).then_inc(*bv_.tell("a", k))
            for k in each:
                dve.wait_ge(w_used, s.n_b + 4 * (k // 4 + 1))
                dve.tensor_tensor(gate_b[:, k, :], sets[k // 4][k % 4][:], gate_b[:, k, :], ALU.mult).then_inc(*bv_.tell("b", k))
                dve.wait_ge(*bv_("b", k))
                dve.tensor_tensor(gate_a[:, k, :], gate_a[:, k, :], gate_b[:, k, :], ALU.add).then_inc(*bv_.tell("sum", k))
            for k in each:
                dve.wait_ge(x_hi_ready, s.x0 + 2 * KT + k + 1)
                dve.tensor_tensor(x_lo[:, k, :], gate_a[:, k, :], x_hi[:, k, :].bitcast(F32), ALU.subtract).then_inc(x_lo_ready, 1)
            for k in each:
                dve.wait_ge(w_used, s.n_out + KT * (k // 4 + 1))
                dve.scalar_tensor_tensor(out=h[:, k, :], in0=sets[k // 4][k % 4][:], scalar=mod[:, 2 * KT + k:2 * KT + k + 1], in1=h[:, k, :],
                                         op0=ALU.mult, op1=ALU.add).then_inc(*bv_.tell("h", k))
            for k in each:
                add_square(dve, s.final, k)
            norm_diag(dve, s.final)
            dve.wait_ge(wide_ready, s.final.n + 1)
            for k in each:
                dve.scalar_tensor_tensor(out=f[:, k, :], in0=h[:, k, :], scalar=vcol("final", k), in1=bank[SETA][1][:],
                                         op0=ALU.mult, op1=ALU.mult).then_inc(*bv_.tell("out", k))

        f0 = Ffn(0, 0, 0, 0, 0, 0)
        mix = Rwkv(f0.end, KT, 1)
        f1 = Ffn(1, 0, 1, mix.end, 8 * KT, 2)
        f2 = Ffn(2, 1, 0, f1.end + KT, 10 * KT, 3, kv=f1.end)
        swa = Swa(f2.end, 11 * KT, 4)
        f3 = Ffn(3, 1, 1, swa.end, 13 * KT, 5)
        second = Second(f3.end, 14 * KT, 6)
        assert second.end == n_units

        block = ctx.enter_context(nc.Block())

        @block.sync
        def _(sp):
            sp.dma_start(vec[:], vectors).then_inc(in_loaded, 16)
            sp.dma_start(h[:], xT).then_inc(in_loaded, 16)
            for t, source in ((masks, masks_in), (gather, gather_in), (spread, spread_in), (rows, rows_in), (rope_c, rope_in)):
                sp.dma_start(t[:], source).then_inc(in_loaded, 16)
            for n in range(RS):
                load_unit(sp, n)
            with sp.Fori(1, n_units // RS) as i:
                for j in range(RS):
                    sp.wait_ge(w_lo_ready, i * RS + (j - RS + 1))
                    load_unit(sp, j, i)
            for n in range(n_units // RS * RS, n_units):
                sp.wait_ge(w_lo_ready, n - RS + 1)
                load_unit(sp, n)
            for k in range(KT):
                sp.wait_ge(*bv_("out", k))
                sp.dma_start(out[:, k, :], f[:, k, :]).then_inc(stored, 16)
            sp.wait_ge(stored, 16 * KT)

        @block.gpsimd
        def _(pool):
            pool.memset(ones[:], 1.0).then_inc(const_ready, 1)
            pool.memset(eps[:], EPS).then_inc(const_ready, 1)
            pool.memset(ident[:], 0.0).then_inc(const_ready, 1)
            pool.wait_ge(const_ready, 3)
            pool.affine_select(out=ident[:], in_=ident[:], compare_op=ALU.not_equal, fill=1.0, base=0,
                               pattern=[[-1, P]], channel_multiplier=1).then_inc(const_ready, 1)

            for n in range(RW):
                split_unit(pool, n)
            with pool.Fori(0, n_units // RW - 1) as i:
                for j in range(RW):
                    split_unit(pool, RW + j, i)
            for n in range(n_units // RW * RW, n_units + 1):
                split_unit(pool, n)

        @block.scalar
        def _(act):
            act.wait_ge(in_loaded, 16 * 7)
            act.wait_ge(const_ready, 4)
            input_parts_scalar(act, f0, 0)
            ffn_scalar(act, f0)
            rwkv_scalar(act, mix)
            pairs_scalar(act)
            group_scalar(act, mix)
            input_parts_scalar(act, f1, 2)
            ffn_scalar(act, f1)
            input_parts_scalar(act, f2, 3)
            ffn_scalar(act, f2)
            input_parts_scalar(act, swa, 4)
            swa_scalar(act, swa)
            input_parts_scalar(act, f3, 5)
            ffn_scalar(act, f3)
            second_scalar(act, second)
            stick_scalar(act, second)
            latent_scalar(act, second)
            mla_scalar(act, second)
            branch_scalar(act, second)

        @block.vector
        def _(dve):
            dve.wait_ge(in_loaded, 16 * 7)
            dve.wait_ge(const_ready, 4)
            input_parts_vector(dve, f0, None)
            ffn_vector(dve, f0)
            for k in range(KT):
                update_h(dve, f0, k)
                add_square(dve, mix.pre, k)
            rwkv_vector(dve, mix)
            pairs_vector(dve)
            group_vector(dve, mix)
            input_parts_vector(dve, f1, mix)
            ffn_vector(dve, f1)
            input_parts_vector(dve, f2, f1)
            ffn_vector(dve, f2)
            input_parts_vector(dve, swa, f2)
            swa_vector(dve, swa)
            input_parts_vector(dve, f3, swa)
            ffn_vector(dve, f3)
            for k in range(KT):
                update_h(dve, f3, k)
                add_square(dve, second.pre, k)
            second_vector(dve, second)
            stick_vector(dve, second)
            latent_vector(dve, second)
            mla_vector(dve, second)
            branch_vector(dve, second)

        @block.tensor
        def _(pe):
            pe.wait_ge(const_ready, 4)
            pe.wait_ge(in_loaded, 16 * 7)
            ffn_tensor(pe, f0)
            rwkv_tensor(pe, mix)
            pairs_tensor(pe)
            group_tensor(pe, mix)
            ffn_tensor(pe, f1)
            ffn_tensor(pe, f2)
            swa_tensor(pe, swa)
            ffn_tensor(pe, f3)
            second_tensor(pe, second)
            stick_tensor(pe, second)
            latent_tensor(pe, second)
            mla_tensor(pe, second)
            branch_tensor(pe, second)


Q_ORDER = [8 * (t % 2) + t // 2 + 4 * j for t in range(KT) for j in range(2)]


def window_table():
    q, k = np.arange(P)[:, None], np.arange(2 * P)[None, :]
    first, other = k <= q, (k > q) & (k <= q + P)
    return np.stack([np.where(m, 0, MASKED) for m in (first, other, other, other)], 1).astype(np.float32)


def second_units(i):
    sizes = (512, 512, 512, 512, 384, 256, 32, 512, D, D)
    q, k, v, z, cq, ckv, rot, mz, ga, gb = np.split(i["w_in_2"][0], np.cumsum(sizes)[:-1], 1)
    none = lambda w, n: np.zeros(w.shape[:-1] + (n,), np.float32)
    swap = lambda w: np.concatenate([w[..., 16:], w[..., :16]], -1)
    w_in = [q, k, v, z, cq, none(cq, 64), rot, swap(rot), ckv, none(ckv, 256), mz, ga, gb]
    uq = i["w_uq_2"][0].reshape(384, HEADS_B, 96)
    uq = np.concatenate([uq, swap(uq[..., 64:])], 2).reshape(384, D)
    ukv = i["w_ukv_2"][0].reshape(256, HEADS_B, 128)
    uk = np.concatenate([ukv[..., :64], none(ukv, 64)], 2).reshape(256, D)
    return [in_units(np.concatenate(w_in, 1)), in_units(uq), in_units(uk), in_units(ukv[..., 64:].reshape(256, 512)),
            in_units(i["w_branch_a_2"][0]), in_units(i["w_branch_b_2"][0]), in_units(i["w_out_2"][0])]


def second_tables():
    p, n = np.arange(P)[:, None], np.arange(P)[None, :]
    rope = np.zeros((P, 4), np.float32)
    rows = np.arange(64, P)
    rope[rows, 0] = np.float32(10000.0) ** (-(rows % 16 * 2).astype(np.float32) / np.float32(32))
    rope[:, 1] = np.where(np.arange(P) < 96, 0.25, 0)
    rope[:, 2] = np.where(np.arange(P) < 96, np.pi / 2, 0)
    rope[:, 3] = np.where((np.arange(P) >= 96) & (np.arange(P) < 112), -1, 1)
    fold = ((p >= 64) & (n >= 64) & (p % 32 == n % 32)).astype(np.float32)
    tri = (p >= n).astype(np.float32)
    stick, latent = np.where(p < n, 0, MASKED), np.where(n <= p, 0, MASKED)
    mask_a, mask_b = np.zeros((2, P, TRI), np.float32)
    for t, a in enumerate((0, 512, 1024, 896)):
        mask_a[:, a:a + P] = stick
    for t, a in enumerate((896, 1024, 512, 0)):
        mask_b[:, a + t * P:a + (t + 1) * P] = latent
    return dict(rope_in=rope, fold_in=fold, tri_in=tri, mask_a_in=mask_a, mask_b_in=mask_b)


def host(i):
    parts = ffn_units(i["ffn_w_in"][0, 0], i["ffn_w_out"][0, 0])
    parts += rwkv_units(*(i["rwkv_" + n][0] for n in "w1 a1 g1 w_rkv w2 a2 g2 w_o".split()))
    parts += ffn_units(i["ffn_w_in"][0, 1], i["ffn_w_out"][0, 1])
    parts += [in_units(i["w_kv"])]
    parts += ffn_units(i["ffn_w_in"][1, 0], i["ffn_w_out"][1, 0])
    parts += [in_units(i["attn_w_q"][0].reshape(D, 16, 64)[:, Q_ORDER].reshape(D, D)),
              in_units(i["attn_w_o"][0].reshape(16, 64, D)[Q_ORDER].reshape(D, D))]
    parts += ffn_units(i["ffn_w_in"][1, 1], i["ffn_w_out"][1, 1])
    parts += second_units(i)
    units = np.concatenate(parts)
    vec = [i["norm_g"], i["rwkv_mu"]] + [i["rwkv_" + n] for n in "w0 a0 k_k k_a r_k gn_g gn_b".split()]
    vec += [i["kv_norm_g"], i["b_kv"][:KV], i["attn_b_q"][0].reshape(16, 64)[Q_ORDER], i["attn_b_o"]]
    vec += [i[n + "_2"] for n in "norm_gain b_ada q_norm_gain kv_norm_gain final_norm_gain c".split()]
    vec = np.concatenate([v.reshape(-1, P) for v in vec]).T
    rows = np.concatenate([i["b_kv"][KV:], i["attn_sinks"][0][Q_ORDER]])
    x = i["x"][0].T.reshape(KT, P, T).transpose(1, 0, 2)
    gather, spread = heads_tables()
    c = np.ascontiguousarray
    return dict(xT=c(x), weights=c(units), vectors=c(vec), masks_in=masks_table(), gather_in=c(gather), spread_in=c(spread),
                rows_in=np.tile(rows, (P, 1)), window_in=window_table(), ada_in=c(i["w_ada_2"][0].reshape(KT, P, 3 * D)),
                pos_in=np.tile(i["positions_2"], (P, 1)), **second_tables())


def kernel(**inputs):
    import concourse.bacc as _bacc
    from concourse.bass_utils import run_bass_kernel_spmd as _run

    arrays = host({name: np.asarray(a) for name, a in inputs.items()})
    nc = _bacc.Bacc("TRN2", target_bir_lowering=False, num_devices=1)
    args = {name: nc.dram_tensor(name, a.shape, mybir.dt.from_np(a.dtype), kind="ExternalInput").ap() for name, a in arrays.items()}
    out = nc.dram_tensor("out", (P, KT, T), F32, kind="ExternalOutput").ap()
    program(nc, out=out, **args)
    r = _run(nc, [arrays], core_ids=[0])
    got = np.asarray(r.results[0]["out"])
    return np.ascontiguousarray(got.transpose(1, 0, 2).reshape(D, T).T)[None]
```
